# Optimizing a Trainium2 kernel written in Bass

```python
import jax, jax.numpy as jnp
from jax import lax
import numpy as np

D_MODEL = 1024
BATCH = 1
SEQ = 1024
DEPTH = 2

N_MEM = 256
RET_HEADS = 4
RET_HEAD_DIM = 128
RET_WIDTH = RET_HEADS * RET_HEAD_DIM
RET_CHUNK = 128
MLA_HEADS = 4
MLA_NOPE = 128
MLA_ROPE = 64
MLA_V = 64
MLA_Q_RANK = 256
MLA_KV_RANK = 128
MLA_WIDTH = MLA_HEADS * MLA_V
MEM_HEADS = 4
MEM_HEAD_DIM = 64
MEM_WIDTH = MEM_HEADS * MEM_HEAD_DIM
MIX_WIDTH = RET_WIDTH + MLA_WIDTH + MEM_WIDTH
IN_SPLITS = (RET_WIDTH, RET_WIDTH, RET_WIDTH, RET_WIDTH, MLA_Q_RANK, MLA_KV_RANK, MLA_ROPE, MEM_WIDTH)
IN_WIDTH = sum(IN_SPLITS)
D_FF = -(-8 * D_MODEL // (3 * 256)) * 256
ATTN_BLOCK = 128
ROPE_BASE = 10000.0
EPS = 1e-6

kernel_name = 'hymba_style_retention_mla_memory_hybrid'

def rmsnorm(x, g):
    xf = x.astype(jnp.float32)
    y = xf * lax.rsqrt(jnp.mean(xf * xf, axis=-1, keepdims=True) + EPS)
    return (y * g.astype(jnp.float32)).astype(x.dtype)

def head_rms(x):
    xf = x.astype(jnp.float32)
    return xf * lax.rsqrt(jnp.mean(xf * xf, axis=-1, keepdims=True) + EPS)

def rope(x, pos):
    half = x.shape[-1] // 2
    inv = ROPE_BASE ** (-jnp.arange(half, dtype=jnp.float32) / half)
    ang = pos.astype(jnp.float32)[..., None] * inv
    cos = jnp.cos(ang)[:, :, None, :]
    sin = jnp.sin(ang)[:, :, None, :]
    x1 = x[..., :half].astype(jnp.float32)
    x2 = x[..., half:].astype(jnp.float32)
    return jnp.concatenate([x1 * cos - x2 * sin, x2 * cos + x1 * sin], axis=-1).astype(x.dtype)

def split_cols(p):
    idx = np.cumsum(IN_SPLITS)[:-1].tolist()
    return jnp.split(p, idx, axis=-1)

def retention(q, k, v):
    B, S, H, dk = q.shape
    dv = v.shape[-1]
    C = RET_CHUNK
    n = S // C
    f32 = jnp.float32
    lg = jnp.log(1.0 - 2.0 ** (-5.0 - jnp.arange(H, dtype=f32)))

    def chunks(t):
        return t.astype(f32).reshape(B, n, C, H, t.shape[-1]).transpose(0, 3, 1, 2, 4)

    qc = chunks(q) * (dk ** -0.5)
    kc = chunks(k)
    vc = chunks(v)
    idx = jnp.arange(C, dtype=f32)
    diff = idx[:, None] - idx[None, :]
    decay = jnp.where(diff >= 0, jnp.exp(lg[:, None, None] * jnp.maximum(diff, 0.0)), 0.0)
    scores = jnp.einsum('bhnqd,bhnkd->bhnqk', qc, kc) * decay[None, :, None]
    inner = jnp.einsum('bhnqk,bhnkv->bhnqv', scores, vc)
    zeta = jnp.exp(lg[:, None] * (C - 1.0 - idx)[None])
    upd = jnp.einsum('bhnkd,bhnkv->nbhdv', kc * zeta[None, :, None, :, None], vc)
    chunk_decay = jnp.exp(lg * C)[None, :, None, None]

    def step(state, u):
        return chunk_decay * state + u, state

    _, prev = lax.scan(step, jnp.zeros((B, H, dk, dv), f32), upd)
    xi = jnp.exp(lg[:, None] * (idx + 1.0)[None])
    cross = jnp.einsum('bhnqd,nbhdv->bhnqv', qc, prev) * xi[None, :, None, :, None]
    return (inner + cross).transpose(0, 2, 3, 1, 4).reshape(B, S, H, dv)

def retention_group(rq, rk, rv, rg, pos):
    B, S, _ = rq.shape
    shp = (B, S, RET_HEADS, RET_HEAD_DIM)
    q = rope(rq.reshape(shp), pos)
    k = rope(rk.reshape(shp), pos)
    o = head_rms(retention(q, k, rv.reshape(shp))).reshape(B, S, RET_WIDTH)
    return (jax.nn.silu(rg.astype(jnp.float32)) * o).astype(rq.dtype)

def mla_group(cq_pre, ckv_pre, kr_pre, q_norm_g, w_uq, kv_norm_g, w_ukv, pos):
    B, S, _ = cq_pre.shape
    H = MLA_HEADS
    q = (rmsnorm(cq_pre, q_norm_g) @ w_uq).reshape(B, S, H, MLA_NOPE + MLA_ROPE)
    q_nope = q[..., :MLA_NOPE]
    q_rope = rope(q[..., MLA_NOPE:], pos)
    kv = (rmsnorm(ckv_pre, kv_norm_g) @ w_ukv).reshape(B, S, H, MLA_NOPE + MLA_V)
    k_nope = kv[..., :MLA_NOPE]
    v = kv[..., MLA_NOPE:]
    k_rope = rope(kr_pre[:, :, None, :], pos)[:, :, 0, :]
    scale = (MLA_NOPE + MLA_ROPE) ** -0.5
    nb = S // ATTN_BLOCK
    qn_b = (q_nope * scale).reshape(B, nb, ATTN_BLOCK, H, MLA_NOPE).transpose(1, 0, 2, 3, 4)
    qr_b = (q_rope * scale).reshape(B, nb, ATTN_BLOCK, H, MLA_ROPE).transpose(1, 0, 2, 3, 4)
    kpos = jnp.arange(S, dtype=jnp.int32)

    def block(args):
        qn, qr, i = args
        s = jnp.einsum('bqhd,bkhd->bhqk', qn, k_nope) + jnp.einsum('bqhr,bkr->bhqk', qr, k_rope)
        qpos = i * ATTN_BLOCK + jnp.arange(ATTN_BLOCK, dtype=jnp.int32)
        s = jnp.where(kpos[None, :] <= qpos[:, None], s.astype(jnp.float32), jnp.finfo(jnp.float32).min)
        p = jax.nn.softmax(s, axis=-1).astype(v.dtype)
        return jnp.einsum('bhqk,bkhv->bqhv', p, v)

    o = lax.map(block, (qn_b, qr_b, jnp.arange(nb, dtype=jnp.int32)))
    return o.transpose(1, 0, 2, 3, 4).reshape(B, S, MLA_WIDTH)

def memory_group(mq, mem, mem_g, w_mem_kv):
    B, S, _ = mq.shape
    M = mem.shape[1]
    kv = rmsnorm(mem, mem_g) @ w_mem_kv
    k = kv[..., :MEM_WIDTH].reshape(B, M, MEM_HEADS, MEM_HEAD_DIM)
    v = kv[..., MEM_WIDTH:].reshape(B, M, MEM_HEADS, MEM_HEAD_DIM)
    q = mq.reshape(B, S, MEM_HEADS, MEM_HEAD_DIM) * (MEM_HEAD_DIM ** -0.5)
    s = jnp.einsum('bshd,bmhd->bhsm', q, k).astype(jnp.float32)
    p = jax.nn.softmax(s, axis=-1).astype(v.dtype)
    return jnp.einsum('bhsm,bmhd->bshd', p, v).reshape(B, S, MEM_WIDTH)

def setup_inputs(seed: int = 0) -> dict:
    key = jax.random.key(seed)
    ks = jax.random.split(key, 20)
    f32 = jnp.float32

    def w(k, shape, fan_in):
        return jax.random.normal(k, shape, f32) * fan_in ** -0.5

    def gain(k, shape):
        return 1.0 + 0.02 * jax.random.normal(k, shape, f32)

    x = jax.random.normal(ks[0], (BATCH, SEQ, D_MODEL), f32)
    mem = jax.random.normal(ks[1], (BATCH, N_MEM, D_MODEL), f32)
    offset = jax.random.randint(ks[2], (BATCH, 1), 0, 1024, dtype=jnp.int32)
    positions = offset + jnp.arange(SEQ, dtype=jnp.int32)[None, :]
    L = DEPTH
    return {
        'x': x,
        'mem': mem,
        'positions': positions,
        'pre_mix_g': gain(ks[3], (L, D_MODEL)),
        'w_in': w(ks[4], (L, D_MODEL, IN_WIDTH), D_MODEL),
        'mla_q_norm_g': gain(ks[5], (L, MLA_Q_RANK)),
        'w_uq': w(ks[6], (L, MLA_Q_RANK, MLA_HEADS * (MLA_NOPE + MLA_ROPE)), MLA_Q_RANK),
        'mla_kv_norm_g': gain(ks[7], (L, MLA_KV_RANK)),
        'w_ukv': w(ks[8], (L, MLA_KV_RANK, MLA_HEADS * (MLA_NOPE + MLA_V)), MLA_KV_RANK),
        'mem_norm_g': gain(ks[9], (L, D_MODEL)),
        'w_mem_kv': w(ks[10], (L, D_MODEL, 2 * MEM_WIDTH), D_MODEL),
        'w_out': w(ks[11], (L, MIX_WIDTH, D_MODEL), MIX_WIDTH),
        'post_mix_g': gain(ks[12], (L, D_MODEL)),
        'pre_ffn_g': gain(ks[13], (L, D_MODEL)),
        'w_gate': w(ks[14], (L, D_MODEL, D_FF), D_MODEL),
        'w_up': w(ks[15], (L, D_MODEL, D_FF), D_MODEL),
        'w_down': w(ks[16], (L, D_FF, D_MODEL), D_FF),
        'post_ffn_g': gain(ks[17], (L, D_MODEL)),
    }

def reference(x, mem, positions, pre_mix_g, w_in, mla_q_norm_g, w_uq, mla_kv_norm_g, w_ukv, mem_norm_g, w_mem_kv, w_out, post_mix_g, pre_ffn_g, w_gate, w_up, w_down, post_ffn_g):
    for l in range(DEPTH):
        h = rmsnorm(x, pre_mix_g[l])
        rq, rk, rv, rg, cq, ckv, kr, mq = split_cols(h @ w_in[l])
        ret = retention_group(rq, rk, rv, rg, positions)
        att = mla_group(cq, ckv, kr, mla_q_norm_g[l], w_uq[l], mla_kv_norm_g[l], w_ukv[l], positions)
        mo = memory_group(mq, mem, mem_norm_g[l], w_mem_kv[l])
        mixed = jnp.concatenate([ret, att.astype(ret.dtype), mo.astype(ret.dtype)], axis=-1) @ w_out[l]
        x = x + rmsnorm(mixed, post_mix_g[l])
        h = rmsnorm(x, pre_ffn_g[l])
        f = (jax.nn.silu(h @ w_gate[l]) * (h @ w_up[l])) @ w_down[l]
        x = x + rmsnorm(f, post_ffn_g[l])
    return x


_drawn_inputs = setup_inputs


def setup_inputs(seed=0):
    import zlib

    import numpy as np

    out = dict(_drawn_inputs(seed))
    spreads = {}
    factors = {'mla_q_norm_g': 8.0, 'mla_kv_norm_g': 8.0, 'mem_norm_g': 8.0, 'post_ffn_g': 2.98}
    for name, (base, spread) in spreads.items():
        noise = np.random.default_rng([zlib.crc32(name.encode()), seed]).standard_normal(out[name].shape)
        drawn = base * np.exp(spread * noise) if base else spread * noise
        out[name] = __import__('jax').numpy.asarray(drawn.astype(out[name].dtype))
    for name, factor in factors.items():
        out[name] = (out[name] * factor).astype(out[name].dtype)
    return out
```

```python
from contextlib import ExitStack, contextmanager

import numpy as np

import concourse.bass as bass
from concourse import mybir

ALU = mybir.AluOpType
ACT = mybir.ActivationFunctionType
AX = mybir.AxisListType
F32 = mybir.dt.float32
F32R = mybir.dt.float32r
I32 = mybir.dt.int32

P = 128
LAYERS = 2
SEQ = 1024
D = 1024
HALF = 512
KT = D // P
HEADS = 4
MEM = 256
QRANK = 256
KVRANK = 128
NOPE, ROPE, VDIM = 128, 64, 64
D_FF = 2816
GROUPS = (8, 8, 6)
BLOCK = 1024
MIXER_BLOCKS, OUT_BLOCKS, FFN_BLOCKS = 28, 8, 68
STORED_BLOCKS = MIXER_BLOCKS + OUT_BLOCKS + FFN_BLOCKS
EPS = 1e-6
LAYER_TILES = 372
ATT_SCALE = float(NOPE + ROPE) ** -0.5
MEM_SCALE = float(64) ** -0.5

RAW, SPLIT, TILES, AUX, OUTS = 2, 4, 4, 2, 2
SCORES, PROBS, PARTS = 3, 4, 3

G_Q, G_KV, G_MEM, G_POST_MIX, G_PRE_FFN, G_POST_FFN, G_NEXT = 0, 2, 3, 11, 19, 27, 35
GAINS = 43

K_ID, K_ONES, K_TRI, K_CAUSAL, K_COLS = 0, 128, 256, 512, 1024
K_PAIR, K_HALVES, K_EPS, K_SIGN, K_FREQ, K_ALL = 1024, 1026, 1028, 1029, 1030, 1032

TWO_PI = 2.0 * np.pi
MAGIC = 12582912.0


class Count:

    def __init__(self, engine, name, start=0, ring=1):
        self.engine, self.ring, self.slot, self.since = engine, ring, 0, 0
        self.base = engine.alloc_register(name)
        engine.reg_mov(self.base, start)

    def at(self, ahead=0):
        return self.engine.snap(self.base) + (self.since + ahead)

    def next(self, n=1):
        self.skip(n)
        return self.at()

    def skip(self, n=1):
        self.since += n
        self.slot = (self.slot + n) % self.ring

    def other(self, n=1):
        self.since += n

    def fold(self):
        if self.since:
            self.engine.reg_add(self.base, self.base, self.since)
            self.since = 0


@contextmanager
def repeat(engine, times, counts):
    for c in counts:
        c.fold()
    with engine.Fori(0, times) as i:
        yield i
        for c in counts:
            c.fold()


def build(nc, x, mem, positions, weights, value_weights, gains, first_gains, consts, decay, out):
    cos_sin = nc.dram_tensor("cos_sin", (2, P, 2, SEQ), F32, kind="Internal").ap()
    with ExitStack() as ctx:
        def sb(name, shape, dt=F32, within=None):
            return (within or ctx).enter_context(nc.sbuf_tensor(name, [P] + shape, dt))

        def sem(name):
            return ctx.enter_context(nc.semaphore(name))

        op_h, op_l = sb("op_high", [2, KT, HALF], F32R), sb("op_low", [2, KT, HALF], F32R)
        w_raw = sb("w_raw", [RAW, BLOCK])
        w_h, w_l = sb("w_high", [SPLIT, BLOCK], F32R), sb("w_low", [SPLIT, BLOCK], F32R)
        branch = sb("branch", [2, KT, HALF])
        const = sb("const", [K_ALL])
        gain = sb("gain", [GAINS])
        stat = sb("stat", [4, 8])
        ident, ones = const[:, K_ID:K_ID + P], const[:, K_ONES:K_ONES + P]
        tri = const[:, K_TRI:K_TRI + 256]
        eps = const[:, K_EPS:K_EPS + 1]

        phase = ExitStack()
        s_pos, s_posf = sb("s_pos", [SEQ], I32, phase), sb("s_posf", [SEQ], F32, phase)
        s_ang, s_turn = sb("s_ang", [SEQ], F32, phase), sb("s_turn", [SEQ], F32, phase)
        s_tab = sb("s_tab", [2, SEQ], F32, phase)
        phase.close()

        phase = ExitStack()
        x_buf = sb("x_buf", [KT, HALF], F32, phase)
        f_square = sb("f_square", [2, HALF], F32, phase)
        f_sum = sb("f_sum", [HALF], F32, phase)
        f_log, f_rsqrt = sb("f_log", [HALF], F32, phase), sb("f_rsqrt", [HALF], F32, phase)
        f_gate, f_hidden = sb("f_gate", [2, HALF], F32, phase), sb("f_hidden", [2, HALF], F32, phase)
        a_h, a_l = sb("a_high", [8, HALF], F32R, phase), sb("a_low", [8, HALF], F32R, phase)
        phase.close()

        phase = ExitStack()
        r_qh, r_ql = sb("r_q_high", [SEQ], F32R, phase), sb("r_q_low", [SEQ], F32R, phase)
        r_kh, r_kl = sb("r_k_high", [SEQ], F32R, phase), sb("r_k_low", [SEQ], F32R, phase)
        r_vh, r_vl = sb("r_v_high", [SEQ], F32R, phase), sb("r_v_low", [SEQ], F32R, phase)
        r_sh, r_sl = sb("r_s_high", [SCORES, HALF], F32R, phase), sb("r_s_low", [SCORES, HALF], F32R, phase)
        r_vt = sb("r_v_transposed", [HALF], F32, phase)
        r_gate = sb("r_gate", [SEQ], F32, phase)
        r_tab = sb("r_cos_sin", [2, SEQ], F32, phase)
        r_decay = sb("r_decay", [SEQ + 2], F32, phase)
        r_t = sb("r_temp", [3, HALF], F32, phase)
        r_square = sb("r_square", [HALF], F32, phase)
        r_log, r_rsqrt = sb("r_log", [HALF], F32, phase), sb("r_rsqrt", [HALF], F32, phase)
        phase.close()

        phase = ExitStack()
        m_vh, m_vl = sb("m_v_high", [8, 256], F32R, phase), sb("m_v_low", [8, 256], F32R, phase)
        latent = ExitStack()
        c_kv, c_kr = sb("c_kv", [SEQ], F32, latent), sb("c_kr", [SEQ], F32, latent)
        c_tab = sb("c_cos_sin", [2, SEQ], F32, latent)
        c_t = sb("c_temp", [3, HALF], F32, latent)
        c_square, c_sum = sb("c_square", [2, HALF], F32, latent), sb("c_sum", [HALF], F32, latent)
        c_log, c_rsqrt = sb("c_log", [HALF], F32, latent), sb("c_rsqrt", [HALF], F32, latent)
        c_norm = sb("c_norm", [2, HALF], F32, latent)
        z_raw = sb("z_raw", [256], F32, latent)
        z_h, z_l = sb("z_high", [256], F32R, latent), sb("z_low", [256], F32R, latent)
        latent.close()
        m_qh, m_ql = sb("m_q_high", [SEQ], F32R, phase), sb("m_q_low", [SEQ], F32R, phase)
        m_kh, m_kl = sb("m_k_high", [SEQ], F32R, phase), sb("m_k_low", [SEQ], F32R, phase)
        m_p = sb("m_p", [PROBS, SEQ], F32, phase)
        m_ph, m_pl = sb("m_p_high", [PARTS, 512], F32R, phase), sb("m_p_low", [PARTS, 512], F32R, phase)
        phase.close()

        phase = ExitStack()
        e_mem = sb("e_mem", [KT, MEM], F32, phase)
        e_square = sb("e_square", [KT, MEM], F32, phase)
        e_nh, e_nl = sb("e_norm_high", [KT, MEM], F32R, phase), sb("e_norm_low", [KT, MEM], F32R, phase)
        e_kh, e_kl = sb("e_k_high", [HEADS, MEM], F32R, phase), sb("e_k_low", [HEADS, MEM], F32R, phase)
        e_vh, e_vl = sb("e_v_high", [2, 256], F32R, phase), sb("e_v_low", [2, 256], F32R, phase)
        e_p = sb("e_p", [PROBS, MEM], F32, phase)
        e_ph, e_pl = sb("e_p_high", [PARTS, 512], F32R, phase), sb("e_p_low", [PARTS, 512], F32R, phase)
        e_log, e_rsqrt = sb("e_log", [MEM], F32, phase), sb("e_rsqrt", [MEM], F32, phase)
        phase.close()

        def slot(n):
            return [t[:, n // 4, 2 * (n % 4):2 * (n % 4) + 2, :] for t in (op_h, op_l)]

        CQ, CKV, KROPE, QROPE, MQ = 0, 2, 3, 5, 0

        psum = ctx.enter_context(nc.psum_tensor("psum", [P, 8 * 512], F32))

        def tile(s, n=512, at=0):
            return psum[:, s * 512 + at:s * 512 + at + n]

        def aux(s, n=512, at=0):
            return psum[:, (TILES + s) * 512 + at:(TILES + s) * 512 + at + n]

        def outs(s, n=512, at=0):
            return psum[:, (TILES + AUX + s) * 512 + at:(TILES + AUX + s) * 512 + at + n]

        w_loaded = [sem(f"w_loaded{i}") for i in range(RAW)]
        loaded = sem("loaded")
        decay_loaded = sem("decay_loaded")
        x_loaded = sem("x_loaded")
        stored = sem("stored")
        w_rounded = sem("w_rounded")
        w_split = sem("w_split")
        pool_waited = sem("pool_waited")
        tile_done = sem("tile_done")
        aux_done = sem("aux_done")
        out_step = sem("out_step")
        tile_read = sem("tile_read")
        aux_read = sem("aux_read")
        out_read = sem("out_read")
        dve_link = sem("dve_link")
        low_ready = sem("low_ready")
        value_ready = sem("value_ready")
        sum_ready = sem("sum_ready")
        part_ready = sem("part_ready")
        square_used = sem("square_used")
        rsqrt_used = sem("rsqrt_used")
        x_ready = sem("x_ready")
        phase_done = sem("phase_done")
        high_ready = sem("high_ready")
        act_ready = sem("act_ready")
        square_ready = sem("square_ready")
        log_ready = sem("log_ready")
        rsqrt_ready = sem("rsqrt_ready")

        block = ctx.enter_context(nc.Block())

        def score_width(j):
            return (0, 512), (128, 384), (256, 256), (256, 256)

        STEPS = [(0, kb) for kb in range(4)] + [(1, kb) for kb in range(8)]

        def columns(half, kb):
            local = kb - 4 * half
            return (0, False) if local < 0 else (min(128 * local, 256), True)

        @block.sync
        def _(sp):
            split = Count(sp, "sp_split", 0, RAW)

            def load(index):
                s = split.slot
                sp.wait_ge(w_split, split.next())
                sp.dma_start(w_raw[:, s, :], weights[index]).then_inc(w_loaded[s], 16)

            layer = Count(sp, "sp_layer")
            with sp.Fori(0, LAYERS) as l:
                def run(first, n):
                    split.fold()
                    with sp.Fori(0, n // RAW) as i:
                        for s in range(RAW):
                            load(l * STORED_BLOCKS + i * RAW + (first + s))
                        split.fold()
                run(0, MIXER_BLOCKS)
                for half in range(2):
                    run(MIXER_BLOCKS, OUT_BLOCKS)
                for half in range(2):
                    run(MIXER_BLOCKS + OUT_BLOCKS, FFN_BLOCKS)

        @block.gpsimd
        def _(pool):
            pool.sem_inc(w_split, RAW)
            raw = [Count(pool, f"pool_loaded{i}") for i in range(RAW)]
            rounded = Count(pool, "pool_rounded")
            split = Count(pool, "pool_split", RAW)
            done = Count(pool, "pool_tiles", TILES)
            turn = [0]

            def counted():
                pool.sem_inc(pool_waited, 1)

            def block_split(last_use, more=0):
                r, s = turn[0] % RAW, turn[0] % SPLIT
                turn[0] += 1
                pool.wait_ge(w_loaded[r], raw[r].next(16))
                counted()
                pool.wait_ge(tile_done, done.at(last_use + 1) + more)
                counted()
                pool.tensor_scalar(w_h[:, s, :], w_raw[:, r, :], 1.0, 1.0, ALU.mult, ALU.mult).then_inc(w_rounded, 1)
                pool.wait_ge(w_rounded, rounded.next())
                pool.tensor_tensor(w_l[:, s, :], w_raw[:, r, :], w_h[:, s, :].bitcast(F32),
                                   ALU.subtract).then_inc(w_split, 1)
                pool.wait_ge(w_split, split.next())
                counted()

            counts = raw + [rounded, split]
            with repeat(pool, LAYERS, counts):
                for s in range(4):
                    block_split(s - 4)
                with repeat(pool, HEADS - 1, counts) as h:
                    for s in range(4):
                        block_split(4 + s, h * 20)
                for last in (64, 65, 66, 67, 84, 85, 86, 87, 90, 91, 165, 167, 184, 185, 187, 187):
                    block_split(last)
                with repeat(pool, 148 // 4, counts) as i:
                    for s in range(4):
                        block_split(220 + s, i * 4)
                done.skip(LAYER_TILES)
                done.fold()

        @block.tensor
        def _(pe):
            pe.sem_inc(tile_done, TILES)
            pe.sem_inc(out_step, SCORES)
            split = Count(pe, "pe_split", RAW, SPLIT)
            tiles = Count(pe, "pe_tiles", 0, TILES)
            auxs = Count(pe, "pe_aux", 0, AUX)
            outr = Count(pe, "pe_outs", 0, OUTS)
            low = Count(pe, "pe_low")
            sums = Count(pe, "pe_sums")
            parts = Count(pe, "pe_parts")
            squares = Count(pe, "pe_squares")
            phases = Count(pe, "pe_phase")
            counts = [split, tiles, auxs, outr, low, sums, parts, squares, phases]

            def product(to, left, right, first, last):
                pe.matmul(to, left[0], right[1], start=first, stop=False)
                pe.matmul(to, left[1], right[0], start=False, stop=False)
                return pe.matmul(to, left[0], right[0], start=False, stop=last)

            def weight(s, at, n=P):
                return w_h[:, s, at:at + n], w_l[:, s, at:at + n]

            def new_tile(n=1):
                s = tiles.slot
                pe.wait_ge(tile_read, tiles.next(n))
                return s

            def new_aux():
                s = auxs.slot
                pe.wait_ge(aux_read, auxs.next())
                return s

            def column_sums(source, n=HALF):
                pe.wait_ge(sum_ready, sums.next())
                pe.matmul(aux(new_aux(), n), ones, source, start=True, stop=True).then_inc(aux_done, 1)

            def project(half, s, source_h, source_l, depth=KT, ready=None):
                to = tile(new_tile())
                for k in range(depth):
                    if ready is not None:
                        pe.wait_ge(low_ready, low.at(ready + k + 1))
                    mm = product(to, weight(s, k * P), (source_h[:, k, :], source_l[:, k, :]),
                                 k == 0, k == depth - 1)
                mm.then_inc(tile_done, 1)

            def boundary(half):
                return [lambda: column_sums(f_sum[:, :]), lambda: column_sums(f_sum[:, :])]

            for half in range(2):
                if half == 0:
                    pe.wait_ge(phase_done, phases.next())
                column_sums(f_sum[:, :])

            squares.skip(2 * KT)
            low.skip(2 * KT)

            with repeat(pe, LAYERS, counts):
                pe.wait_ge(phase_done, phases.next())
                with repeat(pe, HEADS, counts):
                    for half in range(2):
                        for s in range(4):
                            if half == 0:
                                pe.wait_ge(w_split, split.at(s + 1))
                            project(half, s, op_h[:, half], op_l[:, half])
                        pe.wait_ge(part_ready, parts.next())
                        a = new_aux()
                        for b in range(4):
                            mm = pe.transpose(aux(a, P, b * P), r_vt[:, b * P:(b + 1) * P], ident)
                        mm.then_inc(aux_done, 1)
                    split.skip(4)
                    first_tile = tiles.since

                    def score(i):
                        half, kb = STEPS[i]
                        c, _ = columns(half, kb)
                        if kb == 0:
                            pe.wait_ge(low_ready, low.next(2))
                        q0 = half * HALF
                        mm = product(tile(new_tile(), HALF - c),
                                     (r_kh[:, kb * P:(kb + 1) * P], r_kl[:, kb * P:(kb + 1) * P]),
                                     (r_qh[:, q0 + c:q0 + HALF], r_ql[:, q0 + c:q0 + HALF]), True, True)
                        mm.then_inc(tile_done, 1)

                    def value(i):
                        half, kb = STEPS[i]
                        c, _ = columns(half, kb)
                        if kb == 0:
                            pe.wait_ge(out_read, outr.next())
                            pe.wait_ge(aux_read, auxs.at(AUX - 1 + half))
                        pe.wait_ge(tile_read, tiles.at(first_tile + i + 1 - tiles.since + TILES))
                        s = i % SCORES
                        mm = product(outs(half, HALF - c, c),
                                     (r_vh[:, kb * P:(kb + 1) * P], r_vl[:, kb * P:(kb + 1) * P]),
                                     (r_sh[:, s, 0:HALF - c], r_sl[:, s, 0:HALF - c]),
                                     kb == 0, kb == 4 * half + 3)
                        mm.then_inc(out_step, 1)

                    def head_norm():
                        pe.wait_ge(square_ready, squares.next())
                        pe.matmul(aux(new_aux()), ones, r_square[:, :], start=True, stop=True).then_inc(aux_done, 1)

                    for i in range(len(STEPS)):
                        score(i)
                        if i >= 2:
                            value(i - 2)
                        if i == 7:
                            head_norm()
                    value(len(STEPS) - 2)
                    value(len(STEPS) - 1)
                    head_norm()

                squares.skip(6 + 1 + 2 * 2 * 2 * KT)

                pe.wait_ge(phase_done, phases.next())
                for group in (range(4), range(2)):
                    for half in range(2):
                        for s in group:
                            if half == 0:
                                pe.wait_ge(w_split, split.at(s + 1))
                            project(half, (split.slot + s) % SPLIT, op_h[:, half], op_l[:, half])
                    split.skip(len(group))
                for n in range(4):
                    column_sums(c_sum[:, :])
                kv_h, kv_l = slot(CKV)
                pe.wait_ge(low_ready, low.next(3))
                for t in range(8):
                    at = slice((t % 4) * P, (t % 4 + 1) * P)
                    product(tile(new_tile(), 256), (kv_h[:, t // 4, at], kv_l[:, t // 4, at]),
                            (z_h[:, :], z_l[:, :]), True, True).then_inc(tile_done, 1)
                lat = [[slot(CQ)[i][:, :, :], op] for i, op in enumerate((op_h, op_l))]
                pe.wait_ge(low_ready, low.next(4))
                split.skip(2)
                pe.wait_ge(w_split, split.at())
                wx, wy = (split.slot - 2) % SPLIT, (split.slot - 1) % SPLIT

                def q_latent(k, half):
                    return tuple(t[:, 0, 2 * k + half, :] for t in (op_h, op_l))

                def kv_latent(half):
                    return tuple(t[:, half, :] for t in slot(CKV))

                for pair in range(2):
                    for half in range(2):
                        to = tile(new_tile())
                        for k in range(2):
                            mm = product(to, weight(wy, k * 256 + pair * P), q_latent(k, half), k == 0, k == 1)
                        mm.then_inc(tile_done, 1)
                pe.wait_ge(low_ready, low.next(2 + 4))

                def attend(heads, scores, values, p_of, width_of, prob, prob_parts, prepare=None):
                    step = 0
                    for h in heads:
                        if prepare:
                            prepare(h)

                        def steps(i):
                            nonlocal step
                            n = width_of(2 * i) // 256
                            pe.wait_ge(part_ready, parts.next(2))
                            o = outr.slot
                            pe.wait_ge(out_read, outr.next())

                            def turn(j):
                                a = new_aux()
                                for kb in range(2):
                                    for q in range(2):
                                        mm = pe.transpose(aux(a, P, kb * 256 + q * P),
                                                          prob[:, (2 * i + q) % PROBS, (2 * j + kb) * P:(2 * j + kb + 1) * P],
                                                          ident)
                                mm.then_inc(aux_done, 1)

                            def use(j, s):
                                pe.wait_ge(aux_read, auxs.at(AUX - (0 if j == n - 1 else 1)))
                                for kb in range(2):
                                    mm = product(outs(o, 256), values(h, 2 * j + kb),
                                                 (prob_parts[0][:, s, kb * 256:(kb + 1) * 256],
                                                  prob_parts[1][:, s, kb * 256:(kb + 1) * 256]),
                                                 j == 0 and kb == 0, j == n - 1 and kb == 1)
                                mm.then_inc(out_step, 1)

                            for j in range(n):
                                turn(j)
                                if j:
                                    use(j - 1, (step + j - 1) % PARTS)
                            use(n - 1, (step + n - 1) % PARTS)
                            step += n

                        for i in range(4):
                            for q in (2 * i, 2 * i + 1):
                                scores(h, q)
                            if i:
                                steps(i - 1)
                        steps(3)

                pe.wait_ge(phase_done, phases.next())

                def latent_head(h):
                    for half in range(2):
                        to = tile(new_tile())
                        for k in range(2):
                            mm = product(to, weight(wx, k * 512 + h * P), q_latent(k, half), k == 0, k == 1)
                        mm.then_inc(tile_done, 1)
                    for half in range(2):
                        product(tile(new_tile()), weight(wy, 512 + h * P), kv_latent(half), True, True)\
                            .then_inc(tile_done, 1)
                    pe.wait_ge(tile_read, tiles.at(TILES))

                def latent_scores(h, q):
                    s = new_tile(2)
                    n = 256 * (q // 2 + 1)
                    kr = slot(KROPE + h % 2)
                    qr = slot(QROPE + h // 2)
                    at = slice((q % 4) * P, (q % 4 + 1) * P)
                    for c in range(0, n, 512):
                        w = min(512, n - c)
                        to = tile(s, w, c)
                        product(to, (m_qh[:, q * P:(q + 1) * P], m_ql[:, q * P:(q + 1) * P]),
                                (m_kh[:, c:c + w], m_kl[:, c:c + w]), True, False)
                        mm = product(to, tuple(t[:, q // 4, at] for t in qr),
                                     tuple(t[:, c // 512, 0:w] for t in kr), False, True)
                    mm.then_inc(tile_done, 2)

                attend(range(HEADS), latent_scores,
                       lambda h, kb: tuple(t[:, kb, (h // 2) * P:(h // 2 + 1) * P] for t in (m_vh, m_vl)),
                       None, lambda q: 256 * (q // 2 + 1), m_p, (m_ph, m_pl), latent_head)

                pe.wait_ge(phase_done, phases.next())
                column_sums(e_square[:, 0, :], MEM)
                pe.wait_ge(low_ready, low.next(2))
                for t in range(2):
                    s = split.slot
                    pe.wait_ge(w_split, split.next())
                    to = tile(new_tile(), MEM)
                    for k in range(KT):
                        mm = product(to, weight(s, k * P), (e_nh[:, k, :], e_nl[:, k, :]), k == 0, k == KT - 1)
                    mm.then_inc(tile_done, 1)
                s = split.slot
                pe.wait_ge(w_split, split.next(2))
                for t in range(2):
                    to = tile(new_tile(), MEM)
                    for k in range(KT):
                        mm = product(to, (e_nh[:, k, t * P:(t + 1) * P], e_nl[:, k, t * P:(t + 1) * P]),
                                     weight((s + k // 4) % SPLIT, (k % 4) * 256, 256), k == 0, k == KT - 1)
                    mm.then_inc(tile_done, 1)
                pe.wait_ge(tile_read, tiles.at(TILES))

                def memory_scores(h, q):
                    mq = slot(MQ + h // 2)
                    at = slice((q % 4) * P, (q % 4 + 1) * P)
                    product(tile(new_tile(), MEM), tuple(t[:, q // 4, at] for t in mq),
                            (e_kh[:, h, :], e_kl[:, h, :]), True, True).then_inc(tile_done, 1)

                attend(range(HEADS), memory_scores,
                       lambda h, kb: tuple(t[:, kb, (h // 2) * P:(h // 2 + 1) * P] for t in (e_vh, e_vl)),
                       None, lambda q: 256, e_p, (e_ph, e_pl))

                pe.wait_ge(phase_done, phases.next())
                for half in range(2):
                    for m in range(KT):
                        s = split.slot
                        pe.wait_ge(w_split, split.next())
                        project(half, s, op_h[:, half], op_l[:, half],
                                ready=half * KT if m == 0 else None)
                        if half == 1 and m in (0, 3):
                            column_sums(f_sum[:, :])
                low.skip(2 * KT)
                column_sums(f_sum[:, :])
                column_sums(f_sum[:, :])

                for half in range(2):
                    if half == 0:
                        low.skip(2 * KT)
                    for g, size in enumerate(GROUPS):
                        if g == 0:
                            pe.wait_ge(low_ready, low.at(0 if half else -KT))
                        with repeat(pe, size // 2, counts):
                            for s in range(4):
                                pe.wait_ge(w_split, split.next())
                                project(half, s, op_h[:, half], op_l[:, half])
                        with repeat(pe, 2, [c for c in counts if c is not low]):
                            for s in range(4):
                                pe.wait_ge(w_split, split.next())
                                project(half, s, a_h, a_l, depth=size, ready=0 if s == 0 else None)
                        low.skip(size)
                    column_sums(f_sum[:, :])
                    column_sums(f_sum[:, :])
                    low.skip(KT)

        @block.scalar
        def _(act):
            act.sem_inc(square_used, 2)
            done = Count(act, "act_tiles", TILES, TILES)
            auxd = Count(act, "act_aux", 0, AUX)
            outd = Count(act, "act_outs", 0)
            value = Count(act, "act_value")
            used = Count(act, "act_square_used", 0, 2)
            rs_used = Count(act, "act_rsqrt_used")
            high = Count(act, "act_high")
            out_ = Count(act, "act_out")
            sqr = Count(act, "act_square")
            log = Count(act, "act_log")
            rsq = Count(act, "act_rsqrt")
            ld = Count(act, "act_loaded")
            xs = Count(act, "act_x")
            st = Count(act, "act_stored")
            phases = Count(act, "act_phase")
            counts = [done, auxd, outd, value, used, rs_used, high, out_, sqr, log, rsq, ld, xs, st, phases]

            def to_high(to, source, scale=1.0):
                act.activation(to, source, ACT.Copy, scale=scale).then_inc(high_ready, 1)
                act.wait_ge(high_ready, high.next())

            def to_value(to, source, func, **more):
                act.activation(to, source, func, **more).then_inc(act_ready, 1)
                act.wait_ge(act_ready, out_.next())

            def square(to, source):
                act.activation(to, source, ACT.Square).then_inc(square_ready, 1)
                act.wait_ge(square_ready, sqr.next())

            def square_ring(ring, source):
                s = used.slot
                act.wait_ge(square_used, used.next())
                square(ring[:, s, :], source)

            def rsqrt(log_to, to, dim, n=HALF):
                s = auxd.slot
                act.wait_ge(aux_done, auxd.next())
                act.activation(log_to, aux(s, n), ACT.Ln, bias=eps, scale=1.0 / dim).then_inc(log_ready, 1)
                act.wait_ge(log_ready, log.next())
                act.wait_ge(rsqrt_used, rs_used.next())
                act.activation(to, log_to, ACT.Exp, scale=-0.5).then_inc(rsqrt_ready, 1)
                act.wait_ge(rsqrt_ready, rsq.next())

            def load_x(half, source):
                act.dma_start(x_buf[:, :, :], source[half]).then_inc(x_loaded, 16)

            def boundary(half, last):
                rsqrt(f_log[:, :], f_rsqrt[:, :], D)
                load_x(half, out)
                for m in range(KT):
                    act.wait_ge(x_ready, xs.next())
                    square_ring(f_square, x_buf[:, m, :])
                act.dma_start(out[half], x_buf[:, :, :]).then_inc(stored, 16)
                rsqrt(f_log[:, :], f_rsqrt[:, :], D)
                for m in range(KT):
                    act.wait_ge(value_ready, value.next())
                    to_high(op_h[:, half, m, :], f_hidden[:, m % 2, :])
                act.wait_ge(stored, st.next(16))

            act.dma_start(const[:, :], consts).then_inc(loaded, 16)
            act.dma_start(gain[:, 0:KT], first_gains).then_inc(loaded, 16)
            act.dma_start(s_pos[:, :], positions.partition_broadcast(P)).then_inc(loaded, 16)
            act.wait_ge(loaded, ld.next(48))
            for t in range(2):
                for f in range(2):
                    act.wait_ge(value_ready, value.next())
                    to_value(s_tab[:, f, :], s_ang[:, :], ACT.Sin,
                             scale=const[:, K_SIGN:K_SIGN + 1] if f else 1.0)
                act.dma_start(cos_sin[t], s_tab[:, :, :]).then_inc(stored, 16)
                act.wait_ge(stored, st.next(16))
            for half in range(2):
                if half == 0:
                    act.wait_ge(phase_done, phases.next())
                else:
                    act.wait_ge(value_ready, value.at())
                load_x(half, x)
                act.wait_ge(x_loaded, 16 * (half + 1))
                act.dma_start(out[half], x_buf[:, :, :]).then_inc(stored, 16)
                for m in range(KT):
                    square_ring(f_square, x_buf[:, m, :])
                rsqrt(f_log[:, :], f_rsqrt[:, :], D)
                for m in range(KT):
                    act.wait_ge(value_ready, value.next())
                    to_high(op_h[:, half, m, :], f_hidden[:, m % 2, :])
                act.wait_ge(stored, st.next(16))

            with repeat(act, LAYERS, counts) as l:
                act.wait_ge(phase_done, phases.next())
                act.dma_start(gain[:, :], gains[l]).then_inc(loaded, 16)
                act.dma_start(r_tab[:, :, :], cos_sin[0]).then_inc(loaded, 16)
                with repeat(act, HEADS, counts) as h:
                    act.dma_start(r_decay[:, :], decay[h]).then_inc(decay_loaded, 16)
                    for half in range(2):
                        cols = slice(half * HALF, (half + 1) * HALF)
                        for to in (r_qh, r_kh):
                            act.wait_ge(value_ready, value.next())
                            to_high(to[:, cols], r_t[:, 0, :])
                        done.skip(3)
                        s = done.slot
                        act.wait_ge(tile_done, done.next())
                        to_value(r_gate[:, cols], tile(s), ACT.Silu)
                        a = auxd.slot
                        act.wait_ge(aux_done, auxd.next())
                        to_high(r_vh[:, cols], aux(a))

                    def head_square(half, steps):
                        act.wait_ge(out_step, outd.at(SCORES + steps))
                        square(r_square[:, :], outs(half))

                    for i, (half, kb) in enumerate(STEPS):
                        c, diagonal = columns(half, kb)
                        s = done.slot
                        act.wait_ge(tile_done, done.next())
                        if diagonal:
                            act.wait_ge(value_ready, value.next())
                        act.wait_ge(out_step, outd.at(i + 1))
                        cross = 0 if kb < 4 * half else 1
                        to_high(r_sh[:, i % SCORES, 0:HALF - c], tile(s, HALF - c),
                                r_decay[:, SEQ + cross:SEQ + cross + 1])
                        if i == 6:
                            head_square(0, 4)
                        if i == 8:
                            rsqrt(r_log[:, :], r_rsqrt[:, :], P)
                    head_square(1, 12)
                    rsqrt(r_log[:, :], r_rsqrt[:, :], P)
                    outd.skip(12)
                ld.skip(32)

                act.wait_ge(phase_done, phases.next())
                act.dma_start(c_tab[:, :, :], cos_sin[1]).then_inc(loaded, 16)
                act.dma_start(z_raw[:, :], value_weights[l]).then_inc(loaded, 16)
                act.wait_ge(loaded, ld.next(32))
                to_high(z_h[:, :], z_raw[:, :])
                done.skip(12)

                def latent_square(n, sources):
                    for source in sources:
                        square_ring(c_square, source)

                act.wait_ge(value_ready, value.next())
                for half in range(2):
                    square_ring(c_square, c_kv[:, half * HALF:(half + 1) * HALF])
                    rsqrt(c_log[:, :], c_rsqrt[:, :], KVRANK)
                    act.wait_ge(value_ready, value.next())
                    to_high(slot(CKV)[0][:, half, :], c_norm[:, 0, :])
                for half in range(2):
                    for k in range(2):
                        square_ring(c_square, branch[:, half, 4 + k, :])
                    rsqrt(c_log[:, :], c_rsqrt[:, :], QRANK)
                    for k in range(2):
                        act.wait_ge(value_ready, value.next())
                        to_high(slot(CQ + k)[0][:, half, :], c_norm[:, k, :])
                for half in range(2):
                    act.wait_ge(value_ready, value.next())
                    for n in range(2):
                        to_high(slot(KROPE + n)[0][:, half, :], c_t[:, 0, :], const[:, K_PAIR + n:K_PAIR + n + 1])
                for t in range(8):
                    s = done.slot
                    act.wait_ge(tile_done, done.next())
                    to_high(m_vh[:, t, :], tile(s, 256))
                for pair in range(2):
                    for half in range(2):
                        done.skip(1)
                        act.wait_ge(value_ready, value.next())
                        to_high(slot(QROPE + pair)[0][:, half, :], c_t[:, 0, :])

                def attend(width_of, banks, scale, prob, parts_h, prepare=None):
                    step = 0
                    for h in range(HEADS):
                        if prepare:
                            prepare(h)

                        def softmax(q):
                            n = width_of(q)
                            s = done.slot
                            done.skip(banks)
                            act.wait_ge(value_ready, value.next())
                            to_value(prob[:, q % PROBS, 0:n], tile(s, n), ACT.Exp, scale=scale,
                                     bias=stat[:, 1, q:q + 1], accum_out=stat[:, 2, q:q + 1])

                        def steps(i):
                            nonlocal step
                            for j in range(width_of(2 * i) // 256):
                                a = auxd.slot
                                act.wait_ge(aux_done, auxd.next())
                                act.wait_ge(out_step, outd.next())
                                to_high(parts_h[:, step % PARTS, :], aux(a))
                                step += 1

                        for i in range(4):
                            softmax(2 * i)
                            softmax(2 * i + 1)
                            if i:
                                steps(i - 1)
                        steps(3)

                act.wait_ge(phase_done, phases.next())

                def latent_head(h):
                    for to in (m_qh, m_kh):
                        for half in range(2):
                            s = done.slot
                            act.wait_ge(tile_done, done.next())
                            to_high(to[:, half * HALF:(half + 1) * HALF], tile(s))

                attend(lambda q: 256 * (q // 2 + 1), 2, ATT_SCALE, m_p, m_ph, latent_head)

                act.wait_ge(phase_done, phases.next())
                act.dma_start(e_mem[:, :, :], mem).then_inc(loaded, 16)
                act.wait_ge(loaded, ld.next(16))
                square(e_square[:, :, :], e_mem[:, :, :])
                for k in range(2):
                    to_high(slot(MQ + k)[0], branch[:, :, 6 + k, :])
                rsqrt(e_log[:, :], e_rsqrt[:, :], D, MEM)
                act.wait_ge(value_ready, value.next())
                to_high(e_nh[:, :, :], e_mem[:, :, :])
                for t in range(2):
                    s = done.slot
                    act.wait_ge(tile_done, done.next())
                    for n in range(2):
                        to_high(e_kh[:, 2 * t + n, :], tile(s, MEM), const[:, K_HALVES + n:K_HALVES + n + 1])
                for t in range(2):
                    s = done.slot
                    act.wait_ge(tile_done, done.next())
                    to_high(e_vh[:, t, :], tile(s, MEM))
                attend(lambda q: 256, 1, MEM_SCALE, e_p, e_ph)

                act.wait_ge(phase_done, phases.next())

                def out_tile(half, m, first):
                    s = done.slot
                    act.wait_ge(tile_done, done.next())
                    to_value(branch[:, half, m, :], tile(s), ACT.Copy)
                    square_ring(f_square, tile(s))

                for half in range(2):
                    for m in range(KT):
                        to_high(op_h[:, half, m, :], branch[:, half, m, :])
                for half in range(2):
                    for m in range(KT):
                        out_tile(half, m, True)
                    if half == 0:
                        pass
                    boundary(half, False)

                for half in range(2):
                    for g, size in enumerate(GROUPS):
                        with repeat(act, size // 2, counts) as i:
                            for u in range(2):
                                s = done.slot
                                act.wait_ge(tile_done, done.next())
                                to_value(f_gate[:, u, :], tile(s), ACT.Silu)
                                done.skip(1)
                                act.wait_ge(value_ready, value.next())
                                to_high(a_h[:, i * 2 + u, :], f_hidden[:, u, :])
                        if g == 0:
                            done.skip(KT)
                        elif g == 1:
                            done.skip(KT)
                        else:
                            for m in range(KT):
                                done.skip(1)
                                act.wait_ge(value_ready, value.next())
                                square_ring(f_square, branch[:, half, m, :])
                    boundary(half, True)

        @block.vector
        def _(dve):
            dve.sem_inc(tile_read, TILES)
            dve.sem_inc(aux_read, AUX)
            dve.sem_inc(out_read, OUTS)
            dve.sem_inc(rsqrt_used, 1)
            done = Count(dve, "dve_tiles", TILES, TILES)
            auxd = Count(dve, "dve_aux", 0, AUX)
            outd = Count(dve, "dve_outs", SCORES)
            high = Count(dve, "dve_high")
            acts = Count(dve, "dve_act")
            sqr = Count(dve, "dve_square", 0, 2)
            rsq = Count(dve, "dve_rsqrt")
            ld = Count(dve, "dve_loaded")
            decays = Count(dve, "dve_decay_loaded")
            xl = Count(dve, "dve_x_loaded")
            link_ = Count(dve, "dve_linked")
            read = Count(dve, "dve_read", TILES)
            auxr = Count(dve, "dve_aux_read", AUX)
            outr = Count(dve, "dve_out_read", OUTS, OUTS)
            low = Count(dve, "dve_low")
            value = Count(dve, "dve_value")
            part = Count(dve, "dve_part")
            xr = Count(dve, "dve_x_ready")
            counts = [done, auxd, outd, high, acts, sqr, rsq, ld, decays, xl, link_, read, auxr, outr, low, value, part, xr]

            def link(instruction):
                instruction.then_inc(dve_link, 1)
                dve.wait_ge(dve_link, link_.next())

            def signal(instruction, semaphore, count):
                instruction.then_inc(semaphore, 1)
                dve.wait_ge(semaphore, count.next())

            def to_low(to, to_h, source):
                dve.wait_ge(high_ready, high.next())
                signal(dve.tensor_tensor(to, source, to_h.bitcast(F32), ALU.subtract), low_ready, low)

            def add_square(total, ring, first):
                s = sqr.slot
                dve.wait_ge(square_ready, sqr.next())
                if first:
                    link(dve.tensor_copy(total, ring[:, s, :]))
                else:
                    link(dve.tensor_tensor(total, total, ring[:, s, :], ALU.add))
                dve.sem_inc(square_used, 1)

            def take_rsqrt():
                dve.wait_ge(rsqrt_ready, rsq.next())
                auxd.skip(1)
                auxr.skip(1)
                dve.sem_inc(aux_read, 1)

            def norm_x(half, g):
                take_rsqrt()
                for m in range(KT + 1):
                    if m < KT:
                        signal(dve.scalar_tensor_tensor(
                            out=f_hidden[:, m % 2, :], in0=x_buf[:, m, :], scalar=gain[:, g + m:g + m + 1],
                            in1=f_rsqrt[:, :], op0=ALU.mult, op1=ALU.mult), value_ready, value)
                    if m:
                        to_low(op_l[:, half, m - 1, :], op_h[:, half, m - 1, :], f_hidden[:, (m - 1) % 2, :])
                dve.sem_inc(rsqrt_used, 1)

            def boundary(half, g_post, g_next):
                dve.sem_inc(sum_ready, 1)
                take_rsqrt()
                dve.wait_ge(x_loaded, xl.next(16))
                for m in range(KT + 1):
                    if m < KT:
                        y = branch[:, half, m, :]
                        link(dve.scalar_tensor_tensor(out=y, in0=y, scalar=gain[:, g_post + m:g_post + m + 1],
                                                      in1=f_rsqrt[:, :], op0=ALU.mult, op1=ALU.mult))
                        signal(dve.tensor_tensor(x_buf[:, m, :], x_buf[:, m, :], y, ALU.add), x_ready, xr)
                    if m == KT - 1:
                        dve.sem_inc(rsqrt_used, 1)
                    if m:
                        add_square(f_sum[:, :], f_square, m == 1)
                dve.sem_inc(sum_ready, 1)
                norm_x(half, g_next)

            dve.wait_ge(loaded, ld.next(48))
            link(dve.tensor_copy(s_posf[:, :], s_pos[:, :]))
            c1 = 6.28125
            c2 = float(np.round((TWO_PI - c1) * 2 ** 19) / 2 ** 19)
            c3 = float(np.float32(TWO_PI - c1 - c2))
            for t in range(2):
                for f in range(2):
                    quarter = 0.0 if f else 0.25
                    link(dve.tensor_scalar(s_ang[:, :], s_posf[:, :], const[:, K_FREQ + t:K_FREQ + t + 1], None,
                                           ALU.mult))
                    link(dve.tensor_scalar(s_turn[:, :], s_ang[:, :], 1.0 / TWO_PI, quarter, ALU.mult, ALU.add))
                    link(dve.tensor_scalar(s_turn[:, :], s_turn[:, :], MAGIC, -MAGIC, ALU.add, ALU.add))
                    for c in (c1, c2, c3):
                        link(dve.scalar_tensor_tensor(out=s_ang[:, :], in0=s_turn[:, :], scalar=-c,
                                                      in1=s_ang[:, :], op0=ALU.mult, op1=ALU.add))
                    if not f:
                        link(dve.tensor_scalar(s_ang[:, :], s_ang[:, :], np.pi / 2, None, ALU.add))
                    signal(dve.tensor_scalar(s_ang[:, :], s_ang[:, :], 3.1415925, -3.1415925, ALU.min, ALU.max),
                           value_ready, value)
                    dve.wait_ge(act_ready, acts.next())
            dve.sem_inc(phase_done, 1)

            for half in range(2):
                for m in range(KT):
                    add_square(f_sum[:, :], f_square, m == 0)
                dve.sem_inc(sum_ready, 1)
                norm_x(half, 0)
            xl.skip(32)
            dve.sem_inc(phase_done, 1)

            def rope(s, table, half, temp):
                cols = slice(half * HALF, (half + 1) * HALF)
                link(dve.tensor_tensor(temp[:, 1, :], tile(s), table[:, 0, cols], ALU.mult))
                link(dve.tensor_tensor(temp[0:64, 2, :], tile(s)[64:128], table[0:64, 1, cols], ALU.mult))
                signal(dve.tensor_tensor(temp[64:128, 2, :], tile(s)[0:64], table[64:128, 1, cols], ALU.mult),
                       tile_read, read)

            with repeat(dve, LAYERS, counts):
                dve.wait_ge(loaded, ld.next(32))
                with repeat(dve, HEADS, counts) as h:
                    dve.wait_ge(decay_loaded, decays.next(16))
                    for half in range(2):
                        cols = slice(half * HALF, (half + 1) * HALF)
                        for n, (th, tl) in enumerate(((r_qh, r_ql), (r_kh, r_kl))):
                            s = done.slot
                            dve.wait_ge(tile_done, done.next())
                            rope(s, r_tab, half, r_t)
                            if n:
                                signal(dve.tensor_tensor(r_t[:, 0, :], r_t[:, 1, :], r_t[:, 2, :], ALU.add),
                                       value_ready, value)
                            else:
                                link(dve.tensor_tensor(r_t[:, 1, :], r_t[:, 1, :], r_t[:, 2, :], ALU.add))
                                signal(dve.tensor_tensor(r_t[:, 0, :], r_t[:, 1, :], r_decay[:, 0:HALF], ALU.mult),
                                       value_ready, value)
                            to_low(tl[:, cols], th[:, cols], r_t[:, 0, :])
                        s = done.slot
                        dve.wait_ge(tile_done, done.next())
                        signal(dve.tensor_tensor(r_vt[:, :], tile(s), r_decay[:, HALF:SEQ], ALU.mult),
                               tile_read, read)
                        dve.sem_inc(part_ready, 1)
                        done.skip(1)
                        dve.wait_ge(act_ready, acts.next())
                        read.skip(1)
                        dve.sem_inc(tile_read, 1)
                        a = auxd.slot
                        auxd.skip(1)
                        dve.wait_ge(high_ready, high.next())
                        signal(dve.tensor_tensor(r_vl[:, cols], aux(a), r_vh[:, cols].bitcast(F32), ALU.subtract),
                               aux_read, auxr)

                    def head_out(half):
                        take_rsqrt()
                        link(dve.tensor_tensor(r_t[:, 1, :], outs(half), r_rsqrt[:, :], ALU.mult))
                        dve.sem_inc(rsqrt_used, 1)
                        outr.skip(1)
                        dve.sem_inc(out_read, 1)
                        link(dve.tensor_tensor(branch[:, half, h, :], r_t[:, 1, :],
                                               r_gate[:, half * HALF:(half + 1) * HALF], ALU.mult))

                    for i, (half, kb) in enumerate(STEPS):
                        c, diagonal = columns(half, kb)
                        s = done.slot
                        dve.wait_ge(tile_done, done.next())
                        if diagonal:
                            local = kb - 4 * half
                            n = 256 if local == 3 else P
                            view = tile(s, n)
                            signal(dve.tensor_tensor(view, view, tri[:, 256 - n:256], ALU.mult), value_ready, value)
                        cross = 0 if kb < 4 * half else 1
                        dve.wait_ge(high_ready, high.next())
                        signal(dve.scalar_tensor_tensor(
                            out=r_sl[:, i % SCORES, 0:HALF - c], in0=tile(s, HALF - c),
                            scalar=r_decay[:, SEQ + cross:SEQ + cross + 1],
                            in1=r_sh[:, i % SCORES, 0:HALF - c].bitcast(F32),
                            op0=ALU.mult, op1=ALU.subtract), tile_read, read)
                        if i == 6:
                            sqr.other()
                        if i == 9:
                            head_out(0)
                    sqr.other()
                    head_out(1)
                    outd.skip(12)
                dve.sem_inc(phase_done, 1)

                dve.wait_ge(loaded, ld.next(32))
                to_low(z_l[:, :], z_h[:, :], z_raw[:, :])
                raw = [[branch[:, half, 4, :], branch[:, half, 5, :], c_kv[:, half * HALF:(half + 1) * HALF],
                        c_kr[:, half * HALF:(half + 1) * HALF]] for half in range(2)]
                raw += [[branch[:, half, 6, :], branch[:, half, 7, :]] for half in range(2)]
                for group in raw:
                    for to in group:
                        s = done.slot
                        dve.wait_ge(tile_done, done.next())
                        signal(dve.tensor_copy(to, tile(s)), tile_read, read)
                value.skip(1)
                dve.sem_inc(value_ready, 1)
                for half in range(2):
                    add_square(c_sum[:, :], c_square, True)
                    dve.sem_inc(sum_ready, 1)
                    take_rsqrt()
                    signal(dve.scalar_tensor_tensor(
                        out=c_norm[:, 0, :], in0=c_kv[:, half * HALF:(half + 1) * HALF],
                        scalar=gain[:, G_KV:G_KV + 1], in1=c_rsqrt[:, :], op0=ALU.mult, op1=ALU.mult),
                        value_ready, value)
                    dve.sem_inc(rsqrt_used, 1)
                    to_low(slot(CKV)[1][:, half, :], slot(CKV)[0][:, half, :], c_norm[:, 0, :])
                for half in range(2):
                    for k in range(2):
                        add_square(c_sum[:, :], c_square, k == 0)
                    dve.sem_inc(sum_ready, 1)
                    take_rsqrt()
                    for k in range(2):
                        signal(dve.scalar_tensor_tensor(
                            out=c_norm[:, k, :], in0=branch[:, half, 4 + k, :],
                            scalar=gain[:, G_Q + k:G_Q + k + 1], in1=c_rsqrt[:, :], op0=ALU.mult, op1=ALU.mult),
                            value_ready, value)
                    dve.sem_inc(rsqrt_used, 1)
                    for k in range(2):
                        to_low(slot(CQ + k)[1][:, half, :], slot(CQ + k)[0][:, half, :], c_norm[:, k, :])
                for half in range(2):
                    cols = slice(half * HALF, (half + 1) * HALF)
                    link(dve.tensor_tensor(c_t[:, 1, :], c_kr[:, cols], c_tab[:, 0, cols], ALU.mult))
                    link(dve.tensor_copy(c_t[0:64, 2, :], c_kr[64:128, cols]))
                    link(dve.tensor_copy(c_t[64:128, 2, :], c_kr[0:64, cols]))
                    link(dve.tensor_tensor(c_t[:, 2, :], c_t[:, 2, :], c_tab[:, 1, cols], ALU.mult))
                    signal(dve.tensor_tensor(c_t[:, 0, :], c_t[:, 1, :], c_t[:, 2, :], ALU.add), value_ready, value)
                    for n in range(2):
                        dve.wait_ge(high_ready, high.next())
                        link(dve.scalar_tensor_tensor(
                            out=slot(KROPE + n)[1][:, half, :], in0=c_t[:, 0, :],
                            scalar=const[:, K_PAIR + n:K_PAIR + n + 1],
                            in1=slot(KROPE + n)[0][:, half, :].bitcast(F32), op0=ALU.mult, op1=ALU.subtract))
                    low.skip(1)
                    dve.sem_inc(low_ready, 1)
                for t in range(8):
                    s = done.slot
                    done.skip(1)
                    dve.wait_ge(high_ready, high.next())
                    signal(dve.tensor_tensor(m_vl[:, t, :], tile(s, 256), m_vh[:, t, :].bitcast(F32), ALU.subtract),
                           tile_read, read)
                for pair in range(2):
                    for half in range(2):
                        s = done.slot
                        dve.wait_ge(tile_done, done.next())
                        rope(s, c_tab, half, c_t)
                        signal(dve.tensor_tensor(c_t[:, 0, :], c_t[:, 1, :], c_t[:, 2, :], ALU.add),
                               value_ready, value)
                        to_low(slot(QROPE + pair)[1][:, half, :], slot(QROPE + pair)[0][:, half, :], c_t[:, 0, :])
                dve.sem_inc(phase_done, 1)

                def attend(width_of, banks, scale, masked, prob, parts_h, parts_l, to_tile, prepare=None):
                    step = 0
                    for h in range(HEADS):
                        if prepare:
                            prepare(h)

                        def maximum(q):
                            n = width_of(q)
                            s = done.slot
                            dve.wait_ge(tile_done, done.next(banks))
                            if masked:
                                view = tile(s, 256, n - 256)
                                at = K_CAUSAL + 256 * (q % 2)
                                link(dve.tensor_tensor(view, view, const[:, at:at + 256], ALU.add))
                            link(dve.reduce_max(stat[:, 0, q:q + 1], tile(s, n), AX.X))
                            signal(dve.tensor_scalar(stat[:, 1, q:q + 1], stat[:, 0, q:q + 1], -scale, None, ALU.mult),
                                   value_ready, value)

                        def normalise(q):
                            n = width_of(q)
                            dve.wait_ge(act_ready, acts.next())
                            read.skip(banks)
                            dve.sem_inc(tile_read, banks)
                            link(dve.reciprocal(stat[:, 3, q:q + 1], stat[:, 2, q:q + 1]))
                            signal(dve.tensor_scalar(prob[:, q % PROBS, 0:n], prob[:, q % PROBS, 0:n],
                                                     stat[:, 3, q:q + 1], None, ALU.mult), part_ready, part)

                        def steps(i):
                            nonlocal step
                            n = width_of(2 * i) // 256
                            for j in range(n):
                                a = auxd.slot
                                auxd.skip(1)
                                dve.wait_ge(high_ready, high.next())
                                signal(dve.tensor_tensor(parts_l[:, step % PARTS, :], aux(a),
                                                         parts_h[:, step % PARTS, :].bitcast(F32), ALU.subtract),
                                       aux_read, auxr)
                                step += 1
                            o = outr.slot
                            dve.wait_ge(out_step, outd.next(n))
                            rows = slice(64 * (h % 2), 64 * (h % 2) + 64)
                            to = branch[rows, i // 2, to_tile + h // 2, (i % 2) * 256:(i % 2) * 256 + 256]
                            signal(dve.tensor_copy(to, outs(o, 256)[rows]), out_read, outr)

                        for i in range(4):
                            maximum(2 * i)
                            maximum(2 * i + 1)
                            normalise(2 * i)
                            normalise(2 * i + 1)
                            if i:
                                steps(i - 1)
                        steps(3)

                def latent_head(h):
                    for th, tl in ((m_qh, m_ql), (m_kh, m_kl)):
                        for half in range(2):
                            cols = slice(half * HALF, (half + 1) * HALF)
                            s = done.slot
                            done.skip(1)
                            dve.wait_ge(high_ready, high.next())
                            signal(dve.tensor_tensor(tl[:, cols], tile(s), th[:, cols].bitcast(F32), ALU.subtract),
                                   tile_read, read)

                attend(lambda q: 256 * (q // 2 + 1), 2, ATT_SCALE, True, m_p, m_ph, m_pl, 4, latent_head)
                dve.sem_inc(phase_done, 1)

                ld.skip(16)
                sqr.other()
                dve.wait_ge(square_ready, sqr.at())
                for k in range(1, KT):
                    link(dve.tensor_tensor(e_square[:, 0, :], e_square[:, 0, :], e_square[:, k, :], ALU.add))
                dve.sem_inc(sum_ready, 1)
                for k in range(2):
                    dve.wait_ge(high_ready, high.next())
                    link(dve.tensor_tensor(slot(MQ + k)[1], branch[:, :, 6 + k, :], slot(MQ + k)[0].bitcast(F32),
                                           ALU.subtract))
                low.skip(1)
                dve.sem_inc(low_ready, 1)
                take_rsqrt()
                for k in range(KT):
                    link(dve.scalar_tensor_tensor(
                        out=e_mem[:, k, :], in0=e_mem[:, k, :], scalar=gain[:, G_MEM + k:G_MEM + k + 1],
                        in1=e_rsqrt[:, :], op0=ALU.mult, op1=ALU.mult))
                dve.sem_inc(rsqrt_used, 1)
                value.skip(1)
                dve.sem_inc(value_ready, 1)
                to_low(e_nl[:, :, :], e_nh[:, :, :], e_mem[:, :, :])
                for t in range(2):
                    s = done.slot
                    done.skip(1)
                    dve.wait_ge(high_ready, high.next(2))
                    for n in range(2):
                        ins = dve.scalar_tensor_tensor(
                            out=e_kl[:, 2 * t + n, :], in0=tile(s, MEM), scalar=const[:, K_HALVES + n:K_HALVES + n + 1],
                            in1=e_kh[:, 2 * t + n, :].bitcast(F32), op0=ALU.mult, op1=ALU.subtract)
                        if n:
                            signal(ins, tile_read, read)
                        else:
                            link(ins)
                for t in range(2):
                    s = done.slot
                    done.skip(1)
                    dve.wait_ge(high_ready, high.next())
                    signal(dve.tensor_tensor(e_vl[:, t, :], tile(s, MEM), e_vh[:, t, :].bitcast(F32), ALU.subtract),
                           tile_read, read)
                attend(lambda q: 256, 1, MEM_SCALE, False, e_p, e_ph, e_pl, 6)
                dve.sem_inc(phase_done, 1)

                for half in range(2):
                    for m in range(KT):
                        to_low(op_l[:, half, m, :], op_h[:, half, m, :], branch[:, half, m, :])
                for half in range(2):
                    for m in range(KT):
                        done.skip(1)
                        dve.wait_ge(act_ready, acts.next())
                        add_square(f_sum[:, :], f_square, m == 0)
                        read.skip(1)
                        dve.sem_inc(tile_read, 1)
                    boundary(half, G_POST_MIX, G_PRE_FFN)

                for half in range(2):
                    for g, size in enumerate(GROUPS):
                        with repeat(dve, size // 2, counts) as i:
                            for u in range(2):
                                done.skip(1)
                                s = done.slot
                                dve.wait_ge(tile_done, done.next())
                                dve.wait_ge(act_ready, acts.next())
                                signal(dve.tensor_tensor(f_hidden[:, u, :], f_gate[:, u, :], tile(s), ALU.mult),
                                       value_ready, value)
                                read.skip(2)
                                dve.sem_inc(tile_read, 2)
                                to_low(a_l[:, i * 2 + u, :], a_h[:, i * 2 + u, :], f_hidden[:, u, :])
                        for m in range(KT + (g == 2)):
                            if m < KT:
                                s = done.slot
                                dve.wait_ge(tile_done, done.next())
                                y = branch[:, half, m, :]
                                if g == 0:
                                    signal(dve.tensor_copy(y, tile(s)), tile_read, read)
                                else:
                                    signal(dve.tensor_tensor(y, y, tile(s), ALU.add), tile_read, read)
                                if g == 2:
                                    value.skip(1)
                                    dve.sem_inc(value_ready, 1)
                            if g == 2 and m:
                                add_square(f_sum[:, :], f_square, m == 1)
                    boundary(half, G_POST_FFN, G_NEXT)
                dve.sem_inc(phase_done, 1)


def _block(w):
    k, n = w.shape
    return w.reshape(k // P, P, n).transpose(1, 0, 2).reshape(P, -1)


def _layer_blocks(w_in, w_uq, w_ukv, w_mem_kv, w_out, w_gate, w_up, w_down):
    cols = lambda w, at, n=P: _block(w[:, at:at + n])
    found = []
    for h in range(HEADS):
        found += [cols(w_in, part * 512 + h * P) for part in range(4)]
    rope_key = w_in[:, 2432:2496]
    rope_key = np.concatenate([rope_key[:, :32]] * 2 + [rope_key[:, 32:]] * 2, 1)
    found += [cols(w_in, 2048), cols(w_in, 2176), cols(w_in, 2304), _block(rope_key)]
    found += [cols(w_in, 2496), cols(w_in, 2624)]
    uq = w_uq.reshape(QRANK, HEADS, NOPE + ROPE)
    ukv = w_ukv.reshape(KVRANK, HEADS, NOPE + VDIM)
    found += [_block(uq[:, :, :NOPE].reshape(QRANK, -1))]
    rope_q = uq[:, :, NOPE:].reshape(QRANK, 2, 2, 2, 32).transpose(0, 1, 3, 2, 4).reshape(QRANK, -1)
    found += [np.concatenate([_block(rope_q), ukv[:, :, :NOPE].reshape(KVRANK, -1)], 1)]
    found += [cols(w_mem_kv, 0), cols(w_mem_kv, P)]
    found += [_block(w_mem_kv[k * 512:(k + 1) * 512, 256:]) for k in range(2)]
    found += [cols(w_out, m * P) for m in range(KT)]
    at = 0
    for size in GROUPS:
        for j in range(at, at + size):
            found += [cols(w_gate, j * P), cols(w_up, j * P)]
        rows = w_down[at * P:(at + size) * P]
        found += [np.pad(cols(rows, m * P), ((0, 0), (0, BLOCK - size * P))) for m in range(KT)]
        at += size
    return np.stack(found), np.ascontiguousarray(ukv[:, :, NOPE:].reshape(KVRANK, -1))


def _constants():
    c = np.zeros((P, K_ALL), np.float32)
    row, col = np.arange(P)[:, None], np.arange(P)[None, :]
    c[:, K_ID:K_ID + P] = row == col
    c[:, K_ONES:K_ONES + P] = 1.0
    c[:, K_TRI + P:K_TRI + 2 * P] = col >= row
    low = np.where(col > row, -3.0e38, 0.0)
    c[:, K_CAUSAL:K_CAUSAL + P] = low
    c[:, K_CAUSAL + P:K_CAUSAL + 2 * P] = -3.0e38
    c[:, K_CAUSAL + 3 * P:K_CAUSAL + 4 * P] = low
    for n in range(2):
        c[:, K_PAIR + n] = np.arange(P) // 32 % 2 == n
        c[:, K_HALVES + n] = np.arange(P) // 64 == n
    c[:, K_EPS] = EPS
    c[:, K_SIGN] = np.where(np.arange(P) < 64, -1.0, 1.0)
    for t, half in enumerate((64, 32)):
        c[:, K_FREQ + t] = np.float32(10000.0) ** (-(np.arange(P) % half).astype(np.float32) / np.float32(half))
    return c


def _decay():
    d = np.zeros((HEADS, P, SEQ + 2), np.float32)
    j = np.arange(HALF)
    for h in range(HEADS):
        g = 1.0 - 2.0 ** (-5.0 - h)
        d[h, :, 0:HALF] = g ** j * float(P) ** -0.5
        d[h, :, HALF:SEQ] = g ** -j.astype(np.float64)
        d[h, :, SEQ] = g ** HALF
        d[h, :, SEQ + 1] = 1.0
    return d


def kernel(x, mem, positions, pre_mix_g, w_in, mla_q_norm_g, w_uq, mla_kv_norm_g, w_ukv, mem_norm_g, w_mem_kv,
           w_out, post_mix_g, pre_ffn_g, w_gate, w_up, w_down, post_ffn_g):
    from concourse import bacc
    from concourse.bass_utils import run_bass_kernel_spmd

    names = (x, mem, positions, pre_mix_g, w_in, mla_q_norm_g, w_uq, mla_kv_norm_g, w_ukv, mem_norm_g, w_mem_kv,
             w_out, post_mix_g, pre_ffn_g, w_gate, w_up, w_down, post_ffn_g)
    (x, mem, positions, pre_mix_g, w_in, mla_q_norm_g, w_uq, mla_kv_norm_g, w_ukv, mem_norm_g, w_mem_kv,
     w_out, post_mix_g, pre_ffn_g, w_gate, w_up, w_down, post_ffn_g) = [np.asarray(a) for a in names]

    by_tile = lambda g: g.reshape(-1, P).T
    layers = [_layer_blocks(w_in[l], w_uq[l], w_ukv[l], w_mem_kv[l], w_out[l], w_gate[l], w_up[l], w_down[l])
              for l in range(LAYERS)]
    gains = np.stack([np.concatenate(
        [by_tile(mla_q_norm_g[l]), by_tile(mla_kv_norm_g[l]), by_tile(mem_norm_g[l]), by_tile(post_mix_g[l]),
         by_tile(pre_ffn_g[l]), by_tile(post_ffn_g[l]), by_tile(pre_mix_g[min(l + 1, LAYERS - 1)])], 1)
        for l in range(LAYERS)])
    arrays = {
        "x_in": x[0].T.reshape(KT, P, 2, HALF).transpose(2, 1, 0, 3),
        "mem_in": mem[0].T.reshape(KT, P, MEM).transpose(1, 0, 2),
        "positions_in": positions[0],
        "weights_in": np.concatenate([b for b, _ in layers]),
        "value_weights_in": np.stack([v for _, v in layers]),
        "gains_in": gains,
        "first_gains_in": by_tile(pre_mix_g[0]),
        "consts_in": _constants(),
        "decay_in": _decay(),
    }
    arrays = {n: np.ascontiguousarray(a) for n, a in arrays.items()}
    nc = bacc.Bacc("TRN2", target_bir_lowering=False, num_devices=1)
    aps = [nc.dram_tensor(n, a.shape, mybir.dt.from_np(a.dtype), kind="ExternalInput").ap()
           for n, a in arrays.items()]
    out = nc.dram_tensor("out_0_dram", (2, P, KT, HALF), F32, kind="ExternalOutput").ap()
    build(nc, *aps, out)
    r = run_bass_kernel_spmd(nc, [arrays], core_ids=[0])
    y = r.results[0]["out_0_dram"]
    return np.ascontiguousarray(y.transpose(2, 1, 0, 3).reshape(D, SEQ).T)[None]
```

```python
from contextlib import ExitStack, contextmanager

import numpy as np

import concourse.bass as bass
from concourse import mybir

ALU = mybir.AluOpType
ACT = mybir.ActivationFunctionType
AX = mybir.AxisListType
F32 = mybir.dt.float32
F32R = mybir.dt.float32r
I32 = mybir.dt.int32

P = 128
LAYERS = 2
SEQ = 1024
D = 1024
HALF = 512
KT = D // P
HEADS = 4
MEM = 256
QRANK = 256
KVRANK = 128
NOPE, ROPE, VDIM = 128, 64, 64
D_FF = 2816
GROUPS = (8, 8, 6)
BLOCK = 1024
MIXER_BLOCKS, OUT_BLOCKS, FFN_BLOCKS = 28, 8, 68
STORED_BLOCKS = MIXER_BLOCKS + OUT_BLOCKS + FFN_BLOCKS
EPS = 1e-6
LAYER_TILES = 332
ATT_SCALE = float(NOPE + ROPE) ** -0.5
MEM_SCALE = float(64) ** -0.5

RAW, SPLIT, TILES, AUX, OUTS = 2, 4, 4, 2, 2
X_TILES = 4
SCORES, PARTS = 4, 3

G_Q, G_KV, G_MEM, G_POST_MIX, G_PRE_FFN, G_POST_FFN, G_NEXT = 0, 2, 3, 11, 19, 27, 35
GAINS = 43

K_ID, K_ONES, K_TRI, K_CAUSAL, K_COLS = 0, 128, 256, 512, 1024
K_PAIR, K_HALVES, K_EPS, K_SIGN, K_FREQ, K_TURN, K_SHIFT, K_ALL = 1024, 1026, 1028, 1029, 1030, 1032, 1033, 1034

TWO_PI = 2.0 * np.pi
MAGIC = 12582912.0


class Count:

    def __init__(self, engine, name, start=0, ring=1):
        self.engine, self.ring, self.slot, self.since = engine, ring, 0, 0
        self.base = engine.alloc_register(name)
        engine.reg_mov(self.base, start)

    def at(self, ahead=0):
        return self.engine.snap(self.base) + (self.since + ahead)

    def next(self, n=1):
        self.skip(n)
        return self.at()

    def skip(self, n=1):
        self.since += n
        self.slot = (self.slot + n) % self.ring

    def other(self, n=1):
        self.since += n

    def fold(self):
        if self.since:
            self.engine.reg_add(self.base, self.base, self.since)
            self.since = 0


@contextmanager
def repeat(engine, times, counts):
    for c in counts:
        c.fold()
    with engine.Fori(0, times) as i:
        yield i
        for c in counts:
            c.fold()


def build(nc, x, mem, positions, weights, value_weights, gains, consts, decay, scales, out):
    cos_sin = nc.dram_tensor("cos_sin", (2, P, 2, SEQ), F32, kind="Internal").ap()
    with ExitStack() as ctx:
        def sb(name, shape, dt=F32, within=None):
            return (within or ctx).enter_context(nc.sbuf_tensor(name, [P] + shape, dt))

        def sem(name):
            return ctx.enter_context(nc.semaphore(name))

        op_h, op_l = sb("op_high", [2, KT, HALF], F32R), sb("op_low", [2, KT, HALF], F32R)
        w_raw = sb("w_raw", [RAW, BLOCK])
        w_h, w_l = sb("w_high", [SPLIT, BLOCK], F32R), sb("w_low", [SPLIT, BLOCK], F32R)
        branch = sb("branch", [2, KT, HALF])
        const = sb("const", [K_ALL])
        gain = sb("gain", [GAINS])
        head_scales = sb("head_scales", [HEADS, 8])
        stat = sb("stat", [4, 8])
        ident, ones = const[:, K_ID:K_ID + P], const[:, K_ONES:K_ONES + P]
        tri = const[:, K_TRI:K_TRI + 256]
        eps = const[:, K_EPS:K_EPS + 1]

        phase = ExitStack()
        x_old = sb("x_old", [X_TILES, HALF], F32, phase)
        b_square, f_square = sb("b_square", [2, HALF], F32, phase), sb("f_square", [2, HALF], F32, phase)
        f_sum = sb("f_sum", [2, HALF], F32, phase)
        b_rsqrt = sb("b_rsqrt", [HALF], F32, phase)
        b_norm = sb("b_norm", [2, HALF], F32, phase)
        f_gate, f_hidden = sb("f_gate", [2, HALF], F32, phase), sb("f_hidden", [2, HALF], F32, phase)
        start = ExitStack()
        s_pos, s_posf = sb("s_pos", [SEQ], I32, start), sb("s_posf", [SEQ], F32, start)
        s_ang, s_turn = sb("s_ang", [SEQ], F32, start), sb("s_turn", [SEQ], F32, start)
        s_tab = sb("s_tab", [2, SEQ], F32, start)
        start.close()
        a_h, a_l = sb("a_high", [8, HALF], F32R, phase), sb("a_low", [8, HALF], F32R, phase)
        phase.close()

        phase = ExitStack()
        r_qh, r_ql = sb("r_q_high", [SEQ], F32R, phase), sb("r_q_low", [SEQ], F32R, phase)
        r_kh, r_kl = sb("r_k_high", [SEQ], F32R, phase), sb("r_k_low", [SEQ], F32R, phase)
        r_vh, r_vl = sb("r_v_high", [SEQ], F32R, phase), sb("r_v_low", [SEQ], F32R, phase)
        r_sh, r_sl = sb("r_s_high", [SCORES, HALF], F32R, phase), sb("r_s_low", [SCORES, HALF], F32R, phase)
        r_vt = sb("r_v_transposed", [HALF], F32, phase)
        r_gate = sb("r_gate", [SEQ], F32, phase)
        r_tab = sb("r_cos_sin", [2, SEQ], F32, phase)
        r_decay, r_scale = sb("r_decay", [HALF], F32, phase), sb("r_scale", [8], F32, phase)
        r_t = sb("r_temp", [3, HALF], F32, phase)
        r_square = sb("r_square", [HALF], F32, phase)
        r_rsqrt = sb("r_rsqrt", [HALF], F32, phase)
        phase.close()

        phase = ExitStack()
        m_vh, m_vl = sb("m_v_high", [8, 256], F32R, phase), sb("m_v_low", [8, 256], F32R, phase)
        latent = ExitStack()
        c_kv, c_kr = sb("c_kv", [SEQ], F32, latent), sb("c_kr", [SEQ], F32, latent)
        c_tab = sb("c_cos_sin", [2, SEQ], F32, latent)
        c_t = sb("c_temp", [3, HALF], F32, latent)
        c_square, c_sum = sb("c_square", [2, HALF], F32, latent), sb("c_sum", [HALF], F32, latent)
        c_log, c_rsqrt = sb("c_log", [HALF], F32, latent), sb("c_rsqrt", [HALF], F32, latent)
        c_norm = sb("c_norm", [2, HALF], F32, latent)
        z_raw = sb("z_raw", [256], F32, latent)
        z_h, z_l = sb("z_high", [256], F32R, latent), sb("z_low", [256], F32R, latent)
        latent.close()
        m_qh, m_ql = sb("m_q_high", [SEQ], F32R, phase), sb("m_q_low", [SEQ], F32R, phase)
        m_kh, m_kl = sb("m_k_high", [SEQ], F32R, phase), sb("m_k_low", [SEQ], F32R, phase)
        m_p = sb("m_p", [20 * 256], F32, phase)
        m_ph, m_pl = sb("m_p_high", [PARTS, 512], F32R, phase), sb("m_p_low", [PARTS, 512], F32R, phase)
        phase.close()

        phase = ExitStack()
        e_mem = sb("e_mem", [KT, MEM], F32, phase)
        e_square = sb("e_square", [KT, MEM], F32, phase)
        e_nh, e_nl = sb("e_norm_high", [KT, MEM], F32R, phase), sb("e_norm_low", [KT, MEM], F32R, phase)
        e_kh, e_kl = sb("e_k_high", [HEADS, MEM], F32R, phase), sb("e_k_low", [HEADS, MEM], F32R, phase)
        e_vh, e_vl = sb("e_v_high", [2, 256], F32R, phase), sb("e_v_low", [2, 256], F32R, phase)
        e_p = sb("e_p", [8 * MEM], F32, phase)
        e_ph, e_pl = sb("e_p_high", [PARTS, 512], F32R, phase), sb("e_p_low", [PARTS, 512], F32R, phase)
        e_log, e_rsqrt = sb("e_log", [MEM], F32, phase), sb("e_rsqrt", [MEM], F32, phase)
        phase.close()

        def slot(n):
            return [t[:, n // 4, 2 * (n % 4):2 * (n % 4) + 2, :] for t in (op_h, op_l)]

        CQ, KROPE, CKV, QROPE, MQ = 0, 2, 4, 5, 0

        def latent_width(q):
            return 256 * (q // 2 + 1)

        def latent_probs(q, at=0, n=None):
            pair, width = q // 2, latent_width(q)
            start = 256 * pair * (pair + 1) + (q % 2) * width + at
            return m_p[:, start:start + (n or width)]

        def memory_width(q):
            return MEM

        def memory_probs(q, at=0, n=None):
            return e_p[:, q * MEM + at:q * MEM + at + (n or MEM)]

        def attention_order(head, next_head, steps, mixed):
            mixed(head, 0, (head - 1, 3) if head else None)
            mixed(head, 1, None)
            mixed(head, 2, (head, 0))
            mixed(head, 3, (head, 1))
            next_head(head + 1)
            steps(head, 2)
            if head == HEADS - 1:
                steps(head, 3)

        psum = ctx.enter_context(nc.psum_tensor("psum", [P, 8 * 512], F32))

        def tile(s, n=512, at=0):
            return psum[:, s * 512 + at:s * 512 + at + n]

        def aux(s, n=512, at=0):
            return psum[:, (TILES + s) * 512 + at:(TILES + s) * 512 + at + n]

        def outs(s, n=512, at=0):
            return psum[:, (TILES + AUX + s) * 512 + at:(TILES + AUX + s) * 512 + at + n]

        w_loaded = [sem(f"w_loaded{i}") for i in range(RAW)]
        loaded = sem("loaded")
        decay_loaded = sem("decay_loaded")
        x_loaded = [sem(f"x_loaded{i}") for i in range(X_TILES)]
        stored = [sem(f"x_stored{i}") for i in range(2)]
        tables_stored = sem("tables_stored")
        w_rounded = sem("w_rounded")
        w_split = sem("w_split")
        pool_waited = sem("pool_waited")
        tile_done = sem("tile_done")
        aux_done = sem("aux_done")
        out_step = sem("out_step")
        norm_sums_done = sem("norm_sums_done")
        tile_read = sem("tile_read")
        aux_read = sem("aux_read")
        out_read = sem("out_read")
        dve_link = sem("dve_link")
        low_ready = sem("low_ready")
        value_ready = sem("value_ready")
        sum_ready = sem("sum_ready")
        part_ready = sem("part_ready")
        square_used = sem("square_used")
        rsqrt_used = sem("rsqrt_used")
        x_ready = sem("x_ready")
        norm_sum_ready = sem("norm_sum_ready")
        norm_square_used = sem("norm_square_used")
        norm_value_ready = sem("norm_value_ready")
        norm_low_ready = sem("norm_low_ready")
        phase_done = sem("phase_done")
        high_ready = sem("high_ready")
        act_ready = sem("act_ready")
        square_ready = sem("square_ready")
        log_ready = sem("log_ready")
        rsqrt_ready = sem("rsqrt_ready")
        norm_square_ready = sem("norm_square_ready")
        norm_high_ready = sem("norm_high_ready")
        norm_rsqrt_ready = sem("norm_rsqrt_ready")

        finished = sem("finished")

        block = ctx.enter_context(nc.Block())

        def step_index(half, kb):
            return 4 * half + kb

        def scale_of(half, kb):
            i = kb - 4 * half if kb >= 4 * half else 4 + kb
            return r_scale[:, i:i + 1]

        def columns(half, kb):
            local = kb - 4 * half
            return (0, False) if local < 0 else (min(128 * local, 256), True)

        @block.sync
        def _(sp):
            split = Count(sp, "sp_split", 0, RAW)

            def load(index):
                s = split.slot
                sp.wait_ge(w_split, split.next())
                sp.dma_start(w_raw[:, s, :], weights[index]).then_inc(w_loaded[s], 16)

            layer = Count(sp, "sp_layer")
            with sp.Fori(0, LAYERS) as l:
                def run(first, n):
                    split.fold()
                    with sp.Fori(0, n // RAW) as i:
                        for s in range(RAW):
                            load(l * STORED_BLOCKS + i * RAW + (first + s))
                        split.fold()
                run(0, 20)
                run(0, 4)
                run(20, MIXER_BLOCKS - 20)
                for half in range(2):
                    run(MIXER_BLOCKS, OUT_BLOCKS)
                for half in range(2):
                    run(MIXER_BLOCKS + OUT_BLOCKS, FFN_BLOCKS)

        @block.gpsimd
        def _(pool):
            pool.sem_inc(w_split, RAW)
            raw = [Count(pool, f"pool_loaded{i}") for i in range(RAW)]
            rounded = Count(pool, "pool_rounded")
            split = Count(pool, "pool_split", RAW)
            done = Count(pool, "pool_tiles", TILES)
            turn = [0]

            def counted():
                pool.sem_inc(pool_waited, 1)

            def block_split(last_use, more=0):
                r, s = turn[0] % RAW, turn[0] % SPLIT
                turn[0] += 1
                pool.wait_ge(w_loaded[r], raw[r].next(16))
                counted()
                pool.wait_ge(tile_done, done.at(last_use + 1) + more)
                counted()
                pool.tensor_scalar(w_h[:, s, :], w_raw[:, r, :], 1.0, 1.0, ALU.mult, ALU.mult).then_inc(w_rounded, 1)
                pool.wait_ge(w_rounded, rounded.next())
                pool.tensor_tensor(w_l[:, s, :], w_raw[:, r, :], w_h[:, s, :].bitcast(F32),
                                   ALU.subtract).then_inc(w_split, 1)
                pool.wait_ge(w_split, split.next())
                counted()

            counts = raw + [rounded, split]
            with repeat(pool, LAYERS, counts):
                for s in range(4):
                    block_split(s - 4)
                for s in range(4):
                    block_split(s)
                with repeat(pool, HEADS - 1, counts) as h:
                    for s in range(4):
                        block_split(8 + s, h * 10)
                for last in (37, 38, 40, 41, 42, 43, 45, 46, 50, 51, 125, 127, 144, 145, 147, 147):
                    block_split(last)
                with repeat(pool, 148 // 4, counts) as i:
                    for s in range(4):
                        block_split(180 + s, i * 4)
                done.skip(LAYER_TILES)
                done.fold()

        @block.tensor
        def _(pe):
            pe.sem_inc(tile_done, TILES)
            pe.sem_inc(out_step, SCORES)
            split = Count(pe, "pe_split", RAW, SPLIT)
            tiles = Count(pe, "pe_tiles", 0, TILES)
            auxs = Count(pe, "pe_aux", 0, AUX)
            outr = Count(pe, "pe_outs", 0, OUTS)
            low = Count(pe, "pe_low")
            sums = Count(pe, "pe_sums")
            parts = Count(pe, "pe_parts")
            squares = Count(pe, "pe_squares")
            norm_sums = Count(pe, "pe_norm_sums")
            norm_low = Count(pe, "pe_norm_low")
            phases = Count(pe, "pe_phase")
            counts = [split, tiles, auxs, outr, low, sums, parts, squares, norm_sums, norm_low, phases]

            def product(to, left, right, first, last):
                pe.matmul(to, left[0], right[1], start=first, stop=False)
                pe.matmul(to, left[1], right[0], start=False, stop=False)
                return pe.matmul(to, left[0], right[0], start=False, stop=last)

            def weight(s, at, n=P):
                return w_h[:, s, at:at + n], w_l[:, s, at:at + n]

            def new_tile(n=1):
                s = tiles.slot
                pe.wait_ge(tile_read, tiles.next(n))
                return s

            def new_aux():
                s = auxs.slot
                pe.wait_ge(aux_read, auxs.next())
                return s

            def column_sums(source, n=HALF):
                pe.wait_ge(sum_ready, sums.next())
                pe.matmul(aux(new_aux(), n), ones, source, start=True, stop=True).then_inc(aux_done, 1)

            def project(half, s, source_h, source_l, depth=KT, ready=None, during=None):
                to = tile(new_tile())
                for k in range(depth):
                    if during:
                        during(k)
                    if ready is not None:
                        pe.wait_ge(low_ready, low.at(ready + k + 1))
                    mm = product(to, weight(s, k * P), (source_h[:, k, :], source_l[:, k, :]),
                                 k == 0, k == depth - 1)
                mm.then_inc(tile_done, 1)

            def norm_sum(half):
                pe.wait_ge(norm_sum_ready, norm_sums.next())
                pe.matmul(outs(1), ones, f_sum[:, half, :], start=True, stop=True).then_inc(norm_sums_done, 1)

            pe.wait_ge(phase_done, phases.next())
            norm_sum(0)

            with repeat(pe, LAYERS, counts):
                pe.wait_ge(norm_low_ready, norm_low.next(KT))
                for s in range(4):
                    pe.wait_ge(w_split, split.next())
                    project(0, s, op_h[:, 0], op_l[:, 0])
                    if s in (0, 3):
                        norm_sum(1)
                pe.wait_ge(norm_low_ready, norm_low.next(KT))

                pe.wait_ge(phase_done, phases.next())
                def score(half, kb):
                    c, _ = columns(half, kb)
                    if kb == 0:
                        pe.wait_ge(low_ready, low.next(2))
                    q0 = half * HALF
                    mm = product(aux(new_aux(), HALF - c),
                                 (r_kh[:, kb * P:(kb + 1) * P], r_kl[:, kb * P:(kb + 1) * P]),
                                 (r_qh[:, q0 + c:q0 + HALF], r_ql[:, q0 + c:q0 + HALF]), True, True)
                    mm.then_inc(aux_done, 1)

                def value(half, kb, later):
                    c, _ = columns(half, kb)
                    if kb == 0:
                        pe.wait_ge(out_read, outr.next())
                    pe.wait_ge(aux_read, auxs.at(AUX - later))
                    s = step_index(half, kb) % SCORES
                    mm = product(outs(half, HALF - c, c),
                                 (r_vh[:, kb * P:(kb + 1) * P], r_vl[:, kb * P:(kb + 1) * P]),
                                 (r_sh[:, s, 0:HALF - c], r_sl[:, s, 0:HALF - c]),
                                 kb == 0, kb == 4 * half + 3)
                    mm.then_inc(out_step, 1)

                def head_norm():
                    pe.wait_ge(square_ready, squares.next())
                    pe.matmul(tile(new_tile()), ones, r_square[:, :], start=True, stop=True).then_inc(tile_done, 1)

                def turn_values():
                    pe.wait_ge(part_ready, parts.next())
                    a = new_aux()
                    for b in range(4):
                        mm = pe.transpose(aux(a, P, b * P), r_vt[:, b * P:(b + 1) * P], ident)
                    mm.then_inc(aux_done, 1)

                def second_half(after):
                    for s in range(4):
                        def during(k):
                            if k == 1:
                                score(0, s)
                            elif k == 3 and s:
                                value(0, s - 1, 1)
                            elif k in (3, 5) and s == 0 and after:
                                value(1, 6 + (k == 5), 3 - (k == 5))
                            elif k == 5 and s == 3:
                                turn_values()
                        project(1, s, op_h[:, 1], op_l[:, 1], during=during)
                        if s == 1 and after:
                            head_norm()
                    split.skip(4)

                def under(half, values):
                    for s in range(4):
                        pe.wait_ge(w_split, split.at(s + 1))

                        def during(k):
                            if k in (0, 2):
                                score(1, 2 * s + k // 2)
                            elif k == 4 and s == 0:
                                value(0, 3, 3)
                            elif k in (4, 6) and s:
                                value(1, 2 * s - 2 + (k == 6), 3 - (k == 6))
                            elif k == 7 and s == 3 and values:
                                turn_values()
                        project(half, s, op_h[:, half], op_l[:, half], during=during)
                        if s == 1:
                            head_norm()

                for s in range(4):
                    pe.wait_ge(w_split, split.at(s + 1))
                    project(0, s, op_h[:, 0], op_l[:, 0],
                            during=lambda k: turn_values() if s == 3 and k == 3 else None)
                second_half(False)
                with repeat(pe, HEADS - 1, counts):
                    under(0, True)
                    second_half(True)
                under(1, False)
                split.skip(4)
                value(1, 6, 1)
                value(1, 7, 0)
                head_norm()

                squares.skip(6 + 1 + 2 * 2 * KT)

                pe.wait_ge(phase_done, phases.next())
                for half in range(2):
                    for s in range(2):
                        if half == 0:
                            pe.wait_ge(w_split, split.at(s + 1))
                        project(half, (split.slot + s) % SPLIT, op_h[:, half], op_l[:, half])
                        if s == 0:
                            column_sums(c_sum[:, :])
                split.skip(2)
                column_sums(c_sum[:, :])
                pe.wait_ge(low_ready, low.next(6))
                split.skip(2)
                pe.wait_ge(w_split, split.at())
                wx, wy = (split.slot - 2) % SPLIT, (split.slot - 1) % SPLIT

                def q_latent(k, half):
                    return tuple(t[:, 0, 2 * k + half, :] for t in (op_h, op_l))

                def kv_latent(half):
                    return tuple(t[:, half, :] for t in slot(CKV))

                for pair in range(2):
                    for half in range(2):
                        to = tile(new_tile())
                        for k in range(2):
                            mm = product(to, weight(wy, k * 256 + pair * P), q_latent(k, half), k == 0, k == 1)
                        mm.then_inc(tile_done, 1)
                    if pair == 0:
                        column_sums(c_sum[:, :])
                kv_h, kv_l = slot(CKV)
                pe.wait_ge(low_ready, low.next(2))
                for t in range(8):
                    at = slice((t % 4) * P, (t % 4 + 1) * P)
                    product(tile(new_tile(), 256), (kv_h[:, t // 4, at], kv_l[:, t // 4, at]),
                            (z_h[:, :], z_l[:, :]), True, True).then_inc(tile_done, 1)
                pe.wait_ge(low_ready, low.next(1 + 4))

                def attend(scores, values, width_of, prob, prob_parts, prepare=None):
                    step = 0

                    def next_head(h):
                        if prepare and h < HEADS:
                            prepare(h)

                    def steps(h, i):
                        nonlocal step
                        n = width_of(2 * i) // 256
                        pe.wait_ge(part_ready, parts.next(2))

                        def turn(j):
                            a = new_aux()
                            for kb in range(2):
                                for q in range(2):
                                    mm = pe.transpose(aux(a, P, kb * 256 + q * P),
                                                      prob(2 * i + q, (2 * j + kb) * P, P), ident)
                            mm.then_inc(aux_done, 1)

                        for j in range(n):
                            turn(j)
                            last_use(1)
                            pending.append((h, j, step % PARTS, j == 0, j == n - 1))
                            step += 1

                    pending = []

                    def last_use(later):
                        if not pending:
                            return
                        h, j, s, first, last = pending.pop()
                        if first:
                            pe.wait_ge(out_read, outr.next())
                        pe.wait_ge(aux_read, auxs.at(AUX - later))
                        o = (outr.slot - 1) % OUTS
                        for kb in range(2):
                            mm = product(outs(o, 256), values(h, 2 * j + kb),
                                         (prob_parts[0][:, s, kb * 256:(kb + 1) * 256],
                                          prob_parts[1][:, s, kb * 256:(kb + 1) * 256]),
                                         first and kb == 0, last and kb == 1)
                        mm.then_inc(out_step, 1)

                    def mixed(h, i, before):
                        if i == 0 and prepare:
                            pe.wait_ge(tile_read, tiles.at(TILES))
                        scores(h, 2 * i)
                        scores(h, 2 * i + 1)
                        if before:
                            steps(*before)

                    next_head(0)
                    for h in range(HEADS):
                        attention_order(h, next_head, steps, mixed)
                    last_use(0)

                pe.wait_ge(phase_done, phases.next())

                def latent_head(h):
                    for half in range(2):
                        to = tile(new_tile())
                        for k in range(2):
                            mm = product(to, weight(wx, k * 512 + h * P), q_latent(k, half), k == 0, k == 1)
                        mm.then_inc(tile_done, 1)
                    for half in range(2):
                        product(tile(new_tile()), weight(wy, 512 + h * P), kv_latent(half), True, True)\
                            .then_inc(tile_done, 1)

                def latent_scores(h, q):
                    s = new_tile(2)
                    n = 256 * (q // 2 + 1)
                    kr = slot(KROPE + h % 2)
                    qr = slot(QROPE + h // 2)
                    at = slice((q % 4) * P, (q % 4 + 1) * P)
                    for c in range(0, n, 512):
                        w = min(512, n - c)
                        to = tile(s, w, c)
                        product(to, (m_qh[:, q * P:(q + 1) * P], m_ql[:, q * P:(q + 1) * P]),
                                (m_kh[:, c:c + w], m_kl[:, c:c + w]), True, False)
                        mm = product(to, tuple(t[:, q // 4, at] for t in qr),
                                     tuple(t[:, c // 512, 0:w] for t in kr), False, True)
                    mm.then_inc(tile_done, 2)

                attend(latent_scores,
                       lambda h, kb: tuple(t[:, kb, (h // 2) * P:(h // 2 + 1) * P] for t in (m_vh, m_vl)),
                       latent_width, latent_probs, (m_ph, m_pl), latent_head)

                pe.wait_ge(phase_done, phases.next())
                column_sums(e_square[:, 0, :], MEM)
                pe.wait_ge(low_ready, low.next(2))
                for t in range(2):
                    s = split.slot
                    pe.wait_ge(w_split, split.next())
                    to = tile(new_tile(), MEM)
                    for k in range(KT):
                        mm = product(to, weight(s, k * P), (e_nh[:, k, :], e_nl[:, k, :]), k == 0, k == KT - 1)
                    mm.then_inc(tile_done, 1)
                s = split.slot
                pe.wait_ge(w_split, split.next(2))
                for t in range(2):
                    to = tile(new_tile(), MEM)
                    for k in range(KT):
                        mm = product(to, (e_nh[:, k, t * P:(t + 1) * P], e_nl[:, k, t * P:(t + 1) * P]),
                                     weight((s + k // 4) % SPLIT, (k % 4) * 256, 256), k == 0, k == KT - 1)
                    mm.then_inc(tile_done, 1)
                pe.wait_ge(tile_read, tiles.at(TILES))

                def memory_scores(h, q):
                    mq = slot(MQ + h // 2)
                    at = slice((q % 4) * P, (q % 4 + 1) * P)
                    product(tile(new_tile(), MEM), tuple(t[:, q // 4, at] for t in mq),
                            (e_kh[:, h, :], e_kl[:, h, :]), True, True).then_inc(tile_done, 1)

                attend(memory_scores,
                       lambda h, kb: tuple(t[:, kb, (h // 2) * P:(h // 2 + 1) * P] for t in (e_vh, e_vl)),
                       memory_width, memory_probs, (e_ph, e_pl))

                pe.wait_ge(phase_done, phases.next())
                for half in range(2):
                    for m in range(KT):
                        s = split.slot
                        pe.wait_ge(w_split, split.next())
                        project(half, s, op_h[:, half], op_l[:, half],
                                ready=half * KT if m == 0 else None)
                        if half == 1 and m in (0, 4):
                            norm_sum(0)
                low.skip(2 * KT)

                for half in range(2):
                    pe.wait_ge(norm_low_ready, norm_low.next(KT))

                    def hidden():
                        for s in range(4):
                            pe.wait_ge(w_split, split.next())
                            project(half, s, op_h[:, half], op_l[:, half])

                    for g, size in enumerate(GROUPS):
                        if g == 0:
                            hidden()
                            norm_sum(1 - half)
                            with repeat(pe, size // 2 - 2, counts):
                                hidden()
                            norm_sum(1 - half)
                            hidden()
                        else:
                            with repeat(pe, size // 2, counts):
                                hidden()
                        with repeat(pe, 2, [c for c in counts if c is not low]):
                            for s in range(4):
                                pe.wait_ge(w_split, split.next())
                                project(half, s, a_h, a_l, depth=size, ready=0 if s == 0 else None)
                        low.skip(size)
            norm_sum(1)

        @block.scalar
        def _(act):
            act.sem_inc(square_used, 2)
            act.sem_inc(norm_square_used, 2)
            done = Count(act, "act_tiles", TILES, TILES)
            auxd = Count(act, "act_aux", 0, AUX)
            outd = Count(act, "act_outs", 0)
            value = Count(act, "act_value")
            used = Count(act, "act_square_used", 0, 2)
            rs_used = Count(act, "act_rsqrt_used")
            high = Count(act, "act_high")
            out_ = Count(act, "act_out")
            sqr = Count(act, "act_square")
            log = Count(act, "act_log")
            rsq = Count(act, "act_rsqrt")
            ld = Count(act, "act_loaded")
            xs = Count(act, "act_x")
            st = [Count(act, f"act_stored{i}") for i in range(2)]
            n_value = Count(act, "act_norm_value")
            n_used = Count(act, "act_norm_square_used", 0, 2)
            n_high = Count(act, "act_norm_high")
            n_square = Count(act, "act_norm_square")
            n_sums = Count(act, "act_norm_sums")
            n_rsqrt = Count(act, "act_norm_rsqrt")
            phases = Count(act, "act_phase", 1)
            counts = [done, auxd, outd, value, used, rs_used, high, out_, sqr, log, rsq, ld, xs, phases,
                      n_value, n_used, n_high, n_square, n_sums, n_rsqrt] + st

            def to_high(to, source, scale=1.0):
                act.activation(to, source, ACT.Copy, scale=scale).then_inc(high_ready, 1)
                act.wait_ge(high_ready, high.next())

            def to_value(to, source, func, **more):
                act.activation(to, source, func, **more).then_inc(act_ready, 1)
                act.wait_ge(act_ready, out_.next())

            def square(to, source):
                act.activation(to, source, ACT.Square).then_inc(square_ready, 1)
                act.wait_ge(square_ready, sqr.next())

            def square_ring(ring, source):
                s = used.slot
                act.wait_ge(square_used, used.next())
                square(ring[:, s, :], source)

            def rsqrt(log_to, to, dim, n=HALF):
                s = auxd.slot
                act.wait_ge(aux_done, auxd.next())
                act.wait_ge(rsqrt_used, rs_used.next())
                act.activation(log_to, aux(s, n), ACT.Ln, bias=eps, scale=1.0 / dim).then_inc(log_ready, 1)
                act.wait_ge(log_ready, log.next())
                act.activation(to, log_to, ACT.Exp, scale=-0.5).then_inc(rsqrt_ready, 1)
                act.wait_ge(rsqrt_ready, rsq.next())

            def norm_rsqrt():
                act.wait_ge(norm_sums_done, n_sums.next())
                act.activation(b_rsqrt[:, :], outs(1), ACT.Ln, bias=eps, scale=1.0 / D).then_inc(log_ready, 1)
                act.wait_ge(log_ready, log.next())
                act.activation(b_rsqrt[:, :], b_rsqrt[:, :], ACT.Exp, scale=-0.5).then_inc(norm_rsqrt_ready, 1)
                act.wait_ge(norm_rsqrt_ready, n_rsqrt.next())

            def load_x(half, m):
                act.dma_start(x_old[:, m % X_TILES, :], out[half, :, m, :]).then_inc(x_loaded[m % X_TILES], 16)

            def boundary_open(half):
                act.wait_ge(stored[half], st[half].at())
                for m in range(X_TILES):
                    load_x(half, m)
                norm_rsqrt()

            def norm_squares(half, tiles):
                for m in tiles:
                    s = n_used.slot
                    act.wait_ge(norm_square_used, n_used.next())
                    act.activation(b_square[:, s, :], branch[:, half, m, :], ACT.Square).then_inc(norm_square_ready, 1)
                    act.wait_ge(norm_square_ready, n_square.next())

            def boundary_squares(half, tiles):
                for m in tiles:
                    act.wait_ge(x_ready, xs.next())
                    if m + X_TILES < KT:
                        load_x(half, m + X_TILES)
                    norm_squares(half, (m,))

            def boundary_middle(half):
                act.dma_start(out[half], branch[:, half]).then_inc(stored[half], 16)
                st[half].skip(16)
                norm_rsqrt()

            def norm_highs(half, tiles):
                for m in tiles:
                    act.wait_ge(norm_value_ready, n_value.next())
                    act.activation(op_h[:, half, m, :], b_norm[:, m % 2, :], ACT.Copy).then_inc(norm_high_ready, 1)
                    act.wait_ge(norm_high_ready, n_high.next())

            act.dma_start(const[:, :], consts).then_inc(loaded, 16)
            act.dma_start(s_pos[:, :], positions.partition_broadcast(P)).then_inc(loaded, 16)
            for i in range(4):
                act.dma_start(branch[:, 0, 2 * i:2 * i + 2, :], x[0, :, 2 * i:2 * i + 2, :]).then_inc(x_loaded[i], 16)
            act.dma_start(gain[:, :], gains[0]).then_inc(loaded, 16)
            act.dma_start(head_scales[:, :, :], scales).then_inc(loaded, 16)
            for half in range(2):
                act.dma_start(out[half], x[half]).then_inc(stored[half], 16)
                st[half].skip(16)
            act.wait_ge(loaded, ld.next(64))

            def sines(t):
                act.wait_ge(value_ready, value.next())
                if t:
                    act.wait_ge(tables_stored, 64)
                for f in range(2):
                    to_value(s_tab[:, f, :], s_ang[:, :], ACT.Sin,
                             scale=const[:, K_SIGN:K_SIGN + 1] if f else 1.0)
                for rows in (slice(0, 64), slice(64, P)):
                    act.dma_start(cos_sin[t, rows, 0, :], s_tab[0:64, 0, :]).then_inc(tables_stored, 16)
                act.dma_start(cos_sin[t, 0:64, 1, :], s_tab[64:P, 1, :]).then_inc(tables_stored, 16)
                act.dma_start(cos_sin[t, 64:P, 1, :], s_tab[64:P, 0, :]).then_inc(tables_stored, 16)

            sines(0)
            for m in range(KT):
                if m % 2 == 0:
                    act.wait_ge(x_loaded[m // 2], 16)
                norm_squares(0, (m,))
            norm_rsqrt()
            norm_highs(0, range(KT))
            sines(1)
            act.wait_ge(tables_stored, 128)

            with repeat(act, LAYERS, counts) as l:
                done.skip(4)
                boundary_open(1)
                boundary_squares(1, range(KT))
                boundary_middle(1)
                norm_highs(1, range(KT))

                act.wait_ge(phase_done, phases.next())
                act.dma_start(gain[:, :], gains[l + 1]).then_inc(loaded, 16)
                act.dma_start(r_tab[:, :, :], cos_sin[0]).then_inc(loaded, 16)
                act.dma_start(r_decay[:, :], decay[0]).then_inc(decay_loaded, 16)
                
                def head_tile(half, s, before=lambda: None):
                    cols = slice(half * HALF, (half + 1) * HALF)
                    before()
                    if s < 2:
                        act.wait_ge(value_ready, value.next())
                        to_high((r_qh, r_kh)[s][:, cols], r_t[:, 0, :])
                        done.skip(1)
                    elif s == 2:
                        done.skip(1)
                    else:
                        a = auxd.slot
                        act.wait_ge(aux_done, auxd.next())
                        to_high(r_vh[:, cols], aux(a))
                        s = done.slot
                        act.wait_ge(tile_done, done.next())
                        to_value(r_gate[:, cols], tile(s), ACT.Silu)

                def step(half, kb):
                    c, diagonal = columns(half, kb)
                    a = auxd.slot
                    act.wait_ge(aux_done, auxd.next())
                    if diagonal:
                        act.wait_ge(value_ready, value.next())
                    act.wait_ge(out_step, outd.next())
                    to_high(r_sh[:, step_index(half, kb) % SCORES, 0:HALF - c], aux(a, HALF - c), scale_of(half, kb))

                def head_square(half, later):
                    act.wait_ge(out_step, outd.at(SCORES - later))
                    square(r_square[:, :], outs(half))

                def head_rsqrt():
                    t = done.slot
                    act.wait_ge(tile_done, done.next())
                    act.wait_ge(rsqrt_used, rs_used.next())
                    act.activation(r_rsqrt[:, :], tile(t), ACT.Ln, bias=eps, scale=1.0 / P).then_inc(log_ready, 1)
                    act.wait_ge(log_ready, log.next())
                    act.activation(r_rsqrt[:, :], r_rsqrt[:, :], ACT.Exp, scale=-0.5).then_inc(rsqrt_ready, 1)
                    act.wait_ge(rsqrt_ready, rsq.next())

                def second_half(after):
                    for s in range(4):
                        def before():
                            step(0, s)
                            if s == 1 and after:
                                head_square(1, 2)
                            if s == 2 and after:
                                head_rsqrt()
                        head_tile(1, s, before)

                def second_steps(s):
                    step(1, 2 * s)
                    step(1, 2 * s + 1)
                    if s == 1:
                        head_square(0, 4)
                    if s == 2:
                        head_rsqrt()

                for s in range(4):
                    head_tile(0, s)
                second_half(False)
                with repeat(act, HEADS - 1, counts) as h:
                    act.dma_start(r_decay[:, :], decay[h + 1]).then_inc(decay_loaded, 16)
                    for s in range(4):
                        head_tile(0, s, lambda: second_steps(s))
                    second_half(True)
                for s in range(4):
                    second_steps(s)
                    done.skip(1)
                head_square(1, 0)
                head_rsqrt()
                ld.skip(32)

                act.wait_ge(phase_done, phases.next())
                act.dma_start(c_tab[:, :, :], cos_sin[1]).then_inc(loaded, 16)
                act.dma_start(z_raw[:, :], value_weights[l]).then_inc(loaded, 16)
                act.wait_ge(loaded, ld.next(32))
                to_high(z_h[:, :], z_raw[:, :])
                done.skip(4)

                def latent_parts(to, dim):
                    rsqrt(c_log[:, :], c_rsqrt[:, :], dim)
                    for k, slot_half in enumerate(to):
                        act.wait_ge(value_ready, value.next())
                        to_high(slot_half, c_norm[:, k, :])

                def latent_square(sources):
                    for source in sources:
                        square_ring(c_square, source)

                def rope_key(half):
                    act.wait_ge(value_ready, value.next())
                    for n in range(2):
                        to_high(slot(KROPE + n)[0][:, half, :], c_t[:, 0, :], const[:, K_PAIR + n:K_PAIR + n + 1])

                for half in range(2):
                    latent_square([branch[:, half, 4 + k, :] for k in range(2)])
                latent_parts([slot(CQ + k)[0][:, 0, :] for k in range(2)], QRANK)
                rope_key(0)
                latent_parts([slot(CQ + k)[0][:, 1, :] for k in range(2)], QRANK)
                act.wait_ge(value_ready, value.next())
                latent_square([c_kv[:, half * HALF:(half + 1) * HALF] for half in range(2)])
                for half in range(2):
                    latent_parts([slot(CKV)[0][:, half, :]], KVRANK)
                rope_key(1)
                for pair in range(2):
                    for half in range(2):
                        done.skip(1)
                        act.wait_ge(value_ready, value.next())
                        to_high(slot(QROPE + pair)[0][:, half, :], c_t[:, 0, :])
                for t in range(8):
                    s = done.slot
                    act.wait_ge(tile_done, done.next())
                    to_high(m_vh[:, t, :], tile(s, 256))

                def attend(width_of, banks, scale, prob, parts_h, prepare=None):
                    step = 0

                    def next_head(h):
                        if prepare and h < HEADS:
                            prepare(h)

                    def softmax(q):
                        n = width_of(q)
                        s = done.slot
                        done.skip(banks)
                        act.wait_ge(value_ready, value.next())
                        to_value(prob(q), tile(s, n), ACT.Exp, scale=scale,
                                 bias=stat[:, 1, q:q + 1], accum_out=stat[:, 2, q:q + 1])

                    def one_step():
                        nonlocal step
                        a = auxd.slot
                        act.wait_ge(aux_done, auxd.next())
                        act.wait_ge(out_step, outd.next() + (SCORES - PARTS))
                        to_high(parts_h[:, step % PARTS, :], aux(a))
                        step += 1

                    def steps(h, i):
                        for j in range(width_of(2 * i) // 256):
                            one_step()

                    def mixed(h, i, before):
                        n = width_of(2 * before[1]) // 256 if before else 0
                        softmax(2 * i)
                        if n:
                            one_step()
                        softmax(2 * i + 1)
                        for j in range(n - 1):
                            one_step()

                    next_head(0)
                    for h in range(HEADS):
                        attention_order(h, next_head, steps, mixed)

                act.wait_ge(phase_done, phases.next())

                def latent_head(h):
                    for to in (m_qh, m_kh):
                        for half in range(2):
                            s = done.slot
                            act.wait_ge(tile_done, done.next())
                            to_high(to[:, half * HALF:(half + 1) * HALF], tile(s))

                attend(latent_width, 2, ATT_SCALE, latent_probs, m_ph, latent_head)

                act.wait_ge(phase_done, phases.next())
                act.dma_start(e_mem[:, :, :], mem).then_inc(loaded, 16)
                act.wait_ge(loaded, ld.next(16))
                square(e_square[:, :, :], e_mem[:, :, :])
                for k in range(2):
                    to_high(slot(MQ + k)[0], branch[:, :, 6 + k, :])
                rsqrt(e_log[:, :], e_rsqrt[:, :], D, MEM)
                act.wait_ge(value_ready, value.next())
                to_high(e_nh[:, :, :], e_mem[:, :, :])
                for t in range(2):
                    s = done.slot
                    act.wait_ge(tile_done, done.next())
                    for n in range(2):
                        to_high(e_kh[:, 2 * t + n, :], tile(s, MEM), const[:, K_HALVES + n:K_HALVES + n + 1])
                for t in range(2):
                    s = done.slot
                    act.wait_ge(tile_done, done.next())
                    to_high(e_vh[:, t, :], tile(s, MEM))
                attend(memory_width, 1, MEM_SCALE, memory_probs, e_ph)

                act.wait_ge(phase_done, phases.next())

                def out_tile(half, m):
                    s = done.slot
                    act.wait_ge(tile_done, done.next())
                    to_value(branch[:, half, m, :], tile(s), ACT.Copy)
                    square_ring(f_square, tile(s))

                for half in range(2):
                    for m in range(KT):
                        to_high(op_h[:, half, m, :], branch[:, half, m, :])
                for m in range(KT):
                    out_tile(0, m)
                for m in range(KT):
                    out_tile(1, m)
                    if m == 0:
                        boundary_open(0)
                        boundary_squares(0, range(0, 3))
                    elif m < 4:
                        boundary_squares(0, range(2 * m + 1, min(2 * m + 3, KT)))
                    elif m == 4:
                        boundary_middle(0)
                    else:
                        norm_highs(0, range(3 * m - 15, min(3 * m - 12, KT)))

                for half in range(2):
                    def hidden(j, u):
                        s = done.slot
                        act.wait_ge(tile_done, done.next())
                        to_value(f_gate[:, u, :], tile(s), ACT.Silu)
                        done.skip(1)
                        act.wait_ge(value_ready, value.next())
                        to_high(a_h[:, j, :], f_hidden[:, u, :])

                    for g, size in enumerate(GROUPS):
                        if g == 0:
                            for j in range(size):
                                hidden(j, j % 2)
                                if j == 1:
                                    boundary_open(1 - half)
                                elif j in (2, 3):
                                    boundary_squares(1 - half, range(4 * j - 8, 4 * j - 4))
                                elif j == 5:
                                    boundary_middle(1 - half)
                                elif j > 5:
                                    norm_highs(1 - half, range(4 * j - 24, 4 * j - 20))
                        else:
                            with repeat(act, size // 2, counts) as i:
                                for u in range(2):
                                    hidden(i * 2 + u, u)
                        for m in range(KT):
                            done.skip(1)
                            if g == 2:
                                act.wait_ge(value_ready, value.next())
                                square_ring(f_square, branch[:, half, m, :])

            boundary_open(1)
            for m in range(KT):
                act.wait_ge(x_ready, xs.next())
                if m + X_TILES < KT:
                    load_x(1, m + X_TILES)
                if m % 2:
                    act.dma_start(out[1, :, m - 1:m + 1, :], branch[:, 1, m - 1:m + 1, :]).then_inc(stored[1], 16)
                    st[1].skip(16)
            for half in range(2):
                act.wait_ge(stored[half], st[half].at())
                act.sem_inc(finished, 1)

        @block.vector
        def _(dve):
            dve.sem_inc(tile_read, TILES)
            dve.sem_inc(aux_read, AUX)
            dve.sem_inc(out_read, OUTS)
            dve.sem_inc(rsqrt_used, 1)
            done = Count(dve, "dve_tiles", TILES, TILES)
            auxd = Count(dve, "dve_aux", 0, AUX)
            outd = Count(dve, "dve_outs", SCORES)
            high = Count(dve, "dve_high")
            acts = Count(dve, "dve_act")
            sqr = Count(dve, "dve_square", 0, 2)
            rsq = Count(dve, "dve_rsqrt")
            ld = Count(dve, "dve_loaded")
            decays = Count(dve, "dve_decay_loaded")
            xl = [Count(dve, f"dve_x_loaded{i}") for i in range(X_TILES)]
            st = [Count(dve, f"dve_stored{i}") for i in range(2)]
            n_square = Count(dve, "dve_norm_square", 0, 2)
            n_rsqrt = Count(dve, "dve_norm_rsqrt")
            n_value = Count(dve, "dve_norm_value")
            n_high = Count(dve, "dve_norm_high")
            n_low = Count(dve, "dve_norm_low")
            link_ = Count(dve, "dve_linked")
            read = Count(dve, "dve_read", TILES)
            auxr = Count(dve, "dve_aux_read", AUX)
            outr = Count(dve, "dve_out_read", OUTS, OUTS)
            low = Count(dve, "dve_low")
            value = Count(dve, "dve_value")
            part = Count(dve, "dve_part")
            xr = Count(dve, "dve_x_ready")
            counts = [done, auxd, outd, high, acts, sqr, rsq, ld, decays, link_, read, auxr, outr, low, value, part, xr,
                      n_square, n_rsqrt, n_value, n_high, n_low] + xl + st

            def link(instruction):
                instruction.then_inc(dve_link, 1)
                dve.wait_ge(dve_link, link_.next())

            def signal(instruction, semaphore, count):
                instruction.then_inc(semaphore, 1)
                dve.wait_ge(semaphore, count.next())

            def to_low(to, to_h, source):
                dve.wait_ge(high_ready, high.next())
                signal(dve.tensor_tensor(to, source, to_h.bitcast(F32), ALU.subtract), low_ready, low)

            def add_square(total, ring, first):
                s = sqr.slot
                dve.wait_ge(square_ready, sqr.next())
                if first:
                    link(dve.tensor_copy(total, ring[:, s, :]))
                else:
                    link(dve.tensor_tensor(total, total, ring[:, s, :], ALU.add))
                dve.sem_inc(square_used, 1)

            def take_rsqrt():
                dve.wait_ge(rsqrt_ready, rsq.next())
                auxd.skip(1)
                auxr.skip(1)
                dve.sem_inc(aux_read, 1)

            def norm_add_square(half, first):
                s = n_square.slot
                dve.wait_ge(norm_square_ready, n_square.next())
                total = f_sum[:, half, :]
                if first:
                    link(dve.tensor_copy(total, b_square[:, s, :]))
                else:
                    link(dve.tensor_tensor(total, total, b_square[:, s, :], ALU.add))
                dve.sem_inc(norm_square_used, 1)

            def norm_tiles(half, g, tiles):
                if tiles[0] == 0:
                    dve.wait_ge(norm_rsqrt_ready, n_rsqrt.next())
                for m in (*tiles, None):
                    if m is not None:
                        signal(dve.scalar_tensor_tensor(
                            out=b_norm[:, m % 2, :], in0=branch[:, half, m, :], scalar=gain[:, g + m:g + m + 1],
                            in1=b_rsqrt[:, :], op0=ALU.mult, op1=ALU.mult), norm_value_ready, n_value)
                    if m != tiles[0]:
                        k = tiles[-1] if m is None else m - 1
                        dve.wait_ge(norm_high_ready, n_high.next())
                        signal(dve.tensor_tensor(op_l[:, half, k, :], b_norm[:, k % 2, :],
                                                 op_h[:, half, k, :].bitcast(F32), ALU.subtract),
                               norm_low_ready, n_low)

            def boundary_residual(half, g, tiles, squares=True):
                if tiles[0] == 0:
                    dve.wait_ge(norm_rsqrt_ready, n_rsqrt.next())
                for m in tiles:
                    y = branch[:, half, m, :]
                    link(dve.scalar_tensor_tensor(out=y, in0=y, scalar=gain[:, g + m:g + m + 1],
                                                  in1=b_rsqrt[:, :], op0=ALU.mult, op1=ALU.mult))
                    dve.wait_ge(x_loaded[m % X_TILES], xl[m % X_TILES].next(16))
                    signal(dve.tensor_tensor(y, x_old[:, m % X_TILES, :], y, ALU.add), x_ready, xr)
                    if m and squares:
                        norm_add_square(half, m == 1)
                if squares and tiles[-1] == KT - 1:
                    norm_add_square(half, False)
                    dve.sem_inc(norm_sum_ready, 1)

            def angles(t):
                c1 = 6.28125
                c2 = float(np.round((TWO_PI - c1) * 2 ** 19) / 2 ** 19)
                c3 = float(np.float32(TWO_PI - c1 - c2))
                link(dve.tensor_scalar(s_ang[:, :], s_posf[:, :], const[:, K_FREQ + t:K_FREQ + t + 1], None,
                                       ALU.mult))
                link(dve.tensor_scalar(s_turn[:, :], s_ang[:, :], 1.0 / TWO_PI, const[:, K_TURN:K_TURN + 1],
                                       ALU.mult, ALU.add))
                link(dve.tensor_scalar(s_turn[:, :], s_turn[:, :], MAGIC, -MAGIC, ALU.add, ALU.add))
                for c in (c1, c2, c3):
                    link(dve.scalar_tensor_tensor(out=s_ang[:, :], in0=s_turn[:, :], scalar=-c,
                                                  in1=s_ang[:, :], op0=ALU.mult, op1=ALU.add))
                link(dve.tensor_scalar(s_ang[:, :], s_ang[:, :], const[:, K_SHIFT:K_SHIFT + 1], None, ALU.add))
                signal(dve.tensor_scalar(s_ang[:, :], s_ang[:, :], 3.1415925, -3.1415925, ALU.min, ALU.max),
                       value_ready, value)

            link(dve.memset(branch[:, 1], 0.0))
            link(dve.memset(f_sum[:, 1, :], 0.0))
            dve.wait_ge(loaded, ld.next(64))
            dve.sem_inc(phase_done, 1)
            link(dve.tensor_copy(s_posf[:, :], s_pos[:, :]))
            angles(0)

            for m in range(KT):
                norm_add_square(0, m == 0)
            dve.sem_inc(norm_sum_ready, 1)
            norm_tiles(0, G_NEXT, range(KT))
            dve.wait_ge(act_ready, acts.next(2))
            angles(1)
            acts.skip(2)
            for i in range(X_TILES):
                xl[i].skip(16)
            dve.sem_inc(norm_sum_ready, 1)

            def rope(s, table, half, temp):
                cols = slice(half * HALF, (half + 1) * HALF)
                link(dve.tensor_tensor(temp[:, 1, :], tile(s), table[:, 0, cols], ALU.mult))
                link(dve.tensor_tensor(temp[0:64, 2, :], tile(s)[64:128], table[0:64, 1, cols], ALU.mult))
                signal(dve.tensor_tensor(temp[64:128, 2, :], tile(s)[0:64], table[64:128, 1, cols], ALU.mult),
                       tile_read, read)

            with repeat(dve, LAYERS, counts):
                dve.wait_ge(stored[0], st[0].at(16))
                for t in range(4):
                    s = done.slot
                    dve.wait_ge(tile_done, done.next())
                    signal(dve.tensor_copy(branch[:, 0, 4 + t, :], tile(s)), tile_read, read)
                    if t == 0:
                        boundary_residual(1, G_POST_FFN, range(0, 3))
                    elif t == 1:
                        boundary_residual(1, G_POST_FFN, range(3, 5))
                    elif t == 2:
                        boundary_residual(1, G_POST_FFN, range(5, KT))
                        st[1].skip(16)
                norm_tiles(1, G_NEXT, range(KT))
                dve.sem_inc(phase_done, 1)

                dve.wait_ge(stored[1], st[1].at(16))
                dve.wait_ge(loaded, ld.next(32))

                def head_tile(half, s, before=lambda: None):
                    cols = slice(half * HALF, (half + 1) * HALF)
                    before()
                    if s < 2:
                        th, tl = ((r_qh, r_ql), (r_kh, r_kl))[s]
                        t = done.slot
                        dve.wait_ge(tile_done, done.next())
                        rope(t, r_tab, half, r_t)
                        if s:
                            signal(dve.tensor_tensor(r_t[:, 0, :], r_t[:, 1, :], r_t[:, 2, :], ALU.add),
                                   value_ready, value)
                        else:
                            link(dve.tensor_tensor(r_t[:, 1, :], r_t[:, 1, :], r_t[:, 2, :], ALU.add))
                            signal(dve.tensor_tensor(r_t[:, 0, :], r_t[:, 1, :], r_decay[:, 0:HALF], ALU.mult),
                                   value_ready, value)
                        to_low(tl[:, cols], th[:, cols], r_t[:, 0, :])
                    elif s == 2:
                        t = done.slot
                        dve.wait_ge(tile_done, done.next())
                        signal(dve.tensor_copy(r_vt[:, :], tile(t)), tile_read, read)
                        dve.sem_inc(part_ready, 1)
                    else:
                        a = auxd.slot
                        auxd.skip(1)
                        dve.wait_ge(high_ready, high.next())
                        signal(dve.tensor_tensor(r_vl[:, cols], aux(a), r_vh[:, cols].bitcast(F32), ALU.subtract),
                               aux_read, auxr)
                        done.skip(1)
                        dve.wait_ge(act_ready, acts.next())
                        read.skip(1)
                        dve.sem_inc(tile_read, 1)

                def head_out(half, h):
                    sqr.other()
                    outd.skip(8 if half else 4)
                    dve.wait_ge(rsqrt_ready, rsq.next())
                    done.skip(1)
                    read.skip(1)
                    dve.sem_inc(tile_read, 1)
                    link(dve.tensor_tensor(r_square[:, :], outs(half), r_rsqrt[:, :], ALU.mult))
                    dve.sem_inc(rsqrt_used, 1)
                    outr.skip(1)
                    dve.sem_inc(out_read, 1)
                    link(dve.tensor_tensor(branch[:, half, h, :], r_square[:, :],
                                           r_gate[:, half * HALF:(half + 1) * HALF], ALU.mult))

                def step(half, kb):
                    c, diagonal = columns(half, kb)
                    a = auxd.slot
                    dve.wait_ge(aux_done, auxd.next())
                    if diagonal:
                        n = 256 if kb - 4 * half == 3 else P
                        view = aux(a, n)
                        signal(dve.tensor_tensor(view, view, tri[:, 256 - n:256], ALU.mult), value_ready, value)
                    dve.wait_ge(high_ready, high.next())
                    i = step_index(half, kb) % SCORES
                    low_part, high_part = r_sl[:, i, 0:HALF - c], r_sh[:, i, 0:HALF - c].bitcast(F32)
                    signal(dve.scalar_tensor_tensor(out=low_part, in0=aux(a, HALF - c), scalar=scale_of(half, kb),
                                                    in1=high_part, op0=ALU.mult, op1=ALU.subtract),
                           aux_read, auxr)

                def second_half(h, before_it):
                    link(dve.tensor_copy(r_scale[:, :], head_scales[:, h, :]))
                    for s in range(4):
                        def before():
                            step(0, s)
                            if s == 2 and before_it is not None:
                                head_out(1, before_it)
                        head_tile(1, s, before)

                def second_steps(s, h):
                    step(1, 2 * s)
                    step(1, 2 * s + 1)
                    if s == 2:
                        head_out(0, h)

                dve.wait_ge(decay_loaded, decays.next(16))
                for s in range(4):
                    head_tile(0, s)
                second_half(0, None)
                with repeat(dve, HEADS - 1, counts) as h:
                    for s in range(4):
                        def before():
                            second_steps(s, h)
                            if s == 0:
                                dve.wait_ge(decay_loaded, decays.next(16))
                        head_tile(0, s, before)
                    second_half(h + 1, h)
                for s in range(4):
                    second_steps(s, HEADS - 1)
                    t = done.slot
                    dve.wait_ge(tile_done, done.next())
                    signal(dve.tensor_copy(branch[:, 1, 4 + s, :], tile(t)), tile_read, read)
                head_out(1, HEADS - 1)
                dve.sem_inc(phase_done, 1)

                dve.wait_ge(loaded, ld.next(32))
                to_low(z_l[:, :], z_h[:, :], z_raw[:, :])

                def keep(to):
                    s = done.slot
                    dve.wait_ge(tile_done, done.next())
                    signal(dve.tensor_copy(to, tile(s)), tile_read, read)

                def copied():
                    value.skip(1)
                    dve.sem_inc(value_ready, 1)

                def latent_sum(n):
                    for k in range(n):
                        add_square(c_sum[:, :], c_square, k == 0)
                    dve.sem_inc(sum_ready, 1)

                def latent_parts(sources, g, slots, half):
                    take_rsqrt()
                    for k, source in enumerate(sources):
                        signal(dve.scalar_tensor_tensor(
                            out=c_norm[:, k, :], in0=source, scalar=gain[:, g + k:g + k + 1], in1=c_rsqrt[:, :],
                            op0=ALU.mult, op1=ALU.mult), value_ready, value)
                    dve.sem_inc(rsqrt_used, 1)
                    for k in range(len(sources)):
                        to_low(slot(slots + k)[1][:, half, :], slot(slots + k)[0][:, half, :], c_norm[:, k, :])

                kv = [c_kv[:, half * HALF:(half + 1) * HALF] for half in range(2)]
                kr = [c_kr[:, half * HALF:(half + 1) * HALF] for half in range(2)]
                q_lat = [[branch[:, half, 4 + k, :] for k in range(2)] for half in range(2)]

                def rope_key(half):
                    cols = slice(half * HALF, (half + 1) * HALF)
                    link(dve.tensor_tensor(c_t[:, 1, :], c_kr[:, cols], c_tab[:, 0, cols], ALU.mult))
                    link(dve.tensor_copy(c_t[0:64, 2, :], c_kr[64:128, cols]))
                    link(dve.tensor_copy(c_t[64:128, 2, :], c_kr[0:64, cols]))
                    link(dve.tensor_tensor(c_t[:, 2, :], c_t[:, 2, :], c_tab[:, 1, cols], ALU.mult))
                    signal(dve.tensor_tensor(c_t[:, 0, :], c_t[:, 1, :], c_t[:, 2, :], ALU.add), value_ready, value)
                    for n in range(2):
                        dve.wait_ge(high_ready, high.next())
                        link(dve.scalar_tensor_tensor(
                            out=slot(KROPE + n)[1][:, half, :], in0=c_t[:, 0, :],
                            scalar=const[:, K_PAIR + n:K_PAIR + n + 1],
                            in1=slot(KROPE + n)[0][:, half, :].bitcast(F32), op0=ALU.mult, op1=ALU.subtract))
                    low.skip(1)
                    dve.sem_inc(low_ready, 1)

                latent_sum(2)
                keep(kv[0])
                keep(kr[0])
                latent_parts(q_lat[0], G_Q, CQ, 0)
                rope_key(0)
                latent_sum(2)
                keep(kv[1])
                latent_parts(q_lat[1], G_Q, CQ, 1)
                keep(kr[1])
                copied()
                latent_sum(1)
                latent_parts([kv[0]], G_KV, CKV, 0)
                latent_sum(1)
                latent_parts([kv[1]], G_KV, CKV, 1)
                rope_key(1)
                for pair in range(2):
                    for half in range(2):
                        s = done.slot
                        dve.wait_ge(tile_done, done.next())
                        rope(s, c_tab, half, c_t)
                        signal(dve.tensor_tensor(c_t[:, 0, :], c_t[:, 1, :], c_t[:, 2, :], ALU.add),
                               value_ready, value)
                        to_low(slot(QROPE + pair)[1][:, half, :], slot(QROPE + pair)[0][:, half, :], c_t[:, 0, :])
                for t in range(8):
                    s = done.slot
                    done.skip(1)
                    dve.wait_ge(high_ready, high.next())
                    signal(dve.tensor_tensor(m_vl[:, t, :], tile(s, 256), m_vh[:, t, :].bitcast(F32), ALU.subtract),
                           tile_read, read)
                dve.sem_inc(phase_done, 1)

                def attend(width_of, banks, scale, masked, prob, parts_h, parts_l, to_tile, prepare=None):
                    step = 0

                    def next_head(h):
                        if prepare and h < HEADS:
                            prepare(h)

                    def maximum(q):
                        n = width_of(q)
                        s = done.slot
                        dve.wait_ge(tile_done, done.next(banks))
                        if masked:
                            view = tile(s, 256, n - 256)
                            at = K_CAUSAL + 256 * (q % 2)
                            link(dve.tensor_tensor(view, view, const[:, at:at + 256], ALU.add))
                        link(dve.reduce_max(stat[:, 0, q:q + 1], tile(s, n), AX.X))
                        signal(dve.tensor_scalar(stat[:, 1, q:q + 1], stat[:, 0, q:q + 1], -scale, None, ALU.mult),
                               value_ready, value)

                    def normalise(q):
                        dve.wait_ge(act_ready, acts.next())
                        read.skip(banks)
                        dve.sem_inc(tile_read, banks)
                        link(dve.reciprocal(stat[:, 3, q:q + 1], stat[:, 2, q:q + 1]))
                        signal(dve.tensor_scalar(prob(q), prob(q), stat[:, 3, q:q + 1], None, ALU.mult),
                               part_ready, part)

                    def one_step():
                        nonlocal step
                        a = auxd.slot
                        auxd.skip(1)
                        dve.wait_ge(high_ready, high.next())
                        signal(dve.tensor_tensor(parts_l[:, step % PARTS, :], aux(a),
                                                 parts_h[:, step % PARTS, :].bitcast(F32), ALU.subtract),
                               aux_read, auxr)
                        step += 1

                    def finish(h, i):
                        o = outr.slot
                        dve.wait_ge(out_step, outd.next(width_of(2 * i) // 256))
                        rows = slice(64 * (h % 2), 64 * (h % 2) + 64)
                        to = branch[rows, i // 2, to_tile + h // 2, (i % 2) * 256:(i % 2) * 256 + 256]
                        signal(dve.tensor_copy(to, outs(o, 256)[rows]), out_read, outr)

                    before_last = []

                    def first_step(h, i):
                        one_step()
                        if before_last:
                            finish(*before_last.pop())
                        before_last.append((h, i))

                    def steps(h, i):
                        first_step(h, i)
                        for j in range(width_of(2 * i) // 256 - 1):
                            one_step()

                    def mixed(h, i, before):
                        n = width_of(2 * before[1]) // 256 if before else 0
                        maximum(2 * i)
                        maximum(2 * i + 1)
                        if n:
                            first_step(*before)
                        normalise(2 * i)
                        if n > 1:
                            one_step()
                        normalise(2 * i + 1)
                        for j in range(n - 2):
                            one_step()

                    next_head(0)
                    for h in range(HEADS):
                        attention_order(h, next_head, steps, mixed)
                    finish(*before_last.pop())

                def latent_head(h):
                    for th, tl in ((m_qh, m_ql), (m_kh, m_kl)):
                        for half in range(2):
                            cols = slice(half * HALF, (half + 1) * HALF)
                            s = done.slot
                            done.skip(1)
                            dve.wait_ge(high_ready, high.next())
                            signal(dve.tensor_tensor(tl[:, cols], tile(s), th[:, cols].bitcast(F32), ALU.subtract),
                                   tile_read, read)

                attend(latent_width, 2, ATT_SCALE, True, latent_probs, m_ph, m_pl, 4, latent_head)
                dve.sem_inc(phase_done, 1)

                ld.skip(16)
                sqr.other()
                dve.wait_ge(square_ready, sqr.at())
                for k in range(1, KT):
                    link(dve.tensor_tensor(e_square[:, 0, :], e_square[:, 0, :], e_square[:, k, :], ALU.add))
                dve.sem_inc(sum_ready, 1)
                for k in range(2):
                    dve.wait_ge(high_ready, high.next())
                    link(dve.tensor_tensor(slot(MQ + k)[1], branch[:, :, 6 + k, :], slot(MQ + k)[0].bitcast(F32),
                                           ALU.subtract))
                low.skip(1)
                dve.sem_inc(low_ready, 1)
                take_rsqrt()
                for k in range(KT):
                    link(dve.scalar_tensor_tensor(
                        out=e_mem[:, k, :], in0=e_mem[:, k, :], scalar=gain[:, G_MEM + k:G_MEM + k + 1],
                        in1=e_rsqrt[:, :], op0=ALU.mult, op1=ALU.mult))
                dve.sem_inc(rsqrt_used, 1)
                value.skip(1)
                dve.sem_inc(value_ready, 1)
                to_low(e_nl[:, :, :], e_nh[:, :, :], e_mem[:, :, :])
                for t in range(2):
                    s = done.slot
                    done.skip(1)
                    dve.wait_ge(high_ready, high.next(2))
                    for n in range(2):
                        ins = dve.scalar_tensor_tensor(
                            out=e_kl[:, 2 * t + n, :], in0=tile(s, MEM), scalar=const[:, K_HALVES + n:K_HALVES + n + 1],
                            in1=e_kh[:, 2 * t + n, :].bitcast(F32), op0=ALU.mult, op1=ALU.subtract)
                        if n:
                            signal(ins, tile_read, read)
                        else:
                            link(ins)
                for t in range(2):
                    s = done.slot
                    done.skip(1)
                    dve.wait_ge(high_ready, high.next())
                    signal(dve.tensor_tensor(e_vl[:, t, :], tile(s, MEM), e_vh[:, t, :].bitcast(F32), ALU.subtract),
                           tile_read, read)
                attend(memory_width, 1, MEM_SCALE, False, memory_probs, e_ph, e_pl, 6)
                dve.sem_inc(phase_done, 1)

                for half in range(2):
                    for m in range(KT):
                        to_low(op_l[:, half, m, :], op_h[:, half, m, :], branch[:, half, m, :])
                for half in range(2):
                    for m in range(KT):
                        done.skip(1)
                        dve.wait_ge(act_ready, acts.next())
                        add_square(f_sum[:, half, :], f_square, m == 0)
                        read.skip(1)
                        dve.sem_inc(tile_read, 1)
                        if half:
                            if m == 0:
                                boundary_residual(0, G_POST_MIX, range(0, 3))
                            elif m < 4:
                                boundary_residual(0, G_POST_MIX, range(2 * m + 1, min(2 * m + 3, KT)))
                            elif m > 4:
                                norm_tiles(0, G_PRE_FFN, range(3 * m - 15, min(3 * m - 12, KT)))
                    dve.sem_inc(norm_sum_ready, 1)
                st[0].skip(16)

                for half in range(2):
                    post, pre = (G_POST_FFN, G_NEXT) if half else (G_POST_MIX, G_PRE_FFN)

                    def hidden(j, u):
                        done.skip(1)
                        s = done.slot
                        dve.wait_ge(tile_done, done.next())
                        dve.wait_ge(act_ready, acts.next())
                        signal(dve.tensor_tensor(f_hidden[:, u, :], f_gate[:, u, :], tile(s), ALU.mult),
                               value_ready, value)
                        read.skip(2)
                        dve.sem_inc(tile_read, 2)
                        to_low(a_l[:, j, :], a_h[:, j, :], f_hidden[:, u, :])

                    for g, size in enumerate(GROUPS):
                        if g == 0:
                            for j in range(size):
                                hidden(j, j % 2)
                                if j in (2, 3):
                                    boundary_residual(1 - half, post, range(4 * j - 8, 4 * j - 4))
                                elif j > 5:
                                    norm_tiles(1 - half, pre, range(4 * j - 24, 4 * j - 20))
                            dve.wait_ge(stored[half], st[half].at(16))
                            st[1 - half].skip(16)
                        else:
                            with repeat(dve, size // 2, counts) as i:
                                for u in range(2):
                                    hidden(i * 2 + u, u)
                        for m in range(KT + (g == 2)):
                            if m < KT:
                                s = done.slot
                                dve.wait_ge(tile_done, done.next())
                                y = branch[:, half, m, :]
                                if g == 0:
                                    signal(dve.tensor_copy(y, tile(s)), tile_read, read)
                                else:
                                    signal(dve.tensor_tensor(y, y, tile(s), ALU.add), tile_read, read)
                                if g == 2:
                                    value.skip(1)
                                    dve.sem_inc(value_ready, 1)
                            if g == 2 and m:
                                add_square(f_sum[:, half, :], f_square, m == 1)
                    dve.sem_inc(norm_sum_ready, 1)

            boundary_residual(1, G_POST_FFN, range(KT), squares=False)
            dve.sem_inc(finished, 1)


def _block(w):
    k, n = w.shape
    return w.reshape(k // P, P, n).transpose(1, 0, 2).reshape(P, -1)


def _layer_blocks(w_in, w_uq, w_ukv, w_mem_kv, w_out, w_gate, w_up, w_down):
    cols = lambda w, at, n=P: _block(w[:, at:at + n])
    found = [cols(w_in, at) for at in (2048, 2176, 2496, 2624)]
    for h in range(HEADS):
        found += [cols(w_in, part * 512 + h * P) for part in range(4)]
    rope_key = w_in[:, 2432:2496]
    rope_key = np.concatenate([rope_key[:, :32]] * 2 + [rope_key[:, 32:]] * 2, 1)
    found += [cols(w_in, 2304), _block(rope_key)]
    uq = w_uq.reshape(QRANK, HEADS, NOPE + ROPE)
    ukv = w_ukv.reshape(KVRANK, HEADS, NOPE + VDIM)
    found += [_block(uq[:, :, :NOPE].reshape(QRANK, -1))]
    rope_q = uq[:, :, NOPE:].reshape(QRANK, 2, 2, 2, 32).transpose(0, 1, 3, 2, 4).reshape(QRANK, -1)
    found += [np.concatenate([_block(rope_q), ukv[:, :, :NOPE].reshape(KVRANK, -1)], 1)]
    found += [cols(w_mem_kv, 0), cols(w_mem_kv, P)]
    found += [_block(w_mem_kv[k * 512:(k + 1) * 512, 256:]) for k in range(2)]
    found += [cols(w_out, m * P) for m in range(KT)]
    at = 0
    for size in GROUPS:
        for j in range(at, at + size):
            found += [cols(w_gate, j * P), cols(w_up, j * P)]
        rows = w_down[at * P:(at + size) * P]
        found += [np.pad(cols(rows, m * P), ((0, 0), (0, BLOCK - size * P))) for m in range(KT)]
        at += size
    return np.stack(found), np.ascontiguousarray(ukv[:, :, NOPE:].reshape(KVRANK, -1))


def _constants():
    c = np.zeros((P, K_ALL), np.float32)
    row, col = np.arange(P)[:, None], np.arange(P)[None, :]
    c[:, K_ID:K_ID + P] = row == col
    c[:, K_ONES:K_ONES + P] = 1.0
    c[:, K_TRI + P:K_TRI + 2 * P] = col >= row
    low = np.where(col > row, -3.0e38, 0.0)
    c[:, K_CAUSAL:K_CAUSAL + P] = low
    c[:, K_CAUSAL + P:K_CAUSAL + 2 * P] = -3.0e38
    c[:, K_CAUSAL + 3 * P:K_CAUSAL + 4 * P] = low
    for n in range(2):
        c[:, K_PAIR + n] = np.arange(P) // 32 % 2 == n
        c[:, K_HALVES + n] = np.arange(P) // 64 == n
    c[:, K_EPS] = EPS
    c[:, K_SIGN] = -1.0
    c[:64, K_TURN], c[:64, K_SHIFT] = 0.25, np.pi / 2
    for t, half in enumerate((64, 32)):
        c[:, K_FREQ + t] = np.float32(10000.0) ** (-(np.arange(P) % half).astype(np.float32) / np.float32(half))
    return c


def _decay():
    d, scales = np.zeros((HEADS, P, HALF), np.float32), np.zeros((P, HEADS, 8), np.float32)
    place = np.arange(HALF, dtype=np.float64)
    for h in range(HEADS):
        g = 1.0 - 2.0 ** (-5.0 - h)
        d[h] = g ** place * float(P) ** -0.5
        keys = (g ** -place).reshape(4, P).T
        scales[:, h, 0:4] = keys
        scales[:, h, 4:8] = keys * g ** HALF
    return d, scales


def kernel(x, mem, positions, pre_mix_g, w_in, mla_q_norm_g, w_uq, mla_kv_norm_g, w_ukv, mem_norm_g, w_mem_kv,
           w_out, post_mix_g, pre_ffn_g, w_gate, w_up, w_down, post_ffn_g):
    from concourse import bacc
    from concourse.bass_utils import run_bass_kernel_spmd

    names = (x, mem, positions, pre_mix_g, w_in, mla_q_norm_g, w_uq, mla_kv_norm_g, w_ukv, mem_norm_g, w_mem_kv,
             w_out, post_mix_g, pre_ffn_g, w_gate, w_up, w_down, post_ffn_g)
    (x, mem, positions, pre_mix_g, w_in, mla_q_norm_g, w_uq, mla_kv_norm_g, w_ukv, mem_norm_g, w_mem_kv,
     w_out, post_mix_g, pre_ffn_g, w_gate, w_up, w_down, post_ffn_g) = [np.asarray(a) for a in names]

    by_tile = lambda g: g.reshape(-1, P).T
    layers = [_layer_blocks(w_in[l], w_uq[l], w_ukv[l], w_mem_kv[l], w_out[l], w_gate[l], w_up[l], w_down[l])
              for l in range(LAYERS)]
    gains = np.stack([np.concatenate(
        [by_tile(mla_q_norm_g[l]), by_tile(mla_kv_norm_g[l]), by_tile(mem_norm_g[l]), by_tile(post_mix_g[l]),
         by_tile(pre_ffn_g[l]), by_tile(post_ffn_g[l]), by_tile(pre_mix_g[min(l + 1, LAYERS - 1)])], 1)
        for l in range(LAYERS)])
    first = np.zeros_like(gains[:1])
    first[0, :, G_NEXT:] = by_tile(pre_mix_g[0])
    gains = np.concatenate([first, gains])
    arrays = {
        "x_in": x[0].T.reshape(KT, P, 2, HALF).transpose(2, 1, 0, 3),
        "mem_in": mem[0].T.reshape(KT, P, MEM).transpose(1, 0, 2),
        "positions_in": positions[0],
        "weights_in": np.concatenate([b for b, _ in layers]),
        "value_weights_in": np.stack([v for _, v in layers]),
        "gains_in": gains,
        "consts_in": _constants(),
        "decay_in": _decay()[0],
        "scales_in": _decay()[1],
    }
    arrays = {n: np.ascontiguousarray(a) for n, a in arrays.items()}
    nc = bacc.Bacc("TRN2", target_bir_lowering=False, num_devices=1)
    aps = [nc.dram_tensor(n, a.shape, mybir.dt.from_np(a.dtype), kind="ExternalInput").ap()
           for n, a in arrays.items()]
    out = nc.dram_tensor("out_0_dram", (2, P, KT, HALF), F32, kind="ExternalOutput").ap()
    build(nc, *aps, out)
    r = run_bass_kernel_spmd(nc, [arrays], core_ids=[0])
    y = r.results[0]["out_0_dram"]
    return np.ascontiguousarray(y.transpose(2, 1, 0, 3).reshape(D, SEQ).T)[None]
```

```python
from contextlib import ExitStack, contextmanager

import numpy as np

import concourse.bass as bass
from concourse import mybir

ALU = mybir.AluOpType
ACT = mybir.ActivationFunctionType
AX = mybir.AxisListType
F32 = mybir.dt.float32
F32R = mybir.dt.float32r
I32 = mybir.dt.int32

P = 128
LAYERS = 2
SEQ = 1024
D = 1024
HALF = 512
KT = D // P
HEADS = 4
MEM = 256
QRANK = 256
KVRANK = 128
NOPE, ROPE, VDIM = 128, 64, 64
D_FF = 2816
GROUPS = (8, 8, 6)
BLOCK = 1024
MIXER_BLOCKS, OUT_BLOCKS, FFN_BLOCKS = 28, 8, 68
STORED_BLOCKS = MIXER_BLOCKS + OUT_BLOCKS + FFN_BLOCKS
EPS = 1e-6
LAYER_TILES = 328
ATT_SCALE = float(NOPE + ROPE) ** -0.5
MEM_SCALE = float(64) ** -0.5

RAW, SPLIT, TILES, AUX, OUTS = 2, 4, 4, 2, 2
X_TILES = 4
SCORES, PARTS = 4, 3

G_Q, G_KV, G_MEM, G_POST_MIX, G_PRE_FFN, G_POST_FFN, G_NEXT = 0, 2, 3, 11, 19, 27, 35
GAINS = 43

K_ID, K_ONES, K_TRI, K_CAUSAL, K_COLS = 0, 128, 256, 512, 1024
K_PAIR, K_HALVES, K_EPS, K_SIGN, K_FREQ, K_TURN, K_SHIFT, K_ALL = 1024, 1026, 1028, 1029, 1030, 1032, 1033, 1034

TWO_PI = 2.0 * np.pi
MAGIC = 12582912.0


class Count:

    def __init__(self, engine, name, start=0, ring=1, slot=0):
        self.engine, self.ring, self.slot, self.since = engine, ring, slot, 0
        self.base = engine.alloc_register(name)
        engine.reg_mov(self.base, start)

    def at(self, ahead=0):
        return self.engine.snap(self.base) + (self.since + ahead)

    def next(self, n=1):
        self.skip(n)
        return self.at()

    def skip(self, n=1):
        self.since += n
        self.slot = (self.slot + n) % self.ring

    def other(self, n=1):
        self.since += n

    def fold(self):
        if self.since:
            self.engine.reg_add(self.base, self.base, self.since)
            self.since = 0


@contextmanager
def repeat(engine, times, counts):
    for c in counts:
        c.fold()
    with engine.Fori(0, times) as i:
        yield i
        for c in counts:
            c.fold()


def build(nc, x, mem, positions, weights, value_weights, gains, consts, decay, scales, out):
    cos_sin = nc.dram_tensor("cos_sin", (2, P, 2, SEQ), F32, kind="Internal").ap()
    with ExitStack() as ctx:
        def sb(name, shape, dt=F32, within=None):
            return (within or ctx).enter_context(nc.sbuf_tensor(name, [P] + shape, dt))

        def sem(name):
            return ctx.enter_context(nc.semaphore(name))

        op_h, op_l = sb("op_high", [2, KT, HALF], F32R), sb("op_low", [2, KT, HALF], F32R)
        w_raw = sb("w_raw", [RAW, BLOCK])
        w_h, w_l = sb("w_high", [SPLIT, BLOCK], F32R), sb("w_low", [SPLIT, BLOCK], F32R)
        branch = sb("branch", [2, KT, HALF])
        const = sb("const", [K_ALL])
        gain = sb("gain", [GAINS])
        mem_rsqrt = sb("mem_rsqrt", [MEM])
        head_scales = sb("head_scales", [HEADS, 8])
        stat = sb("stat", [4, 8])
        ident, ones = const[:, K_ID:K_ID + P], const[:, K_ONES:K_ONES + P]
        tri = const[:, K_TRI:K_TRI + 256]
        eps = const[:, K_EPS:K_EPS + 1]

        phase = ExitStack()
        x_old = sb("x_old", [X_TILES, HALF], F32, phase)
        b_square, f_square = sb("b_square", [2, HALF], F32, phase), sb("f_square", [2, HALF], F32, phase)
        f_sum = sb("f_sum", [2, HALF], F32, phase)
        b_rsqrt = sb("b_rsqrt", [HALF], F32, phase)
        b_norm = sb("b_norm", [2, HALF], F32, phase)
        f_gate, f_hidden = sb("f_gate", [2, HALF], F32, phase), sb("f_hidden", [2, HALF], F32, phase)
        start = ExitStack()
        s_pos, s_posf = sb("s_pos", [SEQ], I32, start), sb("s_posf", [SEQ], F32, start)
        s_ang, s_turn = sb("s_ang", [SEQ], F32, start), sb("s_turn", [SEQ], F32, start)
        s_tab = sb("s_tab", [2, SEQ], F32, start)
        s_mem = sb("s_mem", [KT, MEM], F32, start)
        start.close()
        a_h, a_l = sb("a_high", [8, HALF], F32R, phase), sb("a_low", [8, HALF], F32R, phase)
        phase.close()

        phase = ExitStack()
        r_qh, r_ql = sb("r_q_high", [SEQ], F32R, phase), sb("r_q_low", [SEQ], F32R, phase)
        r_kh, r_kl = sb("r_k_high", [SEQ], F32R, phase), sb("r_k_low", [SEQ], F32R, phase)
        r_vh, r_vl = sb("r_v_high", [SEQ], F32R, phase), sb("r_v_low", [SEQ], F32R, phase)
        r_sh, r_sl = sb("r_s_high", [SCORES, HALF], F32R, phase), sb("r_s_low", [SCORES, HALF], F32R, phase)
        r_vt = sb("r_v_transposed", [HALF], F32, phase)
        r_gate = sb("r_gate", [SEQ], F32, phase)
        r_tab = sb("r_cos_sin", [2, SEQ], F32, phase)
        r_decay, r_scale = sb("r_decay", [HALF], F32, phase), sb("r_scale", [8], F32, phase)
        r_t = sb("r_temp", [3, HALF], F32, phase)
        r_square = sb("r_square", [HALF], F32, phase)
        r_rsqrt = sb("r_rsqrt", [HALF], F32, phase)
        phase.close()

        phase = ExitStack()
        m_vh, m_vl = sb("m_v_high", [8, 256], F32R, phase), sb("m_v_low", [8, 256], F32R, phase)
        latent = ExitStack()
        c_kv = sb("c_kv", [SEQ], F32, latent)
        c_spare = sb("c_spare", [SEQ], F32, latent)
        c_tab = sb("c_cos_sin", [2, SEQ], F32, latent)
        c_t = sb("c_temp", [4, HALF], F32, latent)
        c_square, c_sum = sb("c_square", [2, HALF], F32, latent), sb("c_sum", [2, HALF], F32, latent)
        c_q_rsqrt, c_rsqrt = sb("c_q_rsqrt", [SEQ], F32, latent), sb("c_rsqrt", [SEQ], F32, latent)
        c_norm = sb("c_norm", [2, HALF], F32, latent)
        z_raw = sb("z_raw", [256], F32, latent)
        z_h, z_l = sb("z_high", [256], F32R, latent), sb("z_low", [256], F32R, latent)
        latent.close()
        m_qh, m_ql = sb("m_q_high", [SEQ], F32R, phase), sb("m_q_low", [SEQ], F32R, phase)
        m_kh, m_kl = sb("m_k_high", [SEQ], F32R, phase), sb("m_k_low", [SEQ], F32R, phase)
        m_p = sb("m_p", [20 * 256], F32, phase)
        m_ph, m_pl = sb("m_p_high", [PARTS, 512], F32R, phase), sb("m_p_low", [PARTS, 512], F32R, phase)
        phase.close()

        phase = ExitStack()
        e_nh, e_nl = sb("e_norm_high", [KT, MEM], F32R, phase), sb("e_norm_low", [KT, MEM], F32R, phase)
        e_mem = sb("e_mem", [KT, MEM], F32, phase)
        e_kh, e_kl = sb("e_k_high", [HEADS, MEM], F32R, phase), sb("e_k_low", [HEADS, MEM], F32R, phase)
        e_vh, e_vl = sb("e_v_high", [2, 256], F32R, phase), sb("e_v_low", [2, 256], F32R, phase)
        e_p = sb("e_p", [8 * MEM], F32, phase)
        e_ph, e_pl = sb("e_p_high", [PARTS, 512], F32R, phase), sb("e_p_low", [PARTS, 512], F32R, phase)
        phase.close()

        def slot(n):
            return [t[:, n // 4, 2 * (n % 4):2 * (n % 4) + 2, :] for t in (op_h, op_l)]

        CQ, KROPE, CKV, QROPE, MQ = 0, 2, 4, 5, 0

        def latent_width(q):
            return 256 * (q // 2 + 1)

        def latent_probs(q, at=0, n=None):
            pair, width = q // 2, latent_width(q)
            start = 256 * pair * (pair + 1) + (q % 2) * width + at
            return m_p[:, start:start + (n or width)]

        def memory_width(q):
            return MEM

        def memory_probs(q, at=0, n=None):
            return e_p[:, q * MEM + at:q * MEM + at + (n or MEM)]

        def attention_order(head, next_head, steps, mixed):
            mixed(head, 0, (head - 1, 3) if head else None)
            mixed(head, 1, None)
            mixed(head, 2, (head, 0))
            mixed(head, 3, (head, 1))
            next_head(head + 1)
            steps(head, 2)
            if head == HEADS - 1:
                steps(head, 3)

        psum = ctx.enter_context(nc.psum_tensor("psum", [P, 8 * 512], F32))

        def tile(s, n=512, at=0):
            return psum[:, s * 512 + at:s * 512 + at + n]

        def aux(s, n=512, at=0):
            return psum[:, (TILES + s) * 512 + at:(TILES + s) * 512 + at + n]

        def outs(s, n=512, at=0):
            return psum[:, (TILES + AUX + s) * 512 + at:(TILES + AUX + s) * 512 + at + n]

        w_loaded = [sem(f"w_loaded{i}") for i in range(RAW)]
        loaded = sem("loaded")
        gain_loaded = sem("gain_loaded")
        decay_loaded, mem_loaded = sem("decay_loaded"), sem("mem_loaded")
        x_loaded = [sem(f"x_loaded{i}") for i in range(X_TILES)]
        stored = [sem(f"x_stored{i}") for i in range(2)]
        tables_stored = sem("tables_stored")
        w_rounded = sem("w_rounded")
        w_split = sem("w_split")
        pool_waited = sem("pool_waited")
        tile_done = sem("tile_done")
        aux_done = sem("aux_done")
        out_step = sem("out_step")
        norm_sums_done = sem("norm_sums_done")
        tile_read = sem("tile_read")
        aux_read = sem("aux_read")
        out_read = sem("out_read")
        dve_link = sem("dve_link")
        low_ready = sem("low_ready")
        value_ready = sem("value_ready")
        sum_ready = sem("sum_ready")
        part_ready = sem("part_ready")
        square_used = sem("square_used")
        rsqrt_used = sem("rsqrt_used")
        x_ready = sem("x_ready")
        norm_sum_ready = sem("norm_sum_ready")
        norm_square_used = sem("norm_square_used")
        norm_value_ready = sem("norm_value_ready")
        norm_low_ready = sem("norm_low_ready")
        phase_done = sem("phase_done")
        high_ready = sem("high_ready")
        act_ready = sem("act_ready")
        square_ready = sem("square_ready")
        log_ready = sem("log_ready")
        rsqrt_ready = sem("rsqrt_ready")
        norm_square_ready = sem("norm_square_ready")
        norm_high_ready = sem("norm_high_ready")
        norm_rsqrt_ready = sem("norm_rsqrt_ready")

        finished = sem("finished")
        cleared = sem("cleared")

        block = ctx.enter_context(nc.Block())

        def step_index(half, kb):
            return 4 * half + kb

        def scale_of(half, kb):
            i = kb - 4 * half if kb >= 4 * half else 4 + kb
            return r_scale[:, i:i + 1]

        def columns(half, kb):
            local = kb - 4 * half
            return (0, False) if local < 0 else (min(128 * local, 256), True)

        @block.sync
        def _(sp):
            split = Count(sp, "sp_split", 0, RAW)

            def load(index):
                s = split.slot
                sp.wait_ge(w_split, split.next())
                sp.dma_start(w_raw[:, s, :], weights[index]).then_inc(w_loaded[s], 16)

            layer = Count(sp, "sp_layer")
            with sp.Fori(0, LAYERS) as l:
                def run(first, n):
                    split.fold()
                    with sp.Fori(0, n // RAW) as i:
                        for s in range(RAW):
                            load(l * STORED_BLOCKS + i * RAW + (first + s))
                        split.fold()
                run(0, 20)
                run(0, 4)
                run(20, MIXER_BLOCKS - 20)
                for half in range(2):
                    run(MIXER_BLOCKS, OUT_BLOCKS)
                for half in range(2):
                    run(MIXER_BLOCKS + OUT_BLOCKS, FFN_BLOCKS)

        @block.gpsimd
        def _(pool):
            pool.sem_inc(w_split, RAW)
            pool.memset(branch[:, 1], 0.0).then_inc(cleared, 1)
            raw = [Count(pool, f"pool_loaded{i}") for i in range(RAW)]
            rounded = Count(pool, "pool_rounded")
            split = Count(pool, "pool_split", RAW)
            done = Count(pool, "pool_tiles", TILES)
            turn = [0]

            def counted():
                pool.sem_inc(pool_waited, 1)

            def block_split(last_use, more=0):
                r, s = turn[0] % RAW, turn[0] % SPLIT
                turn[0] += 1
                pool.wait_ge(w_loaded[r], raw[r].next(16))
                counted()
                pool.wait_ge(tile_done, done.at(last_use + 1) + more)
                counted()
                pool.tensor_scalar(w_h[:, s, :], w_raw[:, r, :], 1.0, 1.0, ALU.mult, ALU.mult).then_inc(w_rounded, 1)
                pool.wait_ge(w_rounded, rounded.next())
                pool.tensor_tensor(w_l[:, s, :], w_raw[:, r, :], w_h[:, s, :].bitcast(F32),
                                   ALU.subtract).then_inc(w_split, 1)
                pool.wait_ge(w_split, split.next())
                counted()

            counts = raw + [rounded, split]
            with repeat(pool, LAYERS, counts):
                for s in range(4):
                    block_split(s - 4)
                for s in range(4):
                    block_split(s)
                with repeat(pool, HEADS - 1, counts) as h:
                    for s in range(4):
                        block_split(8 + s, h * 10)
                for last in (37, 38, 40, 41, 42, 43, 45, 46, 49, 51, 121, 123, 140, 141, 143, 143):
                    block_split(last)
                with repeat(pool, 148 // 4, counts) as i:
                    for s in range(4):
                        block_split(176 + s, i * 4)
                done.skip(LAYER_TILES)
                done.fold()

        @block.tensor
        def _(pe):
            pe.sem_inc(tile_done, TILES)
            pe.sem_inc(out_step, SCORES)
            split = Count(pe, "pe_split", RAW, SPLIT)
            tiles = Count(pe, "pe_tiles", 0, TILES)
            auxs = Count(pe, "pe_aux", 0, AUX, 1)
            outr = Count(pe, "pe_outs", 0, OUTS)
            low = Count(pe, "pe_low")
            sums = Count(pe, "pe_sums")
            parts = Count(pe, "pe_parts")
            squares = Count(pe, "pe_squares")
            norm_sums = Count(pe, "pe_norm_sums")
            norm_low = Count(pe, "pe_norm_low")
            phases = Count(pe, "pe_phase")
            counts = [split, tiles, auxs, outr, low, sums, parts, squares, norm_sums, norm_low, phases]

            def product(to, left, right, first, last):
                pe.matmul(to, left[0], right[1], start=first, stop=False)
                pe.matmul(to, left[1], right[0], start=False, stop=False)
                return pe.matmul(to, left[0], right[0], start=False, stop=last)

            def weight(s, at, n=P):
                return w_h[:, s, at:at + n], w_l[:, s, at:at + n]

            def new_tile(n=1):
                s = tiles.slot
                pe.wait_ge(tile_read, tiles.next(n))
                return s

            def new_aux():
                s = auxs.slot
                pe.wait_ge(aux_read, auxs.next())
                return s

            def column_sums(source, n=HALF):
                pe.wait_ge(sum_ready, sums.next())
                pe.matmul(aux(new_aux(), n), ones, source, start=True, stop=True).then_inc(aux_done, 1)

            def project(half, s, source_h, source_l, depth=KT, ready=None, during=None):
                to = tile(new_tile())
                for k in range(depth):
                    if during:
                        during(k)
                    if ready is not None:
                        pe.wait_ge(low_ready, low.at(ready + k + 1))
                    mm = product(to, weight(s, k * P), (source_h[:, k, :], source_l[:, k, :]),
                                 k == 0, k == depth - 1)
                mm.then_inc(tile_done, 1)

            def norm_sum(half):
                pe.wait_ge(norm_sum_ready, norm_sums.next())
                pe.matmul(outs(1), ones, f_sum[:, half, :], start=True, stop=True).then_inc(norm_sums_done, 1)

            pe.wait_ge(phase_done, phases.next())
            norm_sum(0)
            column_sums(s_mem[:, 0, :], MEM)
            squares.skip(1)

            with repeat(pe, LAYERS, counts):
                norm_low.skip(KT)
                for s in range(4):
                    pe.wait_ge(w_split, split.next())
                    def during(k):
                        if k == 4:
                            norm_sum(1)
                        pe.wait_ge(norm_low_ready, norm_low.at(k + 1 - KT))
                    project(0, s, op_h[:, 0], op_l[:, 0], during=None if s else during)

                def score(half, kb):
                    c, _ = columns(half, kb)
                    if kb == 0:
                        pe.wait_ge(low_ready, low.next(2))
                    q0 = half * HALF
                    mm = product(aux(new_aux(), HALF - c),
                                 (r_kh[:, kb * P:(kb + 1) * P], r_kl[:, kb * P:(kb + 1) * P]),
                                 (r_qh[:, q0 + c:q0 + HALF], r_ql[:, q0 + c:q0 + HALF]), True, True)
                    mm.then_inc(aux_done, 1)

                def value(half, kb, later):
                    c, _ = columns(half, kb)
                    if kb == 0:
                        pe.wait_ge(out_read, outr.next())
                    pe.wait_ge(aux_read, auxs.at(AUX - later))
                    s = step_index(half, kb) % SCORES
                    mm = product(outs(half, HALF - c, c),
                                 (r_vh[:, kb * P:(kb + 1) * P], r_vl[:, kb * P:(kb + 1) * P]),
                                 (r_sh[:, s, 0:HALF - c], r_sl[:, s, 0:HALF - c]),
                                 kb == 0, kb == 4 * half + 3)
                    mm.then_inc(out_step, 1)

                def head_norm():
                    pe.wait_ge(square_ready, squares.next())
                    pe.matmul(tile(new_tile()), ones, r_square[:, :], start=True, stop=True).then_inc(tile_done, 1)

                def turn_values():
                    pe.wait_ge(part_ready, parts.next())
                    a = new_aux()
                    for b in range(4):
                        mm = pe.transpose(aux(a, P, b * P), r_vt[:, b * P:(b + 1) * P], ident)
                    mm.then_inc(aux_done, 1)

                def second_half(after, turn_first=False):
                    for s in range(4):
                        def during(k):
                            if turn_first and s == 0:
                                pe.wait_ge(norm_low_ready, norm_low.at(k + 1 - KT))
                                if k == 6:
                                    turn_values()
                                elif k == 7:
                                    score(0, s)
                            elif k == 1:
                                score(0, s)
                            elif k == 3 and s:
                                value(0, s - 1, 1)
                            elif k in (3, 5) and s == 0 and after:
                                value(1, 6 + (k == 5), 3 - (k == 5))
                            elif k == 5 and s == 3:
                                turn_values()
                        project(1, s, op_h[:, 1], op_l[:, 1], during=during)
                        if s == 1 and after:
                            head_norm()
                    split.skip(4)

                def under(half, values):
                    for s in range(4):
                        pe.wait_ge(w_split, split.at(s + 1))

                        def during(k):
                            if k in (0, 2):
                                score(1, 2 * s + k // 2)
                            elif k == 4 and s == 0:
                                value(0, 3, 3)
                            elif k in (4, 6) and s:
                                value(1, 2 * s - 2 + (k == 6), 3 - (k == 6))
                            elif k == 7 and s == 3 and values:
                                turn_values()
                        project(half, s, op_h[:, half], op_l[:, half], during=during)
                        if s == 1:
                            head_norm()

                for s in range(4):
                    pe.wait_ge(w_split, split.at(s + 1))
                    project(0, s, op_h[:, 0], op_l[:, 0],
                            during=(lambda k: norm_sum(1) if k == 4 else None) if s == 1 else None)
                norm_low.skip(KT)
                phases.skip(1)
                second_half(False, True)
                with repeat(pe, HEADS - 1, counts):
                    under(0, True)
                    second_half(True)
                under(1, False)
                split.skip(4)

                def pair_sums(source):
                    pe.wait_ge(sum_ready, sums.next())
                    for half in range(2):
                        assert auxs.slot == half
                        pe.matmul(aux(new_aux()), ones, source[:, half, :], start=True, stop=True)\
                            .then_inc(aux_done, 1)

                def during(k):
                    if k in (1, 3):
                        value(1, 6 + k // 2, 1 - k // 2)
                    elif k == 5:
                        pair_sums(r_t)

                def kv_sums(k):
                    if k == 5:
                        pair_sums(c_sum)

                for n, (s, half) in enumerate(((0, 0), (0, 1), (1, 0), (1, 1))):
                    if half == 0:
                        pe.wait_ge(w_split, split.next())
                    project(half, (split.slot - 1) % SPLIT, op_h[:, half], op_l[:, half],
                            during=(during, None, kv_sums, None)[n])
                    if n == 0:
                        squares.skip(4)
                        head_norm()

                squares.skip(2 + 2 * 2 * KT)

                phases.skip(1)
                pe.wait_ge(low_ready, low.next(6))
                split.skip(2)
                pe.wait_ge(w_split, split.at())
                wx, wy = (split.slot - 2) % SPLIT, (split.slot - 1) % SPLIT

                def q_latent(k, half):
                    return tuple(t[:, 0, 2 * k + half, :] for t in (op_h, op_l))

                def kv_latent(half):
                    return tuple(t[:, half, :] for t in slot(CKV))

                for pair in range(2):
                    for half in range(2):
                        to = tile(new_tile())
                        for k in range(2):
                            mm = product(to, weight(wy, k * 256 + pair * P), q_latent(k, half), k == 0, k == 1)
                        mm.then_inc(tile_done, 1)
                kv_h, kv_l = slot(CKV)
                pe.wait_ge(low_ready, low.next(3))
                for t in range(8):
                    at = slice((t % 4) * P, (t % 4 + 1) * P)
                    if t % 2 == 0:
                        s = new_tile()
                    mm = product(tile(s, 256, 256 * (t % 2)), (kv_h[:, t // 4, at], kv_l[:, t // 4, at]),
                                 (z_h[:, :], z_l[:, :]), True, True)
                    if t % 2:
                        mm.then_inc(tile_done, 1)
                pe.wait_ge(low_ready, low.next(4))

                def attend(scores, values, width_of, prob, prob_parts, prepare=None):
                    step = 0

                    def next_head(h):
                        if prepare and h < HEADS:
                            prepare(h)

                    def steps(h, i):
                        nonlocal step
                        n = width_of(2 * i) // 256
                        pe.wait_ge(part_ready, parts.next(2))

                        def turn(j):
                            a = new_aux()
                            for kb in range(2):
                                for q in range(2):
                                    mm = pe.transpose(aux(a, P, kb * 256 + q * P),
                                                      prob(2 * i + q, (2 * j + kb) * P, P), ident)
                            mm.then_inc(aux_done, 1)

                        for j in range(n):
                            turn(j)
                            last_use(1)
                            pending.append((h, j, step % PARTS, j == 0, j == n - 1))
                            step += 1

                    pending = []

                    def last_use(later):
                        if not pending:
                            return
                        h, j, s, first, last = pending.pop()
                        if first:
                            pe.wait_ge(out_read, outr.next())
                        pe.wait_ge(aux_read, auxs.at(AUX - later))
                        o = (outr.slot - 1) % OUTS
                        for kb in range(2):
                            mm = product(outs(o, 256), values(h, 2 * j + kb),
                                         (prob_parts[0][:, s, kb * 256:(kb + 1) * 256],
                                          prob_parts[1][:, s, kb * 256:(kb + 1) * 256]),
                                         first and kb == 0, last and kb == 1)
                        mm.then_inc(out_step, 1)

                    def mixed(h, i, before):
                        if i == 0 and prepare:
                            pe.wait_ge(tile_read, tiles.at(TILES))
                        scores(h, 2 * i)
                        scores(h, 2 * i + 1)
                        if before:
                            steps(*before)

                    next_head(0)
                    for h in range(HEADS):
                        attention_order(h, next_head, steps, mixed)
                    last_use(0)

                pe.wait_ge(phase_done, phases.next())

                def latent_head(h):
                    for half in range(2):
                        to = tile(new_tile())
                        for k in range(2):
                            mm = product(to, weight(wx, k * 512 + h * P), q_latent(k, half), k == 0, k == 1)
                        mm.then_inc(tile_done, 1)
                    for half in range(2):
                        product(tile(new_tile()), weight(wy, 512 + h * P), kv_latent(half), True, True)\
                            .then_inc(tile_done, 1)

                def latent_scores(h, q):
                    s = new_tile(2)
                    n = 256 * (q // 2 + 1)
                    kr = slot(KROPE + h % 2)
                    qr = slot(QROPE + h // 2)
                    at = slice((q % 4) * P, (q % 4 + 1) * P)
                    for c in range(0, n, 512):
                        w = min(512, n - c)
                        to = tile(s, w, c)
                        product(to, (m_qh[:, q * P:(q + 1) * P], m_ql[:, q * P:(q + 1) * P]),
                                (m_kh[:, c:c + w], m_kl[:, c:c + w]), True, False)
                        mm = product(to, tuple(t[:, q // 4, at] for t in qr),
                                     tuple(t[:, c // 512, 0:w] for t in kr), False, True)
                    mm.then_inc(tile_done, 2)

                attend(latent_scores,
                       lambda h, kb: tuple(t[:, kb, (h // 2) * P:(h // 2 + 1) * P] for t in (m_vh, m_vl)),
                       latent_width, latent_probs, (m_ph, m_pl), latent_head)

                pe.wait_ge(phase_done, phases.next())
                pe.wait_ge(low_ready, low.next(2))
                for t in range(2):
                    s = split.slot
                    pe.wait_ge(w_split, split.next())
                    to = tile(new_tile(), MEM)
                    for k in range(KT):
                        if t == 0 and k % 2 == 0:
                            pe.wait_ge(low_ready, low.next())
                        mm = product(to, weight(s, k * P), (e_nh[:, k, :], e_nl[:, k, :]), k == 0, k == KT - 1)
                    mm.then_inc(tile_done, 1)
                s = split.slot
                pe.wait_ge(w_split, split.next(2))
                for t in range(2):
                    to = tile(new_tile(), MEM)
                    for k in range(KT):
                        mm = product(to, (e_nh[:, k, t * P:(t + 1) * P], e_nl[:, k, t * P:(t + 1) * P]),
                                     weight((s + k // 4) % SPLIT, (k % 4) * 256, 256), k == 0, k == KT - 1)
                    mm.then_inc(tile_done, 1)
                pe.wait_ge(tile_read, tiles.at(TILES))

                def memory_scores(h, q):
                    mq = slot(MQ + h // 2)
                    at = slice((q % 4) * P, (q % 4 + 1) * P)
                    product(tile(new_tile(), MEM), tuple(t[:, q // 4, at] for t in mq),
                            (e_kh[:, h, :], e_kl[:, h, :]), True, True).then_inc(tile_done, 1)

                attend(memory_scores,
                       lambda h, kb: tuple(t[:, kb, (h // 2) * P:(h // 2 + 1) * P] for t in (e_vh, e_vl)),
                       memory_width, memory_probs, (e_ph, e_pl))

                pe.wait_ge(phase_done, phases.next())
                for half in range(2):
                    for m in range(KT):
                        s = split.slot
                        pe.wait_ge(w_split, split.next())
                        project(half, s, op_h[:, half], op_l[:, half],
                                ready=half * KT if m == 0 else None,
                                during=(lambda k: norm_sum(0) if k == 4 else None) if half and m in (0, 5) else None)
                low.skip(2 * KT)

                for half in range(2):
                    norm_low.skip(KT)

                    def hidden(first=False):
                        for s in range(4):
                            pe.wait_ge(w_split, split.next())
                            if first and s == 0:
                                project(half, s, op_h[:, half], op_l[:, half],
                                        during=lambda k: pe.wait_ge(norm_low_ready, norm_low.at(k + 1 - KT)))
                            else:
                                project(half, s, op_h[:, half], op_l[:, half])

                    for g, size in enumerate(GROUPS):
                        if g == 0:
                            hidden(True)
                            norm_sum(1 - half)
                            with repeat(pe, size // 2 - 2, counts):
                                hidden()
                            norm_sum(1 - half)
                            hidden()
                        else:
                            with repeat(pe, size // 2, counts):
                                hidden()
                        with repeat(pe, 2, [c for c in counts if c is not low]):
                            for s in range(4):
                                pe.wait_ge(w_split, split.next())
                                project(half, s, a_h, a_l, depth=size, ready=0 if s == 0 else None)
                        low.skip(size)
            norm_sum(1)

        @block.scalar
        def _(act):
            act.sem_inc(square_used, 2)
            act.sem_inc(norm_square_used, 2)
            done = Count(act, "act_tiles", TILES, TILES)
            auxd = Count(act, "act_aux", 0, AUX, 1)
            outd = Count(act, "act_outs", 0)
            outr = Count(act, "act_out_read", OUTS, OUTS)
            value = Count(act, "act_value")
            used = Count(act, "act_square_used", 0, 2)
            rs_used = Count(act, "act_rsqrt_used")
            high = Count(act, "act_high")
            out_ = Count(act, "act_out")
            sqr = Count(act, "act_square")
            log = Count(act, "act_log")
            rsq = Count(act, "act_rsqrt")
            ld = Count(act, "act_loaded")
            mems = Count(act, "act_mem_loaded")
            xs = Count(act, "act_x")
            st = [Count(act, f"act_stored{i}") for i in range(2)]
            n_value = Count(act, "act_norm_value")
            n_used = Count(act, "act_norm_square_used", 0, 2)
            n_high = Count(act, "act_norm_high")
            n_square = Count(act, "act_norm_square")
            n_sums = Count(act, "act_norm_sums")
            n_rsqrt = Count(act, "act_norm_rsqrt")
            phases = Count(act, "act_phase", 1)
            counts = [done, auxd, outd, outr, value, used, rs_used, high, out_, sqr, log, rsq, ld, mems, xs, phases,
                      n_value, n_used, n_high, n_square, n_sums, n_rsqrt] + st

            def to_high(to, source, scale=1.0):
                act.activation(to, source, ACT.Copy, scale=scale).then_inc(high_ready, 1)
                act.wait_ge(high_ready, high.next())

            def to_value(to, source, func, **more):
                act.activation(to, source, func, **more).then_inc(act_ready, 1)
                act.wait_ge(act_ready, out_.next())

            def square(to, source):
                act.activation(to, source, ACT.Square).then_inc(square_ready, 1)
                act.wait_ge(square_ready, sqr.next())

            def square_ring(ring, source):
                s = used.slot
                act.wait_ge(square_used, used.next())
                square(ring[:, s, :], source)

            def rsqrt(log_to, to, dim, n=HALF):
                s = auxd.slot
                act.wait_ge(aux_done, auxd.next())
                act.wait_ge(rsqrt_used, rs_used.next())
                act.activation(log_to, aux(s, n), ACT.Ln, bias=eps, scale=1.0 / dim).then_inc(log_ready, 1)
                act.wait_ge(log_ready, log.next())
                act.activation(to, log_to, ACT.Exp, scale=-0.5).then_inc(rsqrt_ready, 1)
                act.wait_ge(rsqrt_ready, rsq.next())

            def norm_rsqrt():
                act.wait_ge(norm_sums_done, n_sums.next())
                act.activation(b_rsqrt[:, :], outs(1), ACT.Ln, bias=eps, scale=1.0 / D).then_inc(log_ready, 1)
                act.wait_ge(log_ready, log.next())
                act.activation(b_rsqrt[:, :], b_rsqrt[:, :], ACT.Exp, scale=-0.5).then_inc(norm_rsqrt_ready, 1)
                act.wait_ge(norm_rsqrt_ready, n_rsqrt.next())

            def load_x(half, m):
                act.dma_start(x_old[:, m % X_TILES, :], out[half, :, m, :]).then_inc(x_loaded[m % X_TILES], 16)

            def boundary_open(half):
                act.wait_ge(stored[half], st[half].at())
                for m in range(X_TILES):
                    load_x(half, m)
                norm_rsqrt()

            def norm_squares(half, tiles):
                for m in tiles:
                    s = n_used.slot
                    act.wait_ge(norm_square_used, n_used.next())
                    act.activation(b_square[:, s, :], branch[:, half, m, :], ACT.Square).then_inc(norm_square_ready, 1)
                    act.wait_ge(norm_square_ready, n_square.next())

            def boundary_squares(half, tiles):
                for m in tiles:
                    act.wait_ge(x_ready, xs.next())
                    if m + X_TILES < KT:
                        load_x(half, m + X_TILES)
                    norm_squares(half, (m,))

            def boundary_middle(half):
                act.dma_start(out[half], branch[:, half]).then_inc(stored[half], 16)
                st[half].skip(16)
                norm_rsqrt()

            def norm_highs(half, tiles):
                for m in tiles:
                    act.wait_ge(norm_value_ready, n_value.next())
                    act.activation(op_h[:, half, m, :], b_norm[:, m % 2, :], ACT.Copy).then_inc(norm_high_ready, 1)
                    act.wait_ge(norm_high_ready, n_high.next())

            act.dma_start(const[:, :], consts).then_inc(loaded, 16)
            act.dma_start(s_pos[:, :], positions.partition_broadcast(P)).then_inc(loaded, 16)
            act.dma_start(gain[:, :], gains[0]).then_inc(loaded, 16)
            act.dma_start(head_scales[:, :, :], scales).then_inc(loaded, 16)
            for i in range(4):
                act.dma_start(branch[:, 0, 2 * i:2 * i + 2, :], x[0, :, 2 * i:2 * i + 2, :]).then_inc(x_loaded[i], 16)

            act.dma_start(s_mem[:, :, :], mem).then_inc(mem_loaded, 16)

            def copy_x(half):
                act.dma_start(out[half], x[half]).then_inc(stored[half], 16)
                st[half].skip(16)

            act.wait_ge(loaded, ld.next(64))

            def sines(t, angle):
                act.wait_ge(value_ready, value.next())
                if t:
                    act.wait_ge(tables_stored, 64)
                for f in range(2):
                    to_value(s_tab[:, f, :], angle, ACT.Sin,
                             scale=const[:, K_SIGN:K_SIGN + 1] if f else 1.0)

            def store_table(t):
                for rows in (slice(0, 64), slice(64, P)):
                    act.dma_start(cos_sin[t, rows, 0, :], s_tab[0:64, 0, :]).then_inc(tables_stored, 16)
                act.dma_start(cos_sin[t, 0:64, 1, :], s_tab[64:P, 1, :]).then_inc(tables_stored, 16)
                act.dma_start(cos_sin[t, 64:P, 1, :], s_tab[64:P, 0, :]).then_inc(tables_stored, 16)

            sines(0, s_ang[:, :])
            store_table(0)
            copy_x(1)
            copy_x(0)
            for m in range(KT):
                if m % 2 == 0:
                    act.wait_ge(x_loaded[m // 2], 16)
                norm_squares(0, (m,))
            act.wait_ge(mem_loaded, mems.next(16))
            square(s_mem[:, :, :], s_mem[:, :, :])
            sines(1, s_posf[:, :])
            norm_rsqrt()
            norm_highs(0, range(KT))
            store_table(1)
            rsqrt(mem_rsqrt[:, :], mem_rsqrt[:, :], D, MEM)
            act.wait_ge(tables_stored, 128)

            with repeat(act, LAYERS, counts) as l:
                done.skip(4)
                boundary_open(1)
                act.dma_start(r_tab[:, :, :], cos_sin[0]).then_inc(loaded, 16)
                act.dma_start(r_decay[:, :], decay[0]).then_inc(decay_loaded, 16)
                boundary_squares(1, range(KT))
                boundary_middle(1)

                def head_tile(half, s, before=lambda: None):
                    cols = slice(half * HALF, (half + 1) * HALF)
                    before()
                    if s < 2:
                        act.wait_ge(value_ready, value.next())
                        to_high((r_qh, r_kh)[s][:, cols], r_t[:, 0, :])
                        done.skip(1)
                    elif s == 2:
                        done.skip(1)
                    else:
                        a = auxd.slot
                        act.wait_ge(aux_done, auxd.next())
                        to_high(r_vh[:, cols], aux(a))
                        s = done.slot
                        act.wait_ge(tile_done, done.next())
                        to_value(r_gate[:, cols], tile(s), ACT.Silu)

                def step(half, kb):
                    c, diagonal = columns(half, kb)
                    a = auxd.slot
                    act.wait_ge(aux_done, auxd.next())
                    if diagonal:
                        act.wait_ge(value_ready, value.next())
                    act.wait_ge(out_step, outd.next())
                    to_high(r_sh[:, step_index(half, kb) % SCORES, 0:HALF - c], aux(a, HALF - c), scale_of(half, kb))

                def head_square(half, later):
                    act.wait_ge(out_step, outd.at(SCORES - later))
                    square(r_square[:, :], outs(half))

                def head_rsqrt():
                    t = done.slot
                    act.wait_ge(tile_done, done.next())
                    act.wait_ge(rsqrt_used, rs_used.next())
                    act.activation(r_rsqrt[:, :], tile(t), ACT.Ln, bias=eps, scale=1.0 / P).then_inc(log_ready, 1)
                    act.wait_ge(log_ready, log.next())
                    act.activation(r_rsqrt[:, :], r_rsqrt[:, :], ACT.Exp, scale=-0.5).then_inc(rsqrt_ready, 1)
                    act.wait_ge(rsqrt_ready, rsq.next())

                def second_half(after):
                    for s in range(4):
                        def before():
                            step(0, s)
                            if s == 1 and after:
                                head_square(1, 2)
                            if s == 2 and after:
                                head_rsqrt()
                        head_tile(1, s, before)

                def second_steps(s):
                    step(1, 2 * s)
                    step(1, 2 * s + 1)
                    if s == 1:
                        head_square(0, 4)
                    if s == 2:
                        head_rsqrt()

                head_tile(0, 0)
                norm_highs(1, range(KT))
                act.wait_ge(phase_done, phases.next())
                act.dma_start(gain[:, :], gains[l + 1]).then_inc(gain_loaded, 16)
                for s in range(1, 4):
                    head_tile(0, s)
                second_half(False)
                with repeat(act, HEADS - 1, counts) as h:
                    act.dma_start(r_decay[:, :], decay[h + 1]).then_inc(decay_loaded, 16)
                    for s in range(4):
                        head_tile(0, s, lambda: second_steps(s))
                    second_half(True)
                def latent_log(to, dim):
                    assert auxd.slot == 0
                    act.wait_ge(aux_done, auxd.next(2))
                    act.activation(to[:, :], aux(0, SEQ), ACT.Ln, bias=eps, scale=1.0 / dim).then_inc(log_ready, 1)
                    act.wait_ge(log_ready, log.next())

                def latent_exp(to):
                    act.activation(to[:, :], to[:, :], ACT.Exp, scale=-0.5).then_inc(rsqrt_ready, 1)
                    act.wait_ge(rsqrt_ready, rsq.next())

                for s in range(4):
                    second_steps(s)
                    done.skip(1)
                    if s == 1:
                        for k in range(2):
                            square(r_t[:, 2 * k, :], branch[:, 0, 4 + k, :])
                    elif s == 2:
                        act.wait_ge(value_ready, value.next())
                        for k in range(2):
                            square(r_t[:, 1 + k, :], branch[:, 1, 4 + k, :])
                head_square(1, 0)
                outr.skip(2 * HEADS)
                done.skip(1)
                t = done.slot
                act.wait_ge(tile_done, done.next())
                act.wait_ge(rsqrt_used, rs_used.next())
                act.activation(r_rsqrt[:, :], tile(t), ACT.Ln, bias=eps, scale=1.0 / P).then_inc(log_ready, 1)
                act.wait_ge(log_ready, log.next())
                latent_log(c_q_rsqrt, QRANK)
                act.activation(r_rsqrt[:, :], r_rsqrt[:, :], ACT.Exp, scale=-0.5).then_inc(rsqrt_ready, 1)
                act.wait_ge(rsqrt_ready, rsq.next())
                latent_exp(c_q_rsqrt)
                ld.skip(16)

                act.wait_ge(phase_done, phases.next())
                act.dma_start(c_tab[:, :, :], cos_sin[1]).then_inc(loaded, 16)
                act.dma_start(z_raw[:, :], value_weights[l]).then_inc(loaded, 16)
                act.wait_ge(value_ready, value.next())
                for half in range(2):
                    square_ring(c_square, c_kv[:, half * HALF:(half + 1) * HALF])
                latent_log(c_rsqrt, KVRANK)
                latent_exp(c_rsqrt)
                act.wait_ge(loaded, ld.next(32))
                to_high(z_h[:, :], z_raw[:, :])
                done.skip(3)

                def latent_parts(to):
                    for k, slot_half in enumerate(to):
                        act.wait_ge(value_ready, value.next())
                        to_high(slot_half, c_norm[:, k % 2, :])

                def rope_key(half):
                    act.wait_ge(value_ready, value.next())
                    for n in range(2):
                        to_high(slot(KROPE + n)[0][:, half, :], c_t[:, 3 * half, :],
                                const[:, K_PAIR + n:K_PAIR + n + 1])

                rope_key(0)
                latent_parts([slot(CQ + k)[0][:, half, :] for half in range(2) for k in range(2)])
                rope_key(1)
                latent_parts([slot(CKV)[0][:, half, :] for half in range(2)])
                for pair in range(2):
                    for half in range(2):
                        done.skip(1)
                        act.wait_ge(value_ready, value.next())
                        to_high(slot(QROPE + pair)[0][:, half, :], c_t[:, 3 * half, :], ATT_SCALE)
                for t in range(4):
                    s = done.slot
                    act.wait_ge(tile_done, done.next())
                    to_high(m_vh[:, 2 * t:2 * t + 2, :], tile(s))

                def attend(width_of, banks, prob, parts_h, to_tile, prepare=None, at_end=None, between=None):
                    step = 0

                    def next_head(h):
                        if prepare and h < HEADS:
                            prepare(h)
                        if at_end and h == HEADS:
                            at_end()

                    def softmax(q):
                        n = width_of(q)
                        s = done.slot
                        done.skip(banks)
                        act.wait_ge(value_ready, value.next())
                        to_value(prob(q), tile(s, n), ACT.Exp, bias=stat[:, 1, q:q + 1],
                                 accum_out=stat[:, 2, q:q + 1])
                        act.sem_inc(tile_read, banks)

                    def one_step():
                        nonlocal step
                        a = auxd.slot
                        act.wait_ge(aux_done, auxd.next())
                        act.wait_ge(out_step, outd.next() + (SCORES - PARTS))
                        to_high(parts_h[:, step % PARTS, :], aux(a))
                        step += 1

                    before_last = []

                    def finish(later):
                        h, i = before_last.pop()
                        o = outr.slot
                        act.wait_ge(out_step, outd.at(SCORES - later))
                        rows = slice(64 * (h % 2), 64 * (h % 2) + 64)
                        to = branch[rows, i // 2, to_tile + h // 2, (i % 2) * 256:(i % 2) * 256 + 256]
                        act.activation(to, outs(o, 256)[rows], ACT.Copy).then_inc(out_read, 1)
                        act.wait_ge(out_read, outr.next())

                    def first_step(h, i):
                        one_step()
                        if before_last:
                            finish(1)
                        before_last.append((h, i))

                    def steps(h, i):
                        for j in range(width_of(2 * i) // 256):
                            if j:
                                one_step()
                            else:
                                first_step(h, i)
                            if between and h == HEADS - 1:
                                between(i, j)

                    def mixed(h, i, before):
                        n = width_of(2 * before[1]) // 256 if before else 0
                        softmax(2 * i)
                        if n:
                            first_step(*before)
                        softmax(2 * i + 1)
                        for j in range(n - 1):
                            one_step()

                    next_head(0)
                    for h in range(HEADS):
                        attention_order(h, next_head, steps, mixed)
                    finish(0)

                act.wait_ge(phase_done, phases.next())

                def latent_head(h):
                    for to in (m_qh, m_kh):
                        for half in range(2):
                            s = done.slot
                            act.wait_ge(tile_done, done.next())
                            to_high(to[:, half * HALF:(half + 1) * HALF], tile(s),
                                    ATT_SCALE if to is m_qh else 1.0)

                def memory_prepare():
                    act.dma_start(e_mem[:, :, :], mem).then_inc(mem_loaded, 16)
                    mems.skip(16)

                def memory_high(i, j):
                    if i == 2 and j:
                        to_high(slot(MQ + j - 1)[0], branch[:, :, 6 + j - 1, :], MEM_SCALE)

                attend(latent_width, 2, latent_probs, m_ph, 4, latent_head, memory_prepare, memory_high)

                act.wait_ge(phase_done, phases.next())
                act.wait_ge(value_ready, value.next())
                for k in range(0, KT, 2):
                    to_high(e_nh[:, k:k + 2, :], e_mem[:, k:k + 2, :])
                for t in range(2):
                    s = done.slot
                    act.wait_ge(tile_done, done.next())
                    for n in range(2):
                        to_high(e_kh[:, 2 * t + n, :], tile(s, MEM), const[:, K_HALVES + n:K_HALVES + n + 1])
                for t in range(2):
                    s = done.slot
                    act.wait_ge(tile_done, done.next())
                    to_high(e_vh[:, t, :], tile(s, MEM))
                attend(memory_width, 1, memory_probs, e_ph, 6)

                act.wait_ge(phase_done, phases.next())

                def out_tile(half, m):
                    s = done.slot
                    act.wait_ge(tile_done, done.next())
                    to_value(branch[:, half, m, :], tile(s), ACT.Copy)
                    square_ring(f_square, tile(s))

                for half in range(2):
                    for m in range(KT):
                        to_high(op_h[:, half, m, :], branch[:, half, m, :])
                for m in range(KT):
                    out_tile(0, m)
                boundary_open(0)
                boundary_squares(0, range(0, 2))
                for m in range(KT):
                    out_tile(1, m)
                    if m < 2:
                        boundary_squares(0, range(3 * m + 2, 3 * m + 5))
                    elif m == 4:
                        boundary_middle(0)
                        norm_highs(0, range(0, 2))
                    elif m in (5, 6):
                        norm_highs(0, range(3 * m - 13, 3 * m - 10))

                for half in range(2):
                    def hidden(j, u):
                        s = done.slot
                        act.wait_ge(tile_done, done.next())
                        to_value(f_gate[:, u, :], tile(s), ACT.Silu)
                        done.skip(1)
                        act.wait_ge(value_ready, value.next())
                        to_high(a_h[:, j, :], f_hidden[:, u, :])

                    for g, size in enumerate(GROUPS):
                        if g == 0:
                            for j in range(size):
                                hidden(j, j % 2)
                                if j == 1:
                                    boundary_open(1 - half)
                                elif j in (2, 3):
                                    boundary_squares(1 - half, range(4 * j - 8, 4 * j - 4))
                                elif j == 5:
                                    boundary_middle(1 - half)
                                elif j > 5:
                                    norm_highs(1 - half, range(4 * j - 24, 4 * j - 20))
                        else:
                            with repeat(act, size // 2, counts) as i:
                                for u in range(2):
                                    hidden(i * 2 + u, u)
                        for m in range(KT):
                            done.skip(1)
                            if g == 2:
                                act.wait_ge(value_ready, value.next())
                                square_ring(f_square, branch[:, half, m, :])

            boundary_open(1)
            for m in range(KT):
                act.wait_ge(x_ready, xs.next())
                if m + X_TILES < KT:
                    load_x(1, m + X_TILES)
                if m % 2:
                    act.dma_start(out[1, :, m - 1:m + 1, :], branch[:, 1, m - 1:m + 1, :]).then_inc(stored[1], 16)
                    st[1].skip(16)
            for half in range(2):
                act.wait_ge(stored[half], st[half].at())
                act.sem_inc(finished, 1)

        @block.vector
        def _(dve):
            dve.sem_inc(tile_read, TILES)
            dve.sem_inc(aux_read, AUX)
            dve.sem_inc(out_read, OUTS)
            dve.sem_inc(rsqrt_used, 1)
            done = Count(dve, "dve_tiles", TILES, TILES)
            auxd = Count(dve, "dve_aux", 0, AUX, 1)
            high = Count(dve, "dve_high")
            acts = Count(dve, "dve_act")
            sqr = Count(dve, "dve_square", 0, 2)
            rsq = Count(dve, "dve_rsqrt")
            ld = Count(dve, "dve_loaded")
            decays = Count(dve, "dve_decay_loaded")
            xl = [Count(dve, f"dve_x_loaded{i}") for i in range(X_TILES)]
            st = [Count(dve, f"dve_stored{i}") for i in range(2)]
            mems = Count(dve, "dve_mem_loaded", 16)
            gains_ = Count(dve, "dve_gain_loaded")
            n_square = Count(dve, "dve_norm_square", 0, 2)
            n_rsqrt = Count(dve, "dve_norm_rsqrt")
            n_value = Count(dve, "dve_norm_value")
            n_high = Count(dve, "dve_norm_high")
            n_low = Count(dve, "dve_norm_low")
            link_ = Count(dve, "dve_linked")
            read = Count(dve, "dve_read", TILES)
            auxr = Count(dve, "dve_aux_read", AUX)
            outr = Count(dve, "dve_out_read", OUTS, OUTS)
            low = Count(dve, "dve_low")
            value = Count(dve, "dve_value")
            part = Count(dve, "dve_part")
            xr = Count(dve, "dve_x_ready")
            counts = [done, auxd, high, acts, sqr, rsq, ld, decays, link_, read, auxr, outr, low, value, part, xr,
                      n_square, n_rsqrt, n_value, n_high, n_low, mems, gains_] + xl + st

            def link(instruction):
                instruction.then_inc(dve_link, 1)
                dve.wait_ge(dve_link, link_.next())

            def signal(instruction, semaphore, count):
                instruction.then_inc(semaphore, 1)
                dve.wait_ge(semaphore, count.next())

            def to_low(to, to_h, source):
                dve.wait_ge(high_ready, high.next())
                signal(dve.tensor_tensor(to, source, to_h.bitcast(F32), ALU.subtract), low_ready, low)

            def scaled_low(to, to_h, source, scale, semaphore, count):
                dve.wait_ge(high_ready, high.next())
                signal(dve.scalar_tensor_tensor(out=to, in0=source, scalar=scale, in1=to_h.bitcast(F32),
                                                op0=ALU.mult, op1=ALU.subtract), semaphore, count)

            def add_square(total, ring, first):
                s = sqr.slot
                dve.wait_ge(square_ready, sqr.next())
                if first:
                    link(dve.tensor_copy(total, ring[:, s, :]))
                else:
                    link(dve.tensor_tensor(total, total, ring[:, s, :], ALU.add))
                dve.sem_inc(square_used, 1)

            def take_rsqrt():
                dve.wait_ge(rsqrt_ready, rsq.next())
                auxd.skip(1)
                auxr.skip(1)
                dve.sem_inc(aux_read, 1)

            def norm_add_square(half, first):
                s = n_square.slot
                dve.wait_ge(norm_square_ready, n_square.next())
                total = f_sum[:, half, :]
                if first:
                    link(dve.tensor_copy(total, b_square[:, s, :]))
                else:
                    link(dve.tensor_tensor(total, total, b_square[:, s, :], ALU.add))
                dve.sem_inc(norm_square_used, 1)

            def norm_tiles(half, g, tiles):
                if tiles[0] == 0:
                    dve.wait_ge(norm_rsqrt_ready, n_rsqrt.next())
                for m in (*tiles, None):
                    if m is not None:
                        n_value.skip(1)
                        dve.scalar_tensor_tensor(
                            out=b_norm[:, m % 2, :], in0=branch[:, half, m, :], scalar=gain[:, g + m:g + m + 1],
                            in1=b_rsqrt[:, :], op0=ALU.mult, op1=ALU.mult).then_inc(norm_value_ready, 1)
                    if m != tiles[0]:
                        k = tiles[-1] if m is None else m - 1
                        dve.wait_ge(norm_high_ready, n_high.next())
                        signal(dve.tensor_tensor(op_l[:, half, k, :], b_norm[:, k % 2, :],
                                                 op_h[:, half, k, :].bitcast(F32), ALU.subtract),
                               norm_low_ready, n_low)
                dve.wait_ge(norm_value_ready, n_value.at())

            def boundary_residual(half, g, tiles, squares=True):
                if tiles[0] == 0:
                    dve.wait_ge(norm_rsqrt_ready, n_rsqrt.next())
                for m in (*tiles, None):
                    if m is not None:
                        y = branch[:, half, m, :]
                        dve.scalar_tensor_tensor(out=y, in0=y, scalar=gain[:, g + m:g + m + 1],
                                                 in1=b_rsqrt[:, :], op0=ALU.mult, op1=ALU.mult).then_inc(dve_link, 1)
                        link_.skip(1)
                    if m == tiles[0]:
                        continue
                    k = tiles[-1] if m is None else m - 1
                    y = branch[:, half, k, :]
                    dve.wait_ge(dve_link, link_.at(0 if m is None else -1))
                    dve.wait_ge(x_loaded[k % X_TILES], xl[k % X_TILES].next(16))
                    dve.tensor_tensor(y, x_old[:, k % X_TILES, :], y, ALU.add).then_inc(x_ready, 1)
                    xr.skip(1)
                    if k and squares:
                        norm_add_square(half, k == 1)
                dve.wait_ge(x_ready, xr.at())
                if squares and tiles[-1] == KT - 1:
                    norm_add_square(half, False)
                    dve.sem_inc(norm_sum_ready, 1)

            def angles(t, angle):
                c1 = 6.28125
                c2 = float(np.round((TWO_PI - c1) * 2 ** 19) / 2 ** 19)
                c3 = float(np.float32(TWO_PI - c1 - c2))
                link(dve.tensor_scalar(angle, s_posf[:, :], const[:, K_FREQ + t:K_FREQ + t + 1], None,
                                       ALU.mult))
                link(dve.tensor_scalar(s_turn[:, :], angle, 1.0 / TWO_PI, const[:, K_TURN:K_TURN + 1],
                                       ALU.mult, ALU.add))
                link(dve.tensor_scalar(s_turn[:, :], s_turn[:, :], MAGIC, -MAGIC, ALU.add, ALU.add))
                for c in (c1, c2, c3):
                    link(dve.scalar_tensor_tensor(out=angle, in0=s_turn[:, :], scalar=-c,
                                                  in1=angle, op0=ALU.mult, op1=ALU.add))
                link(dve.tensor_scalar(angle, angle, const[:, K_SHIFT:K_SHIFT + 1], None, ALU.add))
                signal(dve.tensor_scalar(angle, angle, 3.1415925, -3.1415925, ALU.min, ALU.max),
                       value_ready, value)

            link(dve.memset(f_sum[:, 1, :], 0.0))
            dve.wait_ge(loaded, ld.next(64))
            dve.sem_inc(phase_done, 1)
            link(dve.tensor_copy(s_posf[:, :], s_pos[:, :]))
            angles(0, s_ang[:, :])
            angles(1, s_posf[:, :])

            for m in range(KT):
                norm_add_square(0, m == 0)
            dve.sem_inc(norm_sum_ready, 1)
            sqr.other()
            dve.wait_ge(square_ready, sqr.at())
            for k in range(1, KT):
                link(dve.tensor_tensor(s_mem[:, 0, :], s_mem[:, 0, :], s_mem[:, k, :], ALU.add))
            dve.sem_inc(sum_ready, 1)
            dve.sem_inc(norm_sum_ready, 1)
            norm_tiles(0, G_NEXT, range(KT))
            acts.skip(4)
            take_rsqrt()
            dve.sem_inc(rsqrt_used, 1)
            dve.wait_ge(cleared, 1)
            for i in range(X_TILES):
                xl[i].skip(16)

            def rope(s, table, half, temp):
                cols = slice(half * HALF, (half + 1) * HALF)
                link(dve.tensor_tensor(temp[:, 1, :], tile(s), table[:, 0, cols], ALU.mult))
                link(dve.tensor_tensor(temp[0:64, 2, :], tile(s)[64:128], table[0:64, 1, cols], ALU.mult))
                signal(dve.tensor_tensor(temp[64:128, 2, :], tile(s)[0:64], table[64:128, 1, cols], ALU.mult),
                       tile_read, read)

            with repeat(dve, LAYERS, counts):
                dve.wait_ge(stored[0], st[0].at(16))
                for t in range(4):
                    boundary_residual(1, G_POST_FFN, range(2 * t, 2 * t + 2))
                    s = done.slot
                    dve.wait_ge(tile_done, done.next())
                    signal(dve.tensor_copy(branch[:, 0, 4 + t, :], tile(s)), tile_read, read)
                st[1].skip(16)

                dve.wait_ge(loaded, ld.next(16))
                dve.wait_ge(decay_loaded, decays.next(16))

                def head_tile(half, s, before=lambda: None):
                    cols = slice(half * HALF, (half + 1) * HALF)
                    before()
                    if s < 2:
                        th, tl = ((r_qh, r_ql), (r_kh, r_kl))[s]
                        t = done.slot
                        dve.wait_ge(tile_done, done.next())
                        rope(t, r_tab, half, r_t)
                        if s:
                            signal(dve.tensor_tensor(r_t[:, 0, :], r_t[:, 1, :], r_t[:, 2, :], ALU.add),
                                   value_ready, value)
                        else:
                            link(dve.tensor_tensor(r_t[:, 1, :], r_t[:, 1, :], r_t[:, 2, :], ALU.add))
                            signal(dve.tensor_tensor(r_t[:, 0, :], r_t[:, 1, :], r_decay[:, 0:HALF], ALU.mult),
                                   value_ready, value)
                        to_low(tl[:, cols], th[:, cols], r_t[:, 0, :])
                    elif s == 2:
                        t = done.slot
                        dve.wait_ge(tile_done, done.next())
                        signal(dve.tensor_copy(r_vt[:, :], tile(t)), tile_read, read)
                        dve.sem_inc(part_ready, 1)
                    else:
                        a = auxd.slot
                        auxd.skip(1)
                        dve.wait_ge(high_ready, high.next())
                        signal(dve.tensor_tensor(r_vl[:, cols], aux(a), r_vh[:, cols].bitcast(F32), ALU.subtract),
                               aux_read, auxr)
                        done.skip(1)
                        dve.wait_ge(act_ready, acts.next())
                        read.skip(1)
                        dve.sem_inc(tile_read, 1)

                def head_out(half, h):
                    sqr.other()
                    dve.wait_ge(rsqrt_ready, rsq.next())
                    done.skip(1)
                    read.skip(1)
                    dve.sem_inc(tile_read, 1)
                    link(dve.tensor_tensor(r_square[:, :], outs(half), r_rsqrt[:, :], ALU.mult))
                    dve.sem_inc(rsqrt_used, 1)
                    outr.skip(1)
                    dve.sem_inc(out_read, 1)
                    link(dve.tensor_tensor(branch[:, half, h, :], r_square[:, :],
                                           r_gate[:, half * HALF:(half + 1) * HALF], ALU.mult))

                def step(half, kb):
                    c, diagonal = columns(half, kb)
                    a = auxd.slot
                    dve.wait_ge(aux_done, auxd.next())
                    if diagonal:
                        n = 256 if kb - 4 * half == 3 else P
                        view = aux(a, n)
                        signal(dve.tensor_tensor(view, view, tri[:, 256 - n:256], ALU.mult), value_ready, value)
                    dve.wait_ge(high_ready, high.next())
                    i = step_index(half, kb) % SCORES
                    low_part, high_part = r_sl[:, i, 0:HALF - c], r_sh[:, i, 0:HALF - c].bitcast(F32)
                    signal(dve.scalar_tensor_tensor(out=low_part, in0=aux(a, HALF - c), scalar=scale_of(half, kb),
                                                    in1=high_part, op0=ALU.mult, op1=ALU.subtract),
                           aux_read, auxr)

                def second_half(h, before_it):
                    link(dve.tensor_copy(r_scale[:, :], head_scales[:, h, :]))
                    for s in range(4):
                        def before():
                            step(0, s)
                            if s == 2 and before_it is not None:
                                head_out(1, before_it)
                        head_tile(1, s, before)

                def second_steps(s, h):
                    step(1, 2 * s)
                    step(1, 2 * s + 1)
                    if s == 2:
                        head_out(0, h)

                head_tile(0, 0)
                norm_tiles(1, G_NEXT, range(KT))
                dve.sem_inc(phase_done, 1)
                for s in range(1, 4):
                    head_tile(0, s)
                second_half(0, None)
                with repeat(dve, HEADS - 1, counts) as h:
                    dve.wait_ge(stored[1], st[1].at(16))
                    for s in range(4):
                        def before():
                            second_steps(s, h)
                            if s == 0:
                                dve.wait_ge(decay_loaded, decays.next(16))
                        head_tile(0, s, before)
                    second_half(h + 1, h)
                for s in range(4):
                    second_steps(s, HEADS - 1)
                    t = done.slot
                    dve.wait_ge(tile_done, done.next())
                    signal(dve.tensor_copy(branch[:, 1, 4 + s, :], tile(t)), tile_read, read)
                    if s == 2:
                        sqr.other(2)
                        dve.wait_ge(square_ready, sqr.at())
                        link(dve.tensor_tensor(r_t[:, 0, :], r_t[:, 0, :], r_t[:, 2, :], ALU.add))
                        value.skip(1)
                        dve.sem_inc(value_ready, 1)

                def keep(to):
                    s = done.slot
                    dve.wait_ge(tile_done, done.next())
                    signal(dve.tensor_copy(to, tile(s)), tile_read, read)

                def copied():
                    value.skip(1)
                    dve.sem_inc(value_ready, 1)

                kv = [c_kv[:, half * HALF:(half + 1) * HALF] for half in range(2)]
                q_lat = [[branch[:, half, 4 + k, :] for k in range(2)] for half in range(2)]
                sqr.other(2)
                dve.wait_ge(square_ready, sqr.at())
                link(dve.tensor_tensor(r_t[:, 1, :], r_t[:, 1, :], r_t[:, 2, :], ALU.add))
                dve.sem_inc(sum_ready, 1)
                keep(kv[0])
                head_out(1, HEADS - 1)
                dve.sem_inc(phase_done, 1)

                def take_pair():
                    dve.wait_ge(rsqrt_ready, rsq.next())
                    auxd.skip(2)
                    auxr.skip(2)
                    dve.sem_inc(aux_read, 2)

                def latent_parts(sources, gains, scale, slots):
                    for k in range(len(sources) + 1):
                        if k < len(sources):
                            half, source = sources[k]
                            signal(dve.scalar_tensor_tensor(
                                out=c_norm[:, k % 2, :], in0=source, scalar=gain[:, gains[k]:gains[k] + 1],
                                in1=scale[:, half * HALF:(half + 1) * HALF], op0=ALU.mult, op1=ALU.mult),
                                value_ready, value)
                        if k:
                            half = sources[k - 1][0]
                            h, l = slot(slots[k - 1])
                            to_low(l[:, half, :], h[:, half, :], c_norm[:, (k - 1) % 2, :])

                def rope_key(half):
                    t = done.slot
                    dve.wait_ge(tile_done, done.next())
                    rope(t, c_tab, half, c_t)
                    signal(dve.tensor_tensor(c_t[:, 3 * half, :], c_t[:, 1, :], c_t[:, 2, :], ALU.add),
                           value_ready, value)

                def rope_key_lows(half):
                    for n in range(2):
                        dve.wait_ge(high_ready, high.next())
                        link(dve.scalar_tensor_tensor(
                            out=slot(KROPE + n)[1][:, half, :], in0=c_t[:, 3 * half, :],
                            scalar=const[:, K_PAIR + n:K_PAIR + n + 1],
                            in1=slot(KROPE + n)[0][:, half, :].bitcast(F32), op0=ALU.mult, op1=ALU.subtract))
                    low.skip(1)
                    dve.sem_inc(low_ready, 1)

                keep(kv[1])
                copied()
                for half in range(2):
                    add_square(c_sum[:, half, :], c_square, True)
                dve.sem_inc(sum_ready, 1)
                take_pair()
                dve.wait_ge(gain_loaded, gains_.next(16))
                dve.wait_ge(loaded, ld.next(32))
                rope_key(0)
                to_low(z_l[:, :], z_h[:, :], z_raw[:, :])
                rope_key_lows(0)
                latent_parts([(half, q_lat[half][k]) for half in range(2) for k in range(2)],
                             [G_Q, G_Q + 1] * 2, c_q_rsqrt, [CQ, CQ + 1] * 2)
                rope_key(1)
                rope_key_lows(1)
                take_pair()
                latent_parts([(half, kv[half]) for half in range(2)], [G_KV] * 2, c_rsqrt, [CKV] * 2)
                for n in range(5):
                    pair, half = n // 2, n % 2
                    if n < 4:
                        t = done.slot
                        dve.wait_ge(tile_done, done.next())
                        rope(t, c_tab, half, c_t)
                    if n:
                        before = (n - 1) // 2
                        scaled_low(slot(QROPE + before)[1][:, 1 - half, :], slot(QROPE + before)[0][:, 1 - half, :],
                                   c_t[:, 3 * (1 - half), :], ATT_SCALE, low_ready, low)
                    if n < 4:
                        signal(dve.tensor_tensor(c_t[:, 3 * half, :], c_t[:, 1, :], c_t[:, 2, :], ALU.add),
                               value_ready, value)
                for t in range(4):
                    s = done.slot
                    done.skip(1)
                    dve.wait_ge(high_ready, high.next())
                    signal(dve.tensor_tensor(m_vl[:, 2 * t:2 * t + 2, :], tile(s), m_vh[:, 2 * t:2 * t + 2, :].bitcast(F32),
                                             ALU.subtract), tile_read, read)
                dve.sem_inc(phase_done, 1)

                def attend(width_of, banks, masked, prob, parts_h, parts_l, prepare=None,
                           between=None):
                    step = 0

                    def next_head(h):
                        if prepare and h < HEADS:
                            prepare(h)

                    def maximum(q):
                        n = width_of(q)
                        s = done.slot
                        dve.wait_ge(tile_done, done.next(banks))
                        if masked:
                            view = tile(s, 256, n - 256)
                            at = K_CAUSAL + 256 * (q % 2)
                            link(dve.tensor_tensor(view, view, const[:, at:at + 256], ALU.add))
                        signal(dve.reduce_max(stat[:, 1, q:q + 1], tile(s, n), AX.X, negate=True),
                               value_ready, value)
                        read.skip(banks)

                    def reciprocals(i):
                        dve.wait_ge(act_ready, acts.next(2))
                        link(dve.reciprocal(stat[:, 3, 2 * i:2 * i + 2], stat[:, 2, 2 * i:2 * i + 2]))

                    def normalise(q):
                        signal(dve.tensor_scalar(prob(q), prob(q), stat[:, 3, q:q + 1], None, ALU.mult),
                               part_ready, part)

                    def one_step():
                        nonlocal step
                        a = auxd.slot
                        auxd.skip(1)
                        dve.wait_ge(high_ready, high.next())
                        signal(dve.tensor_tensor(parts_l[:, step % PARTS, :], aux(a),
                                                 parts_h[:, step % PARTS, :].bitcast(F32), ALU.subtract),
                               aux_read, auxr)
                        step += 1

                    def normalised_steps(last, h, i):
                        n = width_of(2 * i) // 256 if h is not None else 0
                        if n > 1:
                            one_step()
                        if last is not None:
                            reciprocals(last)
                            normalise(2 * last)
                        if n:
                            one_step()
                        if last is not None:
                            normalise(2 * last + 1)
                        for j in range(n - 2):
                            one_step()

                    def steps(h, i):
                        if h < HEADS - 1 or not between:
                            normalised_steps(3 if i == 2 else None, h, i)
                            return
                        for j in range(width_of(2 * i) // 256):
                            one_step()
                            if i == 2 and j < 2:
                                if j == 0:
                                    reciprocals(3)
                                normalise(6 + j)
                            between(i, j)

                    def mixed(h, i, before):
                        maximum(2 * i)
                        maximum(2 * i + 1)
                        normalised_steps(i - 1 if i else None, *(before or (None, 0)))

                    next_head(0)
                    for h in range(HEADS):
                        attention_order(h, next_head, steps, mixed)
                    outr.skip(4 * HEADS)

                def latent_head(h):
                    for th, tl in ((m_qh, m_ql), (m_kh, m_kl)):
                        for half in range(2):
                            cols = slice(half * HALF, (half + 1) * HALF)
                            s = done.slot
                            done.skip(1)
                            scaled_low(tl[:, cols], th[:, cols], tile(s), ATT_SCALE if th is m_qh else 1.0,
                                       tile_read, read)

                def memory_prepare(i, j):
                    if i == 2 and j:
                        k = j - 1
                        scaled_low(slot(MQ + k)[1], slot(MQ + k)[0], branch[:, :, 6 + k, :], MEM_SCALE, low_ready, low)
                    elif i == 3:
                        if j == 0:
                            dve.wait_ge(mem_loaded, mems.next(16))
                        for k in (2 * j, 2 * j + 1):
                            link(dve.scalar_tensor_tensor(
                                out=e_mem[:, k, :], in0=e_mem[:, k, :], scalar=gain[:, G_MEM + k:G_MEM + k + 1],
                                in1=mem_rsqrt[:, :], op0=ALU.mult, op1=ALU.mult))
                        if j == 3:
                            value.skip(1)
                            dve.sem_inc(value_ready, 1)

                attend(latent_width, 2, True, latent_probs, m_ph, m_pl, latent_head, memory_prepare)
                dve.sem_inc(phase_done, 1)

                for k in range(0, KT, 2):
                    to_low(e_nl[:, k:k + 2, :], e_nh[:, k:k + 2, :], e_mem[:, k:k + 2, :])
                for t in range(2):
                    s = done.slot
                    done.skip(1)
                    dve.wait_ge(high_ready, high.next(2))
                    for n in range(2):
                        ins = dve.scalar_tensor_tensor(
                            out=e_kl[:, 2 * t + n, :], in0=tile(s, MEM), scalar=const[:, K_HALVES + n:K_HALVES + n + 1],
                            in1=e_kh[:, 2 * t + n, :].bitcast(F32), op0=ALU.mult, op1=ALU.subtract)
                        if n:
                            signal(ins, tile_read, read)
                        else:
                            link(ins)
                for t in range(2):
                    s = done.slot
                    done.skip(1)
                    dve.wait_ge(high_ready, high.next())
                    signal(dve.tensor_tensor(e_vl[:, t, :], tile(s, MEM), e_vh[:, t, :].bitcast(F32), ALU.subtract),
                           tile_read, read)
                attend(memory_width, 1, False, memory_probs, e_ph, e_pl)
                dve.wait_ge(out_read, outr.at())
                dve.sem_inc(phase_done, 1)

                for half in range(2):
                    for m in range(KT):
                        to_low(op_l[:, half, m, :], op_h[:, half, m, :], branch[:, half, m, :])
                def out_tile(half, m):
                    done.skip(1)
                    dve.wait_ge(act_ready, acts.next())
                    add_square(f_sum[:, half, :], f_square, m == 0)
                    read.skip(1)
                    dve.sem_inc(tile_read, 1)
                    if m == KT - 1:
                        dve.sem_inc(norm_sum_ready, 1)

                for m in range(KT):
                    out_tile(0, m)
                boundary_residual(0, G_POST_MIX, range(0, 2))
                for m in range(KT):
                    out_tile(1, m)
                    if m < 2:
                        boundary_residual(0, G_POST_MIX, range(3 * m + 2, 3 * m + 5))
                    elif m == 4:
                        norm_tiles(0, G_PRE_FFN, range(0, 2))
                    elif m in (5, 6):
                        norm_tiles(0, G_PRE_FFN, range(3 * m - 13, 3 * m - 10))
                st[0].skip(16)

                for half in range(2):
                    post, pre = (G_POST_FFN, G_NEXT) if half else (G_POST_MIX, G_PRE_FFN)

                    def hidden(j, u):
                        done.skip(1)
                        s = done.slot
                        dve.wait_ge(tile_done, done.next())
                        dve.wait_ge(act_ready, acts.next())
                        signal(dve.tensor_tensor(f_hidden[:, u, :], f_gate[:, u, :], tile(s), ALU.mult),
                               value_ready, value)
                        read.skip(2)
                        dve.sem_inc(tile_read, 2)
                        to_low(a_l[:, j, :], a_h[:, j, :], f_hidden[:, u, :])

                    for g, size in enumerate(GROUPS):
                        if g == 0:
                            for j in range(size):
                                hidden(j, j % 2)
                                if j in (2, 3):
                                    boundary_residual(1 - half, post, range(4 * j - 8, 4 * j - 4))
                                elif j > 5:
                                    norm_tiles(1 - half, pre, range(4 * j - 24, 4 * j - 20))
                            dve.wait_ge(stored[half], st[half].at(16))
                            st[1 - half].skip(16)
                        else:
                            with repeat(dve, size // 2, counts) as i:
                                for u in range(2):
                                    hidden(i * 2 + u, u)
                        for m in range(KT + (g == 2)):
                            if m < KT:
                                s = done.slot
                                dve.wait_ge(tile_done, done.next())
                                y = branch[:, half, m, :]
                                if g == 0:
                                    signal(dve.tensor_copy(y, tile(s)), tile_read, read)
                                else:
                                    signal(dve.tensor_tensor(y, y, tile(s), ALU.add), tile_read, read)
                                if g == 2:
                                    value.skip(1)
                                    dve.sem_inc(value_ready, 1)
                            if g == 2 and m:
                                add_square(f_sum[:, half, :], f_square, m == 1)
                    dve.sem_inc(norm_sum_ready, 1)

            boundary_residual(1, G_POST_FFN, range(KT), squares=False)
            dve.sem_inc(finished, 1)


def _block(w):
    k, n = w.shape
    return w.reshape(k // P, P, n).transpose(1, 0, 2).reshape(P, -1)


def _layer_blocks(w_in, w_uq, w_ukv, w_mem_kv, w_out, w_gate, w_up, w_down):
    cols = lambda w, at, n=P: _block(w[:, at:at + n])
    found = [cols(w_in, at) for at in (2048, 2176, 2496, 2624)]
    for h in range(HEADS):
        found += [cols(w_in, part * 512 + h * P) for part in range(4)]
    rope_key = w_in[:, 2432:2496]
    rope_key = np.concatenate([rope_key[:, :32]] * 2 + [rope_key[:, 32:]] * 2, 1)
    found += [cols(w_in, 2304), _block(rope_key)]
    uq = w_uq.reshape(QRANK, HEADS, NOPE + ROPE)
    ukv = w_ukv.reshape(KVRANK, HEADS, NOPE + VDIM)
    found += [_block(uq[:, :, :NOPE].reshape(QRANK, -1))]
    rope_q = uq[:, :, NOPE:].reshape(QRANK, 2, 2, 2, 32).transpose(0, 1, 3, 2, 4).reshape(QRANK, -1)
    found += [np.concatenate([_block(rope_q), ukv[:, :, :NOPE].reshape(KVRANK, -1)], 1)]
    found += [cols(w_mem_kv, 0), cols(w_mem_kv, P)]
    found += [_block(w_mem_kv[k * 512:(k + 1) * 512, 256:]) for k in range(2)]
    found += [cols(w_out, m * P) for m in range(KT)]
    at = 0
    for size in GROUPS:
        for j in range(at, at + size):
            found += [cols(w_gate, j * P), cols(w_up, j * P)]
        rows = w_down[at * P:(at + size) * P]
        found += [np.pad(cols(rows, m * P), ((0, 0), (0, BLOCK - size * P))) for m in range(KT)]
        at += size
    return np.stack(found), np.ascontiguousarray(ukv[:, :, NOPE:].reshape(KVRANK, -1))


def _constants():
    c = np.zeros((P, K_ALL), np.float32)
    row, col = np.arange(P)[:, None], np.arange(P)[None, :]
    c[:, K_ID:K_ID + P] = row == col
    c[:, K_ONES:K_ONES + P] = 1.0
    c[:, K_TRI + P:K_TRI + 2 * P] = col >= row
    low = np.where(col > row, -3.0e38, 0.0)
    c[:, K_CAUSAL:K_CAUSAL + P] = low
    c[:, K_CAUSAL + P:K_CAUSAL + 2 * P] = -3.0e38
    c[:, K_CAUSAL + 3 * P:K_CAUSAL + 4 * P] = low
    for n in range(2):
        c[:, K_PAIR + n] = np.arange(P) // 32 % 2 == n
        c[:, K_HALVES + n] = np.arange(P) // 64 == n
    c[:, K_EPS] = EPS
    c[:, K_SIGN] = -1.0
    c[:64, K_TURN], c[:64, K_SHIFT] = 0.25, np.pi / 2
    for t, half in enumerate((64, 32)):
        c[:, K_FREQ + t] = np.float32(10000.0) ** (-(np.arange(P) % half).astype(np.float32) / np.float32(half))
    return c


def _decay():
    d, scales = np.zeros((HEADS, P, HALF), np.float32), np.zeros((P, HEADS, 8), np.float32)
    place = np.arange(HALF, dtype=np.float64)
    for h in range(HEADS):
        g = 1.0 - 2.0 ** (-5.0 - h)
        d[h] = g ** place * float(P) ** -0.5
        keys = (g ** -place).reshape(4, P).T
        scales[:, h, 0:4] = keys
        scales[:, h, 4:8] = keys * g ** HALF
    return d, scales


def kernel(x, mem, positions, pre_mix_g, w_in, mla_q_norm_g, w_uq, mla_kv_norm_g, w_ukv, mem_norm_g, w_mem_kv,
           w_out, post_mix_g, pre_ffn_g, w_gate, w_up, w_down, post_ffn_g):
    from concourse import bacc
    from concourse.bass_utils import run_bass_kernel_spmd

    names = (x, mem, positions, pre_mix_g, w_in, mla_q_norm_g, w_uq, mla_kv_norm_g, w_ukv, mem_norm_g, w_mem_kv,
             w_out, post_mix_g, pre_ffn_g, w_gate, w_up, w_down, post_ffn_g)
    (x, mem, positions, pre_mix_g, w_in, mla_q_norm_g, w_uq, mla_kv_norm_g, w_ukv, mem_norm_g, w_mem_kv,
     w_out, post_mix_g, pre_ffn_g, w_gate, w_up, w_down, post_ffn_g) = [np.asarray(a) for a in names]

    by_tile = lambda g: g.reshape(-1, P).T
    layers = [_layer_blocks(w_in[l], w_uq[l], w_ukv[l], w_mem_kv[l], w_out[l], w_gate[l], w_up[l], w_down[l])
              for l in range(LAYERS)]
    gains = np.stack([np.concatenate(
        [by_tile(mla_q_norm_g[l]), by_tile(mla_kv_norm_g[l]), by_tile(mem_norm_g[l]), by_tile(post_mix_g[l]),
         by_tile(pre_ffn_g[l]), by_tile(post_ffn_g[l]), by_tile(pre_mix_g[min(l + 1, LAYERS - 1)])], 1)
        for l in range(LAYERS)])
    first = np.zeros_like(gains[:1])
    first[0, :, G_NEXT:] = by_tile(pre_mix_g[0])
    gains = np.concatenate([first, gains])
    arrays = {
        "x_in": x[0].T.reshape(KT, P, 2, HALF).transpose(2, 1, 0, 3),
        "mem_in": mem[0].T.reshape(KT, P, MEM).transpose(1, 0, 2),
        "positions_in": positions[0],
        "weights_in": np.concatenate([b for b, _ in layers]),
        "value_weights_in": np.stack([v for _, v in layers]),
        "gains_in": gains,
        "consts_in": _constants(),
        "decay_in": _decay()[0],
        "scales_in": _decay()[1],
    }
    arrays = {n: np.ascontiguousarray(a) for n, a in arrays.items()}
    nc = bacc.Bacc("TRN2", target_bir_lowering=False, num_devices=1)
    aps = [nc.dram_tensor(n, a.shape, mybir.dt.from_np(a.dtype), kind="ExternalInput").ap()
           for n, a in arrays.items()]
    out = nc.dram_tensor("out_0_dram", (2, P, KT, HALF), F32, kind="ExternalOutput").ap()
    build(nc, *aps, out)
    r = run_bass_kernel_spmd(nc, [arrays], core_ids=[0])
    y = r.results[0]["out_0_dram"]
    return np.ascontiguousarray(y.transpose(2, 1, 0, 3).reshape(D, SEQ).T)[None]
```
